# Optimizing a Trainium2 kernel written in Bass

```python
import jax, jax.numpy as jnp
from jax import lax
import numpy as np

D_MODEL = 1024
BATCH = 1
SEQ = 512
DEPTH = 2

PLE_DIM = 256
D_FF = 2816
CONV_DIM = D_MODEL
CONV_K = 31
N_HEADS = 16
N_KV = 4
HPG = N_HEADS // N_KV
HEAD_DIM = 64
ROPE_DIM = HEAD_DIM // 4
ROPE_THETA = 500000.0
CMP_LEN = 32
CMP_STRIDE = 16
CMP_HID = 256
SEL_LEN = 64
N_SEL = 16
WINDOW = 512
Q_BLOCK = 64
NEG = -1e30
EPS = 1e-6

KV_W = N_KV * HEAD_DIM
OFF_Q = 2 * CONV_DIM
OFF_KV = OFF_Q + N_HEADS * HEAD_DIM
OFF_GATE = OFF_KV + 6 * KV_W
OFF_MERGE = OFF_GATE + 3 * N_HEADS
N_IN = OFF_MERGE + 2 * D_MODEL

kernel_name = "hybrid_conformer_nsa_macaron_block"

def rms_norm(x, g):
    xf = x.astype(jnp.float32)
    y = xf * lax.rsqrt(jnp.mean(xf * xf, axis=-1, keepdims=True) + EPS)
    return (y * g.astype(jnp.float32)).astype(x.dtype)

def layer_norm(x, g, b):
    xf = x.astype(jnp.float32)
    mu = jnp.mean(xf, axis=-1, keepdims=True)
    var = jnp.mean(jnp.square(xf - mu), axis=-1, keepdims=True)
    y = (xf - mu) * lax.rsqrt(var + EPS)
    return (y * g.astype(jnp.float32) + b.astype(jnp.float32)).astype(x.dtype)

def swiglu_ffn(x, norm_g, w_in, w_out):
    a, b = jnp.split(rms_norm(x, norm_g) @ w_in, 2, axis=-1)
    return (jax.nn.silu(a) * b) @ w_out

def partial_rope(x, pos):
    half = ROPE_DIM // 2
    inv = ROPE_THETA ** (-jnp.arange(half, dtype=jnp.float32) / half)
    ang = pos.astype(jnp.float32)[:, None] * inv[None, :]
    cos = jnp.cos(ang)[:, None, :]
    sin = jnp.sin(ang)[:, None, :]
    xr = x[..., :ROPE_DIM].astype(jnp.float32)
    x1, x2 = xr[..., :half], xr[..., half:]
    rot = jnp.concatenate([x1 * cos - x2 * sin, x2 * cos + x1 * sin], axis=-1).astype(x.dtype)
    return jnp.concatenate([rot, x[..., ROPE_DIM:]], axis=-1)

def masked_softmax(s, mask):
    p = jax.nn.softmax(jnp.where(mask, s, NEG), axis=-1)
    return jnp.where(mask, p, 0.0)

def conv_module(u, conv_w, conv_b, ln_g, ln_b, w_out):
    a, gate = jnp.split(u, 2, axis=-1)
    h = a * jax.nn.sigmoid(gate)
    h = lax.conv_general_dilated(
        h, conv_w[:, None, :].astype(h.dtype), window_strides=(1,),
        padding=[(CONV_K - 1, 0)], dimension_numbers=("NWC", "WIO", "NWC"),
        feature_group_count=CONV_DIM) + conv_b
    h = jax.nn.silu(layer_norm(h, ln_g, ln_b))
    return h @ w_out

def compress(kv, pos_emb, w1, b1, w2):
    b_, t_ = kv.shape[:2]
    sub = kv.reshape(b_, t_ // CMP_STRIDE, CMP_STRIDE, N_KV, HEAD_DIM)
    blk = jnp.concatenate([sub[:, :-1], sub[:, 1:]], axis=2)
    blk = blk + pos_emb[None, None, :, None, :]
    blk = jnp.moveaxis(blk, 3, 2).reshape(b_, -1, N_KV, CMP_LEN * HEAD_DIM)
    return jax.nn.gelu(blk @ w1 + b1) @ w2

def nsa(q, kc, vc, ks, vs, kw, vw, gates):
    b_, t_ = q.shape[:2]
    n_cmp = kc.shape[1]
    n_blk = t_ // SEL_LEN
    n_sel = min(N_SEL, n_blk)
    scale = HEAD_DIM ** -0.5
    cmp_end = jnp.arange(n_cmp) * CMP_STRIDE + CMP_LEN - 1
    ci = jnp.arange(n_cmp)[:, None]
    sj = jnp.arange(n_blk)[None, :]
    cmp_to_sel = ((ci * CMP_STRIDE < (sj + 1) * SEL_LEN)
                  & (ci * CMP_STRIDE + CMP_LEN > sj * SEL_LEN)).astype(jnp.float32)
    blk_start = jnp.arange(n_blk) * SEL_LEN

    def to_blocks(a):
        a = a.reshape(b_, n_blk, SEL_LEN, N_KV, HEAD_DIM).transpose(0, 3, 1, 2, 4)
        return a.reshape(b_ * N_KV, n_blk, SEL_LEN, HEAD_DIM)

    ks_blk, vs_blk = to_blocks(ks), to_blocks(vs)
    pad = ((0, 0), (WINDOW, 0), (0, 0), (0, 0))
    kw_pad, vw_pad = jnp.pad(kw, pad), jnp.pad(vw, pad)
    gather = jax.vmap(lambda a, i: jnp.take(a, i, axis=0))

    def block(c):
        start = c * Q_BLOCK
        t = start + jnp.arange(Q_BLOCK)
        qb = lax.dynamic_slice_in_dim(q, start, Q_BLOCK, axis=1)
        gb = lax.dynamic_slice_in_dim(gates, start, Q_BLOCK, axis=1)
        s = jnp.einsum("bqghd,bngd->bghqn", qb, kc, preferred_element_type=jnp.float32) * scale
        p_c = masked_softmax(s, cmp_end[None, :] <= t[:, None])
        o_c = jnp.einsum("bghqn,bngd->bqghd", p_c.astype(vc.dtype), vc)
        imp = jnp.einsum("bghqn,ns->bgqs", p_c, cmp_to_sel)
        cur = (t // SEL_LEN)[:, None]
        jj = jnp.arange(n_blk)[None, :]
        forced = (jj == 0) | (jj == cur) | (jj == cur - 1)
        valid = blk_start[None, :] <= t[:, None]
        imp = jnp.where(valid, jnp.where(forced, 1e4, imp), -1.0)
        top_val, top_idx = lax.top_k(imp, n_sel)
        idx_flat = top_idx.reshape(b_ * N_KV, Q_BLOCK * n_sel)
        k_sel = gather(ks_blk, idx_flat).reshape(b_, N_KV, Q_BLOCK, n_sel * SEL_LEN, HEAD_DIM)
        v_sel = gather(vs_blk, idx_flat).reshape(b_, N_KV, Q_BLOCK, n_sel * SEL_LEN, HEAD_DIM)
        s = jnp.einsum("bqghd,bgqmd->bghqm", qb, k_sel, preferred_element_type=jnp.float32) * scale
        kpos = (top_idx[..., None] * SEL_LEN + jnp.arange(SEL_LEN)).reshape(b_, N_KV, Q_BLOCK, n_sel * SEL_LEN)
        m = (kpos <= t[:, None]) & jnp.repeat(top_val >= 0.0, SEL_LEN, axis=-1)
        p_s = masked_softmax(s, m[:, :, None])
        o_s = jnp.einsum("bghqm,bgqmd->bqghd", p_s.astype(v_sel.dtype), v_sel)
        kwb = lax.dynamic_slice_in_dim(kw_pad, start, WINDOW + Q_BLOCK, axis=1)
        vwb = lax.dynamic_slice_in_dim(vw_pad, start, WINDOW + Q_BLOCK, axis=1)
        s = jnp.einsum("bqghd,bsgd->bghqs", qb, kwb, preferred_element_type=jnp.float32) * scale
        spos = start - WINDOW + jnp.arange(WINDOW + Q_BLOCK)
        m = (spos[None, :] >= 0) & (spos[None, :] <= t[:, None]) & (spos[None, :] > t[:, None] - WINDOW)
        p_w = masked_softmax(s, m)
        o_w = jnp.einsum("bghqs,bsgd->bqghd", p_w.astype(vwb.dtype), vwb)
        return gb[..., 0:1] * o_c + gb[..., 1:2] * o_s + gb[..., 2:3] * o_w

    out = lax.map(block, jnp.arange(t_ // Q_BLOCK))
    return jnp.moveaxis(out, 0, 1).reshape(b_, t_, N_HEADS * HEAD_DIM)

def setup_inputs(seed: int = 0) -> dict:
    key = jax.random.key(seed)
    ks = iter(jax.random.split(key, 40))

    def nrm(shape, scale):
        return jax.random.normal(next(ks), shape, jnp.float32) * scale

    def gain(shape):
        return 1.0 + nrm(shape, 0.02)

    L, D = DEPTH, D_MODEL
    return {
        "x": nrm((BATCH, SEQ, D), 1.0),
        "p": nrm((DEPTH, BATCH, SEQ, PLE_DIM), 1.0),
        "ffn1_norm": gain((L, D)),
        "ffn1_w_in": nrm((L, D, 2 * D_FF), D ** -0.5),
        "ffn1_w_out": nrm((L, D_FF, D), D_FF ** -0.5),
        "mix_norm": gain((L, D)),
        "w_in": nrm((L, D, N_IN), D ** -0.5),
        "b_in": nrm((L, N_IN), 0.02),
        "conv_w": nrm((L, CONV_K, CONV_DIM), CONV_K ** -0.5),
        "conv_b": nrm((L, CONV_DIM), 0.02),
        "conv_ln_g": gain((L, CONV_DIM)),
        "conv_ln_b": nrm((L, CONV_DIM), 0.02),
        "conv_w_out": nrm((L, CONV_DIM, D), CONV_DIM ** -0.5),
        "q_norm": gain((L, HEAD_DIM)),
        "k_norm": gain((L, 3, HEAD_DIM)),
        "cmp_pos": nrm((L, 2, CMP_LEN, HEAD_DIM), 0.02),
        "cmp_w1": nrm((L, 2, CMP_LEN * HEAD_DIM, CMP_HID), (CMP_LEN * HEAD_DIM) ** -0.5),
        "cmp_b1": nrm((L, 2, CMP_HID), 0.02),
        "cmp_w2": nrm((L, 2, CMP_HID, HEAD_DIM), CMP_HID ** -0.5),
        "nsa_w_out": nrm((L, N_HEADS * HEAD_DIM, D), (N_HEADS * HEAD_DIM) ** -0.5),
        "w_out": nrm((L, D, D), D ** -0.5),
        "ffn2_norm": gain((L, D)),
        "ffn2_w_in": nrm((L, D, 2 * D_FF), D ** -0.5),
        "ffn2_w_out": nrm((L, D_FF, D), D_FF ** -0.5),
        "ple_norm": gain((L, D)),
        "ple_w_gate": nrm((L, D, D), D ** -0.5),
        "ple_w_proj": nrm((L, PLE_DIM, D), PLE_DIM ** -0.5),
        "ple_post_norm": gain((L, D)),
    }

def reference(x, p, ffn1_norm, ffn1_w_in, ffn1_w_out, mix_norm, w_in, b_in, conv_w, conv_b,
              conv_ln_g, conv_ln_b, conv_w_out, q_norm, k_norm, cmp_pos, cmp_w1, cmp_b1, cmp_w2,
              nsa_w_out, w_out, ffn2_norm, ffn2_w_in, ffn2_w_out, ple_norm, ple_w_gate,
              ple_w_proj, ple_post_norm):
    b_, t_, _ = x.shape
    pos = jnp.arange(t_)
    n_cmp = t_ // CMP_STRIDE - 1
    cmp_pos_ids = jnp.arange(n_cmp) * CMP_STRIDE + CMP_LEN - 1
    for i in range(DEPTH):
        x = x + 0.5 * swiglu_ffn(x, ffn1_norm[i], ffn1_w_in[i], ffn1_w_out[i])
        h = rms_norm(x, mix_norm[i])
        u = h @ w_in[i] + b_in[i]
        y_conv = conv_module(u[..., :OFF_Q], conv_w[i], conv_b[i], conv_ln_g[i], conv_ln_b[i], conv_w_out[i])
        q = u[..., OFF_Q:OFF_KV].reshape(b_, t_, N_HEADS, HEAD_DIM)
        q = partial_rope(rms_norm(q, q_norm[i]), pos).reshape(b_, t_, N_KV, HPG, HEAD_DIM)
        k_ct, v_ct, k_s, v_s, k_w, v_w = [
            u[..., OFF_KV + j * KV_W: OFF_KV + (j + 1) * KV_W].reshape(b_, t_, N_KV, HEAD_DIM)
            for j in range(6)]
        k_c = compress(k_ct, cmp_pos[i, 0], cmp_w1[i, 0], cmp_b1[i, 0], cmp_w2[i, 0])
        v_c = compress(v_ct, cmp_pos[i, 1], cmp_w1[i, 1], cmp_b1[i, 1], cmp_w2[i, 1])
        k_c = partial_rope(rms_norm(k_c, k_norm[i, 0]), cmp_pos_ids)
        k_s = partial_rope(rms_norm(k_s, k_norm[i, 1]), pos)
        k_w = partial_rope(rms_norm(k_w, k_norm[i, 2]), pos)
        nsa_gates = jax.nn.sigmoid(u[..., OFF_GATE:OFF_MERGE]).reshape(b_, t_, N_KV, HPG, 3)
        y_nsa = nsa(q, k_c, v_c, k_s, v_s, k_w, v_w, nsa_gates) @ nsa_w_out[i]
        g_conv, g_nsa = jnp.split(jax.nn.sigmoid(u[..., OFF_MERGE:]), 2, axis=-1)
        x = x + (g_conv * y_conv + g_nsa * y_nsa) @ w_out[i]
        x = x + 0.5 * swiglu_ffn(x, ffn2_norm[i], ffn2_w_in[i], ffn2_w_out[i])
        e = rms_norm(p[i] @ ple_w_proj[i], ple_post_norm[i])
        x = x + jax.nn.sigmoid(rms_norm(x, ple_norm[i]) @ ple_w_gate[i]) * e
    return x


_drawn_inputs = setup_inputs


def setup_inputs(seed=0):
    import zlib

    import numpy as np

    out = dict(_drawn_inputs(seed))
    spreads = {}
    factors = {'ffn1_norm': 5.356,
     'mix_norm': 5.735,
     'b_in': 4.073,
     'conv_b': 10.297,
     'conv_ln_g': 19.751,
     'conv_ln_b': 20.706,
     'q_norm': 8.0,
     'k_norm': 8.0,
     'cmp_pos': 8.0,
     'cmp_b1': 8.0,
     'ffn2_norm': 6.048,
     'ple_norm': 38.931,
     'ple_post_norm': 26.031}
    for name, (base, spread) in spreads.items():
        noise = np.random.default_rng([zlib.crc32(name.encode()), seed]).standard_normal(out[name].shape)
        drawn = base * np.exp(spread * noise) if base else spread * noise
        out[name] = __import__('jax').numpy.asarray(drawn.astype(out[name].dtype))
    for name, factor in factors.items():
        out[name] = (out[name] * factor).astype(out[name].dtype)
    return out
```

```python
from contextlib import ExitStack

import numpy as np

import concourse.bass as bass
from concourse import mybir

F32 = mybir.dt.float32
F32R = mybir.dt.float32r
ALU = mybir.AluOpType
ACT = mybir.ActivationFunctionType
AX = mybir.AxisListType

P = 128
D, T, DEPTH = 1024, 512, 2
DT = D // P
TT = T // P
FF = 2816
FT = FF // P
FSTEPS = FT // 2
PLE = 256
CONV_K = 31
NH, NKV, HPG, HD = 16, 4, 4, 64
HALF = 8
ROPE_THETA = 500000.0
CMP_LEN, CMP_STRIDE, CMP_HID = 32, 16, 256
NCMP = T // CMP_STRIDE
KVW = NKV * HD
OFF_Q = 2 * D
OFF_KV = OFF_Q + NH * HD
OFF_GATE = OFF_KV + 6 * KVW
OFF_MERGE = OFF_GATE + 3 * NH
NEG = -1e30
EPS = 1e-6
SCALE = HD ** -0.5
XTOK = T + CMP_STRIDE

SLOTS = 4
U_FFN1 = 0
U_CONV = U_FFN1 + 3 * FT
U_CT = U_CONV + 2 * DT
U_GATE = U_CT + 4
U_CMP = U_GATE + 1
U_W2 = U_CMP + 8
U_TOK = U_W2 + 1
U_MERGE = U_TOK + 16
U_OUT = U_MERGE + 4 * DT
U_FFN2 = U_OUT + DT
U_PROJ = U_FFN2 + 3 * FT
U_PLE = U_PROJ + 2
UNITS = U_PLE + DT
assert UNITS % SLOTS == 0
B_FFN1 = 0
B_CONV = B_FFN1 + 2 * FT
B_CT = B_CONV + 2 * DT
B_GATE = B_CT + 4
B_CMP = B_GATE + 2
B_W2 = B_CMP + 4
B_TOK = B_W2 + 2
B_MERGE = B_TOK + 16
B_OUT = B_MERGE + 4 * DT
B_FFN2 = B_OUT + DT
B_PROJ = B_FFN2 + 2 * FT
B_PLE = B_PROJ + DT
BANKS = B_PLE + DT
assert BANKS % SLOTS == 0
BARRIERS = 7
STATS = 4
NSPLIT = 7

C_F1, C_MIX, C_F2, C_PLE, C_POST, C_BA, C_BG, C_BGC, C_BGN = range(0, 72, 8)
C_BCT, C_CB, C_LG, C_LB, C_POS, C_B1, C_CW = 72, 76, 84, 92, 100, 132, 136
NCOL = C_CW + DT * CONV_K
R_B, R_G, R_BG, R_KC = 0, 2048, 3584, 3632
NROW = R_KC + HD
K_ID, K_ONE, K_COS, K_SIN, K_COSC, K_SINC, K_VALID, NCON = 0, 128, 256, 288, 320, 328, 336, 340
K_MASK, K_CM, NMASK = 0, 128, 640


def constants():
    c = np.zeros((P, NCON), np.float32)
    masks = np.zeros((P, NMASK), np.float32)
    c[:, K_ID:K_ID + P] = np.eye(P)
    r = np.arange(P)
    masks[:, K_MASK:K_MASK + P] = np.where(r[None, :] <= r[:, None], 0.0, NEG)
    c[:, K_ONE:K_ONE + P] = 1.0
    inv = (np.float32(ROPE_THETA) ** (-np.arange(HALF, dtype=np.float32) / np.float32(HALF))).astype(np.float32)
    n = np.arange(NCMP)
    for q in range(TT):
        t = q * P + r
        seen = (n[None, :] * CMP_STRIDE + CMP_LEN - 1 <= t[:, None]) & (n[None, :] < NCMP - 1)
        masks[:, K_CM + q * P:K_CM + (q + 1) * P] = np.tile(np.where(seen, 0.0, NEG), (1, 4))
        ang = (t.astype(np.float32)[:, None] * inv[None, :]).astype(np.float32)
        c[:, K_COS + q * HALF:K_COS + (q + 1) * HALF] = np.cos(ang)
        c[:, K_SIN + q * HALF:K_SIN + (q + 1) * HALF] = np.sin(ang)
        c[:, K_VALID + q] = t >= CMP_LEN - 1
    pos = ((r % NCMP) * CMP_STRIDE + CMP_LEN - 1).astype(np.float32)
    ang = (pos[:, None] * inv[None, :]).astype(np.float32)
    c[:, K_COSC:K_COSC + HALF] = np.cos(ang)
    c[:, K_SINC:K_SINC + HALF] = np.sin(ang)
    return c, masks


def pack(i):
    stream = np.zeros((DEPTH * UNITS + SLOTS, P, 1024), np.float32)
    cols = np.zeros((DEPTH + 1, P, NCOL), np.float32)
    rows = np.zeros((DEPTH, NROW), np.float32)

    def tiles(w):
        return w.reshape(w.shape[0] // P, P, w.shape[1]).transpose(1, 0, 2).reshape(P, -1)

    def cm(v):
        return v.reshape(-1, P).T

    for l in range(DEPTH):
        out = stream[l * UNITS:(l + 1) * UNITS]

        def ffn(u, w1, w2):
            for s in range(FSTEPS + 1):
                if s < FSTEPS:
                    for j in range(2):
                        for c in range(2):
                            m = c * FF + (2 * s + j) * P
                            out[u] = tiles(w1[:, m:m + P])
                            u += 1
                if s > 0:
                    for j in range(2):
                        f = (2 * (s - 1) + j) * P
                        out[u] = w2[f:f + P]
                        u += 1

        def cols_of(u, w, n):
            for m in range(n):
                out[u + m] = tiles(w[:, m * P:(m + 1) * P])

        ffn(U_FFN1, i["ffn1_w_in"][l], i["ffn1_w_out"][l])
        ffn(U_FFN2, i["ffn2_w_in"][l], i["ffn2_w_out"][l])
        w, b = i["w_in"][l], i["b_in"][l]
        kv = [slice(OFF_KV + j * KVW, OFF_KV + (j + 1) * KVW) for j in range(6)]
        for m in range(DT):
            out[U_CONV + 2 * m] = tiles(w[:, m * P:(m + 1) * P])
            out[U_CONV + 2 * m + 1] = tiles(w[:, D + m * P:D + (m + 1) * P])
            u = U_MERGE + 4 * m
            out[u] = tiles(w[:, OFF_MERGE + m * P:OFF_MERGE + (m + 1) * P])
            out[u + 1] = tiles(w[:, OFF_MERGE + D + m * P:OFF_MERGE + D + (m + 1) * P])
            out[u + 2] = tiles(i["nsa_w_out"][l][:, m * P:(m + 1) * P])
            out[u + 3] = tiles(i["conv_w_out"][l][:, m * P:(m + 1) * P])
        cols_of(U_CT, w[:, kv[0].start:kv[1].stop], 4)
        out[U_GATE][:, :8 * 48] = tiles(w[:, OFF_GATE:OFF_MERGE])
        for c in range(2):
            w1 = tiles(i["cmp_w1"][l, c]).reshape(P, 4, 1024)
            for j in range(4):
                out[U_CMP + 4 * c + j] = w1[:, j]
            out[U_W2][:, c * 128:(c + 1) * 128] = tiles(i["cmp_w2"][l, c])
        blocks = [(w[:, OFF_Q:OFF_Q + 512], b[OFF_Q:OFF_Q + 512]),
                  (w[:, OFF_Q + 512:OFF_KV], b[OFF_Q + 512:OFF_KV]),
                  (np.concatenate([w[:, kv[2]], w[:, kv[4]]], 1), np.concatenate([b[kv[2]], b[kv[4]]])),
                  (np.concatenate([w[:, kv[3]], w[:, kv[5]]], 1), np.concatenate([b[kv[3]], b[kv[5]]]))]
        for n, (wb, bb) in enumerate(blocks):
            wb = tiles(wb)
            for j in range(4):
                out[U_TOK + 4 * n + j] = wb[:, j * 1024:(j + 1) * 1024]
            rows[l, R_B + n * 512:R_B + (n + 1) * 512] = bb
        cols_of(U_OUT, i["w_out"][l], DT)
        for j in range(2):
            out[U_PROJ + j] = tiles(i["ple_w_proj"][l][:, j * 512:(j + 1) * 512])
        cols_of(U_PLE, i["ple_w_gate"][l], DT)

        for c, v in ((C_F1, i["ffn1_norm"][l]), (C_MIX, i["mix_norm"][l]), (C_F2, i["ffn2_norm"][l]),
                     (C_PLE, i["ple_norm"][l]), (C_POST, i["ple_post_norm"][l]), (C_BA, b[:D]), (C_BG, b[D:2 * D]),
                     (C_BGC, b[OFF_MERGE:OFF_MERGE + D]), (C_BGN, b[OFF_MERGE + D:]),
                     (C_BCT, b[kv[0].start:kv[1].stop]), (C_CB, i["conv_b"][l]), (C_LG, i["conv_ln_g"][l]),
                     (C_LB, i["conv_ln_b"][l]), (C_B1, i["cmp_b1"][l].reshape(-1))):
            v = cm(v)
            cols[l][:, c:c + v.shape[1]] = v
        for c in range(2):
            cols[l][:, C_POS + 16 * c:C_POS + 16 * (c + 1)] = cm(i["cmp_pos"][l, c].reshape(-1))
        cols[l][:, C_CW:] = i["conv_w"][l].reshape(CONV_K, DT, P).transpose(2, 1, 0).reshape(P, -1)
        g = [i["q_norm"][l]] * 16 + [i["k_norm"][l, 1]] * 4 + [i["k_norm"][l, 2]] * 4
        rows[l, R_G:R_BG] = np.concatenate(g)
        rows[l, R_BG:R_KC] = b[OFF_GATE:OFF_MERGE]
        rows[l, R_KC:] = i["k_norm"][l, 0]
    return stream, cols, rows


LINKS = {'act.layer': 2, 'dve.conv': 18, 'dve.tok': 13, 'dve.att': 22, 'dve.merge': 1, 'dve.layer': 538}


class Chain:

    def __init__(self, eng, sem, name, settle):
        self.eng, self.sem, self.name, self.n, self.terms, self.settle = eng, sem, name, 0, [], settle

    def link(self, ins):
        ins.then_inc(self.sem, 1)
        self.n += 1
        v = self.n
        for reg, per in self.terms:
            v = reg * per + v
        self.eng.wait_ge(self.sem, v)

    def loop(self, key, trips):
        return _Loop(self, self.name + key, trips)


class _Loop:
    def __init__(self, chain, key, trips):
        self.c, self.key, self.trips = chain, key, trips

    def __enter__(self):
        self.c.settle(self.c.eng)
        self.fori = self.c.eng.Fori(0, self.trips)
        reg = self.fori.__enter__()
        self.start = self.c.n
        self.per = LINKS.get(self.key, 0)
        self.c.terms.append((reg, self.per))
        return reg

    def __exit__(self, *exc):
        if exc[0] is None:
            got = self.c.n - self.start
            assert got == self.per, f"LINKS[{self.key!r}] = {got}"
            self.c.terms.pop()
            self.c.n = self.start + self.per * self.trips
        return self.fori.__exit__(*exc)


def build(nc, stream, cols_d, rows_d, const_d, mask_d, x_d, p_d, out_d):
    ctx = ExitStack()
    with ctx:
        base = 16512
        end = [base]

        def region(nbytes):
            at = end[0]
            end[0] += (nbytes + 31) // 32 * 32
            return at

        def sb(name, shape, dt, at):
            n = 4
            for s in shape[1:]:
                n *= s
            return nc.alloc_sbuf_tensor_at(name, shape, dt, offset=at), at + n

        def one(name, shape, dt=F32):
            n = 4
            for s in shape[1:]:
                n *= s
            return sb(name, shape, dt, region(n))[0]

        x = one("x", [P, DT, T])
        raw = one("raw", [P, SLOTS, 1024])
        wh = one("w_hi", [P, SLOTS, 1024], F32R)
        wl = one("w_lo", [P, SLOTS, 1024], F32R)
        con = one("con", [P, NCON])
        ident_r = one("ident_r", [P, P], F32R)
        mask_r = one("mask_r", [P, P], F32R)
        cmask_r = one("cmask_r", [P, TT, P], F32R)
        cols = one("cols", [P, NCOL])
        rstd = one("rstd", [P, T])
        rstd_t = one("rstd_t", [P, TT])
        ssq = one("ssq", [P, T])
        sq = one("sq", [P, 2, T])
        gates = one("gates", [P, TT, 3 * NH])
        small = one("small", [P, 64])
        att = one("att", [P, 64])
        rB, rT, rA = region(32768), region(32768), region(4 * DT * (T + CONV_K - 1) + 16384)
        rD = end[0]
        D_BYTES = 229368 - rD

        xh, a = sb("x_hi", [P, DT, T], F32R, rB)
        xl, _ = sb("x_lo", [P, DT, T], F32R, a)
        kT, _ = sb("kT", [P, 2, 2, NKV, T], F32R, rB)
        tqx = sb("tok", [P, 2 * TT * D], F32, rT)[0][:, :]
        tq = tqx[:, 0:TT * D].rearrange("p (t n) -> p t n", t=TT)
        tkv = tqx[:, TT * D:2 * TT * D].rearrange("p (c t n) -> p c t n", c=2, t=TT)
        xc, a = sb("xc", [P, 2, NKV, XTOK], F32, rT)
        ych, a = sb("yc_hi", [P, 8, P], F32R, a)
        ycl, a = sb("yc_lo", [P, 8, P], F32R, a)
        yf, a = sb("yf", [P, DT, T], F32, rT)
        mt, _ = sb("mt", [P, 4, T], F32, a)
        pe_, a = sb("emb", [P, DT, T], F32, rT)
        pf, a = sb("pf", [P, 2, T], F32, a)
        ph, a = sb("p_hi", [P, 2, T], F32R, a)
        pl, a = sb("p_lo", [P, 2, T], F32R, a)
        acc, ch_at = sb("conv_acc", [P, DT, T], F32, rA)
        ch, _ = sb("conv_in", [P, DT, T + CONV_K - 1], F32, ch_at)
        cvl, _ = sb("cv_lo", [P, DT, T], F32R, rA)
        cvh, o_at = sb("cv_hi", [P, DT, T], F32R, ch_at)
        hh, a = sb("h_hi", [P, 2, 2, T], F32R, rD)
        hl, a = sb("h_lo", [P, 2, 2, T], F32R, a)
        fa, a = sb("fa", [P, 2, T], F32, a)
        fb, a = sb("fb", [P, 2, T], F32, a)
        row, a = sb("rows", [P, NROW], F32, rD)
        sqt, a2 = sb("sqt", [P, TT, 512], F32, a)
        ctb, _ = sb("ctb", [P, 4, T], F32, a)
        hvh, a3 = sb("hv_hi", [P, 2, 512], F32R, a)
        hvl, _ = sb("hv_lo", [P, 2, 512], F32R, a3)
        vcb, a = sb("vcb", [P, NKV, HPG, HD], F32, a2)
        kcT, a = sb("kcT", [P, 2, P], F32R, a)
        free_at = a
        cv, _ = sb("cv", [P, 2, T], F32, a)
        hid, a = sb("hid", [P, 2, P], F32, a)
        hkh, a = sb("hk_hi", [P, 2, P], F32R, a)
        hkl, a = sb("hk_lo", [P, 2, P], F32R, a)
        kc, a = sb("kc", [P, HD], F32, a)
        kcw, a = sb("kcw", [P, HD], F32, a)
        assert a <= 229368, (a - rD, D_BYTES)
        kdh, _ = sb("kd_hi", [P, 8, 2, HD], F32R, rD)
        kdl, _ = sb("kd_lo", [P, 8, 2, HD], F32R, rD + 4096)
        pr, a = sb("probs", [P, 2, 2, T], F32, rD)
        ptk, a = sb("probsT", [P, 2, 2, TT, P], F32, a)
        q2, a = sb("q2", [P, HPG, 2, HD], F32R, a)
        q2T, a = sb("q2T", [P, HPG, P], F32R, a)
        pcs, a = sb("pcs", [P, HPG, NCMP], F32, a)
        pc, a = sb("pc", [P, P], F32, a)
        ptc, a = sb("ptc", [P, P], F32, a)
        ot, _ = sb("ot", [P, HPG, HD], F32, free_at)
        assert a <= rD + NROW * 4 + 8192, "the attention's buffers reach into vcb"
        oh, a = sb("o_hi", [P, DT, T], F32R, o_at)
        ol, a = sb("o_lo", [P, DT, T], F32R, a)
        assert a <= 229368, a - 229368
        masks, _ = sb("masks", [P, NMASK], F32, rD)
        kcd, _ = sb("kcd", [P, 2, 2, HD], F32R, rD + 8192)

        con_ = con[:, :]
        ident = con_[:, K_ID:K_ID + P]
        ones = con_[:, K_ONE:K_ONE + P]

        ps = ctx.enter_context(nc.psum_tensor("ps", [P, 8, 512], F32))

        def sem(name):
            return ctx.enter_context(nc.semaphore(name))

        raw_in = [sem(f"raw_in{s}") for s in range(SLOTS)]
        w_hi, w_split, w_used = sem("s_w_hi"), sem("s_w_split"), sem("s_w_used")
        bank_free = sem("bank_free")
        bar = sem("bar")
        mask_in, settled = sem("mask_in"), sem("settled")
        const_in, x_in, cols_in, rows_in, p_in = (sem(n) for n in ("const_in", "x_in", "cols_in", "rows_in", "p_in"))
        xc_zero, ct_ready, xc_in, vcb_zero = sem("xc_zero"), sem("ct_ready"), sem("xc_in"), sem("vcb_zero")
        con_r = sem("con_r")
        s_xh, s_xl = sem("s_xh"), sem("s_xl")
        s_sq, s_ssq, s_sum, s_rinv, s_rstd = sem("s_sq"), sem("s_ssq"), sem("s_sum"), sem("s_rinv"), sem("s_rstd")
        f_silu, f_h, f_hh, f_hl = sem("f_silu"), sem("f_h"), sem("f_hh"), sem("f_hl")
        y_done, y_free = sem("y_done"), sem("y_free")
        c_sig, c_pad = sem("c_sig"), sem("c_pad")
        g_pre = sem("g_pre")
        g_sig = sem("g_sig")
        yc_h, yc_l = sem("yc_h"), sem("yc_l")
        hid_pre, hid_h, hid_l, kc_ready = sem("hid_pre"), sem("hid_h"), sem("hid_l"), sem("kc_ready")
        t_ev, t_sq, t_rinv, t_rs, t_done = sem("t_ev"), sem("t_sq"), sem("t_rinv"), sem("t_rs"), sem("t_done")
        ln_mu, ln_d, ln_sq, ln_var, ln_rinv, ln_rs = (sem(n) for n in ("ln_mu", "ln_d", "ln_sq", "ln_var", "ln_rinv",
                                                                   "ln_rs"))
        ln_e, ln_f, ln_hi, ln_lo = sem("ln_e"), sem("ln_f"), sem("ln_hi"), sem("ln_lo")
        kd_h, kd_l, k_tr, k_ev = sem("kd_h"), sem("kd_l"), sem("k_tr"), sem("k_ev")
        q_h, q_l, q_tr, q_ev = sem("q_h"), sem("q_l"), sem("q_tr"), sem("q_ev")
        sc_done, sc_sub, pc_exp, ptc_tr, ptc_ev, oc_done = (sem(n) for n in ("sc_done", "sc_sub", "pc_exp", "ptc_tr",
                                                                           "ptc_ev", "oc_done"))
        s_done, s_max, p_exp, pt_tr, pt_ev0, pt_ev1, pv_done = (sem(n) for n in ("s_done", "s_max", "p_exp", "pt_tr",
                                                                              "pt_ev0", "pt_ev1", "pv_done"))
        oc_read = sem("oc_read")
        ot_tr, ot_h, ot_l = sem("ot_tr"), sem("ot_h"), sem("ot_l")
        m_pre, m_sig = sem("m_pre"), sem("m_sig")
        p_hi_, p_lo_ = sem("s_p_hi"), sem("s_p_lo")
        e_ev = sem("e_ev")
        g_t, g_s = sem("g_t"), sem("g_s")
        dve_seq, act_seq = sem("dve_seq"), sem("act_seq")
        out_done = sem("out_done")

        def unit(L, c, i=None, pi=0):
            v = L * UNITS + c
            return v if i is None else i * pi + v

        def lay(L, per, c, i=None, pi=0):
            v = L * per + c
            return v if i is None else i * pi + v

        def col(c):
            return cols[:, c:c + 1] if isinstance(c, int) else cols[:, bass.ds(c, 1)]

        def at_pos(c, j):
            n = 2 * j // CMP_STRIDE
            return xc[:, c, :, :].rearrange("p h (n s) -> p h n s", s=CMP_STRIDE)[:, :, n:n + NCMP, 2 * j % CMP_STRIDE]

        def copies(m):
            return hid[:, m, :].rearrange("p (g o n) -> p g o n", g=NKV, o=1).broadcast_to([P, NKV, HPG, NCMP])

        def twice(ap):
            return ap.rearrange("p (o d) -> p o d", o=1).broadcast_to([P, 2, HD])

        def keys_twice(t):
            return tkv[:, 0, t, :].rearrange("p (h o d) -> p h o d", h=8, o=1).broadcast_to([P, 8, 2, HD])

        def heads(q, g, n=0):
            return tqx[:, bass.ds(g * 256 + (q * D + n * 256), 256)].rearrange("p (j d) -> p j d", j=HPG)

        def settle(eng):
            eng.sem_inc(settled, 1)

        def barrier(eng, L, k):
            settle(eng)
            eng.drain().then_inc(bar, 1)
            eng.wait_ge(bar, lay(L, 3 * BARRIERS, 3 * (k + 1)))
            settle(eng)

        block = ctx.enter_context(nc.Block())

        @block.sync
        def _(sp):
            for u in range(SLOTS):
                sp.dma_start(raw[:, u, :], stream[u]).then_inc(raw_in[u], 16)
            with sp.Fori(0, DEPTH * UNITS // SLOTS) as i:
                for s in range(SLOTS):
                    sp.wait_ge(w_split, i * SLOTS + s + 1)
                    sp.dma_start(raw[:, s, :], stream[i * SLOTS + s + SLOTS]).then_inc(raw_in[s], 16)
            for s in range(SLOTS):
                sp.wait_ge(raw_in[s], 16 * (DEPTH * UNITS // SLOTS + 1))
            sp.wait_ge(bar, 3 * BARRIERS * DEPTH)
            sp.dma_start(out_d, x[:, :, :]).then_inc(out_done, 16)
            sp.wait_ge(out_done, 16)

        @block.gpsimd
        def _(pool):
            pool.dma_start(con[:, :], const_d).then_inc(const_in, 16)
            pool.dma_start(masks[:, :], mask_d).then_inc(mask_in, 16)
            pool.dma_start(x[:, :, :], x_d).then_inc(x_in, 16)
            pool.dma_start(cols[:, :], cols_d[0]).then_inc(cols_in, 16)
            with pool.Fori(0, DEPTH) as L:
                pool.wait_ge(bar, lay(L, 3 * BARRIERS, 3))
                settle(pool)
                pool.dma_start(row[:, :], rows_d[L].partition_broadcast(P)).then_inc(rows_in, 16)
                pool.memset(xc[:, :, :, :], 0.0).then_inc(xc_zero, 1)
                pool.memset(vcb[:, :, :, :], 0.0).then_inc(vcb_zero, 1)
                pool.wait_ge(xc_zero, lay(L, 1, 1))
                settle(pool)
                for c in range(4):
                    pool.wait_ge(ct_ready, lay(L, 4, c + 1))
                    settle(pool)
                    for half in range(2):
                        h = 2 * (c % 2) + half
                        src = ctb[64 * half:64 * half + 64, c, :]
                        pool.dma_start(xc[0:64, c // 2, h, 0:T], src).then_inc(xc_in, 16)
                        pool.dma_start(xc[64:128, c // 2, h, 0:T - 1], src[:, 1:T]).then_inc(xc_in, 16)
                pool.wait_ge(bar, lay(L, 3 * BARRIERS, 3 * 4))
                settle(pool)
                pool.dma_start(pf[:, :, :], p_d[L]).then_inc(p_in, 16)
                pool.wait_ge(bar, lay(L, 3 * BARRIERS, 3 * BARRIERS))
                settle(pool)
                pool.dma_start(cols[:, :], cols_d[L + 1]).then_inc(cols_in, 16)
            pool.wait_ge(cols_in, 16 * (DEPTH + 1))

        @block.tensor
        def _(pe):
            mm = nc.tensor.matmul

            def mm3(out, ah, al, bh, bl, start, stop, **kw):
                mm(out, ah, bh, start=start, stop=False, **kw)
                mm(out, ah, bl, start=False, stop=False, **kw)
                return mm(out, al, bh, start=False, stop=stop, **kw)

            def bank(b):
                return ps[:, b % SLOTS, :]

            def product(L, c, b, rh, rl, i=None, pi=0, bi=0, first=None, ready=None):
                s = c % SLOTS
                pe.wait_ge(w_split, unit(L, c + 1, i, pi))
                pe.wait_ge(bank_free, lay(L, BANKS, b + 1, i, bi))
                for k in range(DT):
                    if first is not None:
                        pe.wait_ge(s_xl, lay(L, 8 * 6, first + k + 1))
                    if ready is not None:
                        pe.wait_ge(ready, lay(L, DT, k + 1))
                    last = mm3(bank(b), wh[:, s, k * P:(k + 1) * P], wl[:, s, k * P:(k + 1) * P],
                               rh[:, k, :], rl[:, k, :], k == 0, k == DT - 1)
                last.then_inc(w_used, 1)

            def stat_sum(L, s):
                pe.wait_ge(s_ssq, lay(L, 8 * 5, 8 * s + 8))
                mm(ps[:, 4, :], ones, ssq[:, :], start=True, stop=True).then_inc(s_sum, 1)

            def ffn(L, u0, b0, which, split, stat):
                def ab(c, b, i=None, first=None):
                    for j in range(4):
                        product(L, c + j, b + j, xh, xl, i, 12, 8, first if j == 0 else None)
                        if j == 0 and first is not None:
                            stat_sum(L, stat)

                def y(c, s, par, i=None):
                    pe.wait_ge(w_split, unit(L, c + 2, i, 12))
                    pe.wait_ge(f_hl, lay(L, 2 * FT, which * FT + 2 * s + 2, i, 4))
                    for m in range(DT):
                        pe.wait_ge(y_free, lay(L, 16 * FSTEPS, (which * FSTEPS + s) * 8 + m + 1, i, 16))
                        for j in range(2):
                            sl = (c + j) % SLOTS
                            last = mm3(ps[:, 4 + m % 4, :], wh[:, sl, m * P:(m + 1) * P], wl[:, sl, m * P:(m + 1) * P],
                                       hh[:, par, j, :], hl[:, par, j, :], j == 0, j == 1)
                            if m == DT - 1:
                                last.then_inc(w_used, 1)
                        if m < DT - 1:
                            last.then_inc(y_done, 1)

                ab(u0, b0, first=split)
                with pe.Fori(0, (FSTEPS - 1) // 2) as i:
                    for h in range(2):
                        ab(u0 + 4 + 6 * h, b0 + 4 + 4 * h, i)
                        y(u0 + 8 + 6 * h, h, h, i)
                y(u0 + 4 + 6 * (FSTEPS - 1), FSTEPS - 1, 0)

            with pe.Fori(0, DEPTH) as L:
                pe.wait_ge(const_in, 16)
                ffn(L, U_FFN1, B_FFN1, 0, 0, 0)
                barrier(pe, L, 0)

                product(L, U_CONV, B_CONV, xh, xl, first=8)
                stat_sum(L, 1)
                for t in range(TT):
                    last = mm(ps[:, 5, t:t + 1], ssq[:, t * P:(t + 1) * P], ones[:, 0:1], start=True, stop=True)
                last.then_inc(s_sum, 1)
                for j in range(1, 4):
                    product(L, U_CONV + j, B_CONV + j, xh, xl)
                with pe.Fori(0, 3) as i:
                    for j in range(4):
                        product(L, U_CONV + 4 + j, B_CONV + 4 + j, xh, xl, i, 4, 4)
                for j in range(4):
                    product(L, U_CT + j, B_CT + j, xh, xl)
                s = U_GATE % SLOTS
                pe.wait_ge(w_split, unit(L, U_GATE + 1))
                pe.wait_ge(bank_free, lay(L, BANKS, B_GATE + 1))
                for t in range(TT):
                    for k in range(DT):
                        tk = slice(t * P, (t + 1) * P)
                        last = mm3(bank(B_GATE)[:, t * 48:(t + 1) * 48], xh[:, k, tk], xl[:, k, tk],
                                   wh[:, s, k * 48:(k + 1) * 48], wl[:, s, k * 48:(k + 1) * 48],
                                   t == 0 and k == 0, t == TT - 1 and k == DT - 1, skip_group_check=True)
                last.then_inc(w_used, 1)
                for c in range(2):
                    for j in range(4):
                        u = U_CMP + 4 * c + j
                        pe.wait_ge(w_split, unit(L, u + 1))
                        pe.wait_ge(yc_l, lay(L, 32, 16 * c + 4 * j + 4))
                        for m in range(2):
                            if j == 0:
                                pe.wait_ge(bank_free, lay(L, BANKS, B_CMP + 2 * c + m + 1))
                            for kk in range(4):
                                w = slice(kk * 256 + m * P, kk * 256 + (m + 1) * P)
                                r = (4 * j + kk) % 8
                                last = mm3(bank(B_CMP + 2 * c + m)[:, 0:P], wh[:, u % SLOTS, w], wl[:, u % SLOTS, w],
                                           ych[:, r, :], ycl[:, r, :], j == 0 and kk == 0, j == 3 and kk == 3)
                        last.then_inc(w_used, 1)
                s = U_W2 % SLOTS
                pe.wait_ge(w_split, unit(L, U_W2 + 1))
                pe.wait_ge(hid_l, lay(L, 2, 2))
                pe.wait_ge(bank_free, lay(L, BANKS, B_W2 + 2))
                for m in range(2):
                    w = slice(m * HD, (m + 1) * HD)
                    last = mm3(bank(B_W2)[:, 0:HD], hkh[:, m, :], hkl[:, m, :], wh[:, s, w], wl[:, s, w], m == 0, m == 1)
                last.then_inc(kc_ready, 1)
                for g in range(NKV):
                    for m in range(2):
                        w, r = slice(P + m * HD, P + (m + 1) * HD), slice(g * P, (g + 1) * P)
                        last = mm3(bank(B_W2 + 1)[:, g * HD:(g + 1) * HD], hvh[:, m, r], hvl[:, m, r], wh[:, s, w],
                                   wl[:, s, w], g == 0 and m == 0, g == 3 and m == 1, skip_group_check=True)
                last.then_inc(w_used, 1)

                def tok_block(i=None, c=0, b=0):
                    for j in range(4):
                        s = (U_TOK + j) % SLOTS
                        pe.wait_ge(w_split, unit(L, U_TOK + c + j + 1, i, 4))
                        for t in range(TT):
                            if j == 0:
                                pe.wait_ge(bank_free, lay(L, BANKS, B_TOK + b + t + 1, i, 4))
                            tk = slice(t * P, (t + 1) * P)
                            for kk in range(2):
                                w = slice(kk * 512, (kk + 1) * 512)
                                last = mm3(bank(B_TOK + t), xh[:, 2 * j + kk, tk], xl[:, 2 * j + kk, tk], wh[:, s, w],
                                           wl[:, s, w], j == 0 and kk == 0, j == 3 and kk == 1)
                        last.then_inc(w_used, 1)

                with pe.Fori(0, 2) as i:
                    tok_block(i)
                tok_block(None, 8, 8)
                tok_block(None, 12, 12)
                barrier(pe, L, 1)

                pe.wait_ge(kd_l, lay(L, TT + 1, 1))
                for c in range(2):
                    last = nc.tensor.transpose(ps[:, 6, c * P:(c + 1) * P],
                                               kcd[:, c, :, :].bitcast(F32).rearrange("p a d -> p (a d)"), ident)
                last.then_inc(k_tr, 1)
                for t in range(TT):
                    pe.wait_ge(kd_l, lay(L, TT + 1, t + 2))
                    for kind in range(2):
                        for c, kd in ((0, kdh), (1, kdl)):
                            b = 2 * kind + c
                            if t:
                                pe.wait_ge(k_ev, lay(L, 4 * TT + 1, 4 * (t - 1) + b + 2))
                            for g in range(NKV):
                                a = kd[:, kind * 4 + g, :, :].bitcast(F32).rearrange("p a d -> p (a d)")
                                last = nc.tensor.transpose(ps[:, b, g * P:(g + 1) * P], a, ident)
                            last.then_inc(k_tr, 1)
                pe.wait_ge(k_ev, lay(L, 4 * TT + 1, 4 * TT + 1))

                def turn_q(n):
                    pe.wait_ge(q_l, n)
                    for j in range(HPG):
                        last = nc.tensor.transpose(ps[:, 7, j * P:(j + 1) * P],
                                                   q2[:, j, :, :].bitcast(F32).rearrange("p a d -> p (a d)"), ident)
                    last.then_inc(q_tr, 1)

                turn_q(lay(L, 17, 1))
                for q in range(TT):
                    W = (q + 1) * P
                    settle(pe)
                    with pe.Fori(0, NKV) as g:
                        def a_(c):
                            return lay(L, 16, 4 * q + c, g, 1)

                        def q_(c):
                            return lay(L, 17, 4 * q + c, g, 1)

                        def h_(c):
                            return lay(L, 64, 16 * q + c, g, 4)

                        def scores(j):
                            if j >= 2:
                                pe.wait_ge(p_exp, h_(j - 1))
                            for kind in range(2):
                                o = ps[:, 2 * (j % 2) + kind, 0:W]
                                mm(o, q2T[:, j, :], kT[:, kind, 0, g, 0:W], start=True, stop=False)
                                mm(o, q2T[:, j, :], kT[:, kind, 1, g, 0:W], start=False, stop=False)
                                last = mm(o[:, W - P:W], ident_r[:, :], mask_r[:, :], start=False, stop=True)
                            last.then_inc(s_done, 1)

                        def turn(j):
                            pe.wait_ge(p_exp, h_(j + 1))
                            if j:
                                pe.wait_ge(pt_ev0, h_(j))
                                pe.wait_ge(pt_ev1, h_(j))
                            for kind in range(2):
                                for k in range(q + 1):
                                    last = nc.tensor.transpose(ps[:, 4 + kind, k * P:(k + 1) * P],
                                                               pr[:, j % 2, kind, k * P:(k + 1) * P], ident)
                            last.then_inc(pt_tr, 1)

                        def values(j):
                            pe.wait_ge(pt_ev0, h_(j + 1))
                            pe.wait_ge(pt_ev1, h_(j + 1))
                            for kind in range(2):
                                for k in range(q + 1):
                                    v = tkv[:, 1, k, bass.ds(g * HD + kind * KVW, HD)]
                                    last = mm(ps[:, 6, (kind * 4 + j) * HD:(kind * 4 + j + 1) * HD],
                                              ptk[:, j % 2, kind, k, :], v, start=k == 0, stop=k == q)
                            last.then_inc(pv_done, 1)

                        pe.wait_ge(q_ev, q_(1))
                        mm(ps[:, 7, 0:P], ident_r[:, :], cmask_r[:, q, :], start=True, stop=False,
                           skip_group_check=True)
                        for j in range(HPG):
                            for c in range(2):
                                last = mm(ps[:, 7, j * NCMP:(j + 1) * NCMP], q2T[:, j, :],
                                          kcT[:, c, bass.ds(g * NCMP, NCMP)], start=False,
                                          stop=j == 3 and c == 1, skip_group_check=True)
                        last.then_inc(sc_done, 1)
                        scores(0)
                        scores(1)
                        pe.wait_ge(pc_exp, a_(1))
                        nc.tensor.transpose(ps[:, 7, P:2 * P], pc[:, :], ident).then_inc(ptc_tr, 1)
                        turn(0)
                        pe.wait_ge(ptc_ev, a_(1))
                        mm(ps[:, 7, 2 * P:4 * P], ptc[:, :],
                           vcb[:, g, :, :].rearrange("p j d -> p (j d)"), start=True, stop=True).then_inc(oc_done, 1)
                        scores(2)
                        turn(1)
                        values(0)
                        scores(3)
                        pe.wait_ge(oc_read, a_(1))
                        turn_q(q_(2))
                        turn(2)
                        values(1)
                        turn(3)
                        values(2)
                        values(3)
                barrier(pe, L, 2)

                for m in range(DT):
                    last = mm(ps[:, 4, :], ones, acc[:, m, :], start=m == 0, stop=m == DT - 1)
                last.then_inc(ln_mu, 1)
                product(L, U_MERGE, B_MERGE, xh, xl, first=16)
                for m in range(DT):
                    if m >= 2:
                        pe.wait_ge(ot_l, lay(L, 8, m - 1))
                    for t in range(TT):
                        last = nc.tensor.transpose(ps[:, 6 + m % 2, t * P:(t + 1) * P], tq[:, t, m * P:(m + 1) * P],
                                                   ident)
                    last.then_inc(ot_tr, 1)
                    pe.wait_ge(ln_sq, lay(L, 8, m + 1))
                    mm(ps[:, 5, :], ones, sq[:, m % 2, :], start=m == 0, stop=m == DT - 1).then_inc(ln_var, 1)
                product(L, U_MERGE + 1, B_MERGE + 1, xh, xl)
                product(L, U_MERGE + 2, B_MERGE + 2, oh, ol, ready=ot_l)
                product(L, U_MERGE + 3, B_MERGE + 3, cvh, cvl, ready=ln_lo)
                with pe.Fori(0, DT - 1) as i:
                    for j, (rh, rl) in enumerate(((xh, xl), (xh, xl), (oh, ol), (cvh, cvl))):
                        product(L, U_MERGE + 4 + j, B_MERGE + 4 + j, rh, rl, i, 4, 4)
                barrier(pe, L, 3)
                product(L, U_OUT, B_OUT, xh, xl, first=24)
                for j in range(1, 4):
                    product(L, U_OUT + j, B_OUT + j, xh, xl)
                for j in range(4):
                    product(L, U_OUT + 4 + j, B_OUT + 4 + j, xh, xl)
                barrier(pe, L, 4)
                ffn(L, U_FFN2, B_FFN2, 1, 32, 2)
                barrier(pe, L, 5)

                def proj(j):
                    u = U_PROJ + j
                    pe.wait_ge(w_split, unit(L, u + 1))
                    for m in range(4):
                        b = B_PROJ + 4 * j + m
                        pe.wait_ge(bank_free, lay(L, BANKS, b + 1))
                        for k in range(2):
                            if j == 0 and m == 0:
                                pe.wait_ge(p_lo_, lay(L, 2, k + 1))
                            w = slice(k * 512 + m * P, k * 512 + (m + 1) * P)
                            last = mm3(bank(b), wh[:, u % SLOTS, w], wl[:, u % SLOTS, w], ph[:, k, :], pl[:, k, :],
                                       k == 0, k == 1)
                    last.then_inc(w_used, 1)

                proj(0)
                stat_sum(L, 3)
                proj(1)
                product(L, U_PLE, B_PLE, xh, xl, first=40)
                stat_sum(L, 4)
                for j in range(1, 4):
                    product(L, U_PLE + j, B_PLE + j, xh, xl)
                for j in range(4):
                    product(L, U_PLE + 4 + j, B_PLE + 4 + j, xh, xl)
                barrier(pe, L, 6)

        @block.scalar
        def _(act):
            seq = Chain(act, act_seq, "act.", settle)
            f = nc.scalar.activation

            def hi(L, c, i=None, pi=0):
                s = c % SLOTS
                act.wait_ge(w_used, unit(L, c + 1, i, pi))
                n = lay(L, UNITS // SLOTS, c // SLOTS + 2, i, pi // SLOTS)
                act.wait_ge(raw_in[s], n * 16)
                f(wh[:, s, :], raw[:, s, :], ACT.Copy).then_inc(w_hi, 1)

            def evacuated(L, b, i=None, bi=0):
                act.wait_ge(bank_free, lay(L, BANKS, b + 5, i, bi))

            def norm(L, ev, gain, stat):
                for k in range(DT):
                    f(xh[:, k, :], x[:, k, :], ACT.Copy, scale=col(gain + k)).then_inc(s_xh, 1)
                    if stat is not None:
                        if k >= 2:
                            act.wait_ge(s_ssq, lay(L, 40, 8 * stat + k - 1))
                        f(sq[:, k % 2, :], x[:, k, :], ACT.Square).then_inc(s_sq, 1)

            def root(L, si, t):
                act.wait_ge(s_rinv, lay(L, 6, si + 1))
                f(t, t, ACT.Sqrt).then_inc(s_rstd, 1)

            def ffn(L, u0, b0, which, ev, gain, stat, si):
                def ab(c, b, s, par, i=None):
                    for j in range(2):
                        hi(L, c + 2 * j, i, 12)
                        evacuated(L, b + 2 * j, i, 8)
                        f(fa[:, j, :], fa[:, j, :], ACT.Silu).then_inc(f_silu, 1)
                        hi(L, c + 2 * j + 1, i, 12)
                        act.wait_ge(f_h, lay(L, 2 * FT, which * FT + 2 * s + j + 1, i, 4))
                        f(hh[:, par, j, :], fb[:, j, :], ACT.Copy).then_inc(f_hh, 1)

                norm(L, ev, gain, stat)
                root(L, si, rstd[:, :])
                ab(u0, b0, 0, 0)
                with seq.loop("ffn", (FSTEPS - 1) // 2) as i:
                    for h in range(2):
                        ab(u0 + 4 + 6 * h, b0 + 4 + 4 * h, 1 + h, 1 - h, i)
                        hi(L, u0 + 8 + 6 * h, i, 12)
                        hi(L, u0 + 9 + 6 * h, i, 12)
                hi(L, u0 + 4 + 6 * (FSTEPS - 1))
                hi(L, u0 + 5 + 6 * (FSTEPS - 1))

            act.wait_ge(const_in, 16)
            f(ident_r[:, :], ident, ACT.Copy)
            act.wait_ge(mask_in, 16)
            f(mask_r[:, :], masks[:, K_MASK:K_MASK + P], ACT.Copy)
            f(cmask_r[:, :, :], masks[:, K_CM:K_CM + TT * P].rearrange("p (t k) -> p t k", t=TT),
              ACT.Copy).then_inc(con_r, 1)
            act.wait_ge(x_in, 16)
            for u in range(SLOTS):
                act.wait_ge(raw_in[u], 16)
                f(wh[:, u, :], raw[:, u, :], ACT.Copy).then_inc(w_hi, 1)

            with seq.loop("layer", DEPTH) as L:
                act.wait_ge(cols_in, lay(L, 16, 16))
                ffn(L, U_FFN1, B_FFN1, 0, 0, C_F1, 0, 0)
                barrier(act, L, 0)

                norm(L, 1, C_MIX, 1)
                root(L, 1, rstd[:, :])
                root(L, 2, rstd_t[:, :])

                def pair(m, c, b, i=None):
                    hi(L, c, i, 4)
                    hi(L, c + 1, i, 4)
                    evacuated(L, b + 1, i, 4)
                    f(cv[:, 1, :], cv[:, 1, :], ACT.Sigmoid, bias=col(m + C_BG)).then_inc(c_sig, 1)

                for j in range(2):
                    pair(j, U_CONV + 2 * j, B_CONV + 2 * j)
                with seq.loop("conv", 3) as i:
                    for j in range(2):
                        pair(i * 2 + (2 + j), U_CONV + 4 + 2 * j, B_CONV + 4 + 2 * j, i)
                for j in range(4):
                    hi(L, U_CT + j)
                    evacuated(L, B_CT + j)
                    f(ctb[:, j, :], ctb[:, j, :], ACT.Identity, bias=col(C_BCT + j)).then_inc(ct_ready, 1)
                hi(L, U_GATE)
                evacuated(L, B_GATE + 1)
                f(gates[:, :, :], gates[:, :, :], ACT.Sigmoid).then_inc(g_sig, 1)

                def block_in(jj):
                    c, j = jj // 16, jj % 16
                    if jj >= 8:
                        act.wait_ge(w_used, unit(L, U_CMP + (jj - 8) // 4 + 1))
                    f(ych[:, jj % 8, :].rearrange("p (h n) -> p h n", h=NKV), at_pos(c, j), ACT.Identity,
                      bias=col(C_POS + jj)).then_inc(yc_h, 1)

                act.wait_ge(xc_in, lay(L, 256, 256))
                for jj in range(8):
                    block_in(jj)
                for u in range(8):
                    hi(L, U_CMP + u)
                    if u % 4 == 3:
                        c = u // 4
                        evacuated(L, B_CMP + 2 * c + 1)
                        for m in range(2):
                            ins = f(hid[:, m, :], hid[:, m, :], ACT.Gelu_apprx_tanh, bias=col(C_B1 + 2 * c + m))
                        seq.link(ins)
                        if c == 0:
                            f(hkh[:, :, :], hid[:, :, :], ACT.Copy).then_inc(hid_h, 1)
                        else:
                            for m in range(2):
                                ins = f(hvh[:, m, :].rearrange("p (g j n) -> p g j n", g=NKV, j=HPG), copies(m), ACT.Copy)
                            ins.then_inc(hid_h, 1)
                    if u < 6:
                        for jj in range(8 + 4 * u, 12 + 4 * u):
                            block_in(jj)
                hi(L, U_W2)
                act.wait_ge(t_rinv, lay(L, 4, 1))
                f(small[:, 32:33], small[:, 32:33], ACT.Sqrt).then_inc(t_rs, 1)

                def tok_turns(i=None, c=0, b=0):
                    for j in range(4):
                        hi(L, U_TOK + c + j, i, 4)

                def head_norm(xt, n, i=None):
                    evacuated(L, B_TOK + 4 * n + 3, i, 4)
                    f(sqt[:, :, :], xt, ACT.Square).then_inc(t_sq, 1)
                    act.wait_ge(t_rinv, lay(L, 4, n + 2, i, 1))
                    f(small[:, 0:32], small[:, 0:32], ACT.Sqrt).then_inc(t_rs, 1)

                with seq.loop("tok", 2) as i:
                    tok_turns(i)
                    head_norm(tq[:, :, bass.ds(i * 512, 512)], 0, i)
                tok_turns(None, 8)
                head_norm(tkv[:, 0, :, :], 2)
                tok_turns(None, 12)
                barrier(act, L, 1)

                f(kcd[:, 0, :, :], twice(kc[:, :]), ACT.Copy).then_inc(kd_h, 1)
                for t in range(TT + 1):
                    if t < TT:
                        if t:
                            act.wait_ge(k_tr, lay(L, 17, 4 * t + 1))
                        f(kdh[:, :, :, :], keys_twice(t), ACT.Copy).then_inc(kd_h, 1)
                    if t == 0:
                        act.wait_ge(k_tr, lay(L, 17, 1))
                        f(kcT[:, :, :], ps[:, 6, 0:2 * P].rearrange("p (c k) -> p c k", c=2), ACT.Copy)\
                            .then_inc(k_ev, 1)
                        continue
                    for b in range(4):
                        act.wait_ge(k_tr, lay(L, 17, 4 * (t - 1) + b + 2))
                        f(kT[:, b // 2, b % 2, :, (t - 1) * P:t * P], ps[:, b, :].rearrange("p (g k) -> p g k", g=NKV),
                          ACT.Copy).then_inc(k_ev, 1)
                f(q2[:, :, 0, :], heads(0, 0), ACT.Copy).then_inc(q_h, 1)
                act.wait_ge(q_tr, lay(L, 17, 1))
                f(q2T[:, :, :], ps[:, 7, :].rearrange("p (j k) -> p j k", j=HPG), ACT.Copy).then_inc(q_ev, 1)
                for q in range(TT):
                    W = (q + 1) * P
                    with seq.loop("att", NKV) as g:
                        def a_(c):
                            return lay(L, 16, 4 * q + c, g, 1)

                        def h_(c):
                            return lay(L, 64, 16 * q + c, g, 4)

                        def exps(j):
                            act.wait_ge(s_max, h_(j + 1))
                            for kind in range(2):
                                n = 28 + 4 * kind + j
                                ins = f(pr[:, j % 2, kind, 0:W], ps[:, 2 * (j % 2) + kind, 0:W], ACT.Exp, scale=SCALE,
                                        bias=att[:, 16 + 2 * (j % 2) + kind:17 + 2 * (j % 2) + kind],
                                        accum_out=att[:, n:n + 1])
                            ins.then_inc(p_exp, 1)

                        def turned(j):
                            act.wait_ge(pt_tr, h_(j + 1))
                            f(ptk[:, j % 2, 0, 0:q + 1, :], ps[:, 4, 0:W].rearrange("p (t k) -> p t k", k=P),
                              ACT.Copy).then_inc(pt_ev0, 1)

                        act.wait_ge(sc_sub, a_(1))
                        f(pc[:, :], pcs[:, :, :].rearrange("p j n -> p (j n)"), ACT.Exp, scale=SCALE)\
                            .then_inc(pc_exp, 1)
                        exps(0)
                        exps(1)
                        f(q2[:, :, 0, :], heads(q, g, 1), ACT.Copy).then_inc(q_h, 1)
                        turned(0)
                        exps(2)
                        turned(1)
                        exps(3)
                        act.wait_ge(q_tr, lay(L, 17, 4 * q + 2, g, 1))
                        f(q2T[:, :, :], ps[:, 7, :].rearrange("p (j k) -> p j k", j=HPG), ACT.Copy).then_inc(q_ev, 1)
                        turned(2)
                        turned(3)
                barrier(act, L, 2)

                norm(L, 2, C_MIX, None)
                for m in range(DT):
                    act.wait_ge(ln_d, lay(L, 8, m + 1))
                    if m >= 2:
                        act.wait_ge(ln_var, lay(L, 8, m - 1))
                    f(sq[:, m % 2, :], acc[:, m, :], ACT.Square).then_inc(ln_sq, 1)
                    act.wait_ge(ot_tr, lay(L, 8, m + 1))
                    f(oh[:, m, :], ps[:, 6 + m % 2, :], ACT.Copy).then_inc(ot_h, 1)
                hi(L, U_MERGE)
                act.wait_ge(ln_rinv, lay(L, 1, 1))
                f(ssq[:, :], ssq[:, :], ACT.Sqrt).then_inc(ln_rs, 1)
                for m in range(DT):
                    act.wait_ge(ln_e, lay(L, 8, m + 1))
                    f(acc[:, m, :], acc[:, m, :], ACT.Silu, bias=col(C_LB + m), scale=col(C_LG + m)).then_inc(ln_f, 1)
                    if m:
                        act.wait_ge(ln_f, lay(L, 8, m))
                        f(cvh[:, m - 1, :], acc[:, m - 1, :], ACT.Copy).then_inc(ln_hi, 1)
                act.wait_ge(ln_f, lay(L, 8, 8))
                f(cvh[:, DT - 1, :], acc[:, DT - 1, :], ACT.Copy).then_inc(ln_hi, 1)

                def merge(m, c, i=None):
                    for j in range(4):
                        if c + j:
                            hi(L, U_MERGE + c + j, i, 4)
                        if j < 2:
                            evacuated(L, B_MERGE + c + j, i, 4)
                            f(mt[:, j, :], mt[:, j, :], ACT.Sigmoid, bias=col(m + (C_BGN if j else C_BGC)))\
                                .then_inc(m_sig, 1)

                merge(0, 0)
                with seq.loop("merge", DT - 1) as i:
                    merge(i + 1, 4, i)
                barrier(act, L, 3)
                for k in range(DT):
                    f(xh[:, k, :], yf[:, k, :], ACT.Copy).then_inc(s_xh, 1)
                for j in range(DT):
                    hi(L, U_OUT + j)
                barrier(act, L, 4)
                ffn(L, U_FFN2, B_FFN2, 1, 4, C_F2, 2, 3)
                barrier(act, L, 5)

                act.wait_ge(p_in, lay(L, 16, 16))
                for k in range(2):
                    f(ph[:, k, :], pf[:, k, :], ACT.Copy).then_inc(p_hi_, 1)
                norm(L, 5, C_PLE, 3)
                root(L, 4, rstd[:, :])
                for j in range(2):
                    hi(L, U_PROJ + j)
                for m in range(DT):
                    evacuated(L, B_PROJ + m)
                    if m >= 2:
                        act.wait_ge(s_ssq, lay(L, 40, 32 + m - 1))
                    f(sq[:, m % 2, :], pe_[:, m, :], ACT.Square).then_inc(s_sq, 1)
                for m in range(DT):
                    hi(L, U_PLE + m)
                    if m == 0:
                        root(L, 5, ssq[:, :])
                    evacuated(L, B_PLE + m)
                    f(fb[:, m % 2, :], fa[:, m % 2, :], ACT.Sigmoid).then_inc(g_s, 1)
                barrier(act, L, 6)

        @block.vector
        def _(dve):
            seq = Chain(dve, dve_seq, "dve.", settle)
            link = seq.link
            v = nc.vector
            tt, ts, stt = v.tensor_tensor, v.tensor_scalar, v.scalar_tensor_tensor
            MUL, ADD, SUB = ALU.mult, ALU.add, ALU.subtract

            def f32(ap):
                return ap.bitcast(F32)

            def lo(L, c, i=None, pi=0):
                s = c % SLOTS
                dve.wait_ge(w_hi, unit(L, c + 5, i, pi))
                tt(wl[:, s, :], raw[:, s, :], f32(wh[:, s, :]), SUB).then_inc(w_split, 1)

            def used(L, c, i=None, pi=0):
                dve.wait_ge(w_used, unit(L, c + 1, i, pi))

            def evacuated(L, b, i=None, bi=0):
                dve.wait_ge(bank_free, lay(L, BANKS, b + 5, i, bi))

            def scaled(dst, L, c, b, i=None, pi=0, bi=0):
                used(L, c, i, pi)
                tt(dst, ps[:, b % SLOTS, :], rstd[:, :], MUL).then_inc(bank_free, 1)

            def norm(L, ev, gain, stat):
                for k in range(DT):
                    dve.wait_ge(s_xh, lay(L, 48, 8 * ev + k + 1))
                    stt(xl[:, k, :], x[:, k, :], col(gain + k), f32(xh[:, k, :]), MUL, SUB).then_inc(s_xl, 1)
                    if stat is not None:
                        add_square(L, stat, k)

            def add_square(L, stat, k):
                dve.wait_ge(s_sq, lay(L, 40, 8 * stat + k + 1))
                if k == 0:
                    v.tensor_copy(ssq[:, :], sq[:, 0, :]).then_inc(s_ssq, 1)
                else:
                    dve.wait_ge(s_ssq, lay(L, 40, 8 * stat + k))
                    tt(ssq[:, :], ssq[:, :], sq[:, k % 2, :], ADD).then_inc(s_ssq, 1)

            def mean(L, si, dst, src):
                dve.wait_ge(s_sum, lay(L, 6, si + 1))
                link(ts(dst, src, 1.0 / D, EPS, MUL, ADD))
                v.reciprocal(dst, dst).then_inc(s_rinv, 1)

            def rooted(L, si):
                dve.wait_ge(s_rstd, lay(L, 6, si + 1))

            def ffn(L, u0, b0, which, ev, gain, stat, si):
                def ab(c, b, s, par, i=None):
                    for j in range(2):
                        scaled(fa[:, j, :], L, c + 2 * j, b + 2 * j, i, 12, 8)
                        lo(L, c + 2 * j, i, 12)
                        scaled(fb[:, j, :], L, c + 2 * j + 1, b + 2 * j + 1, i, 12, 8)
                        n = which * FT + 2 * s + j + 1
                        dve.wait_ge(f_silu, lay(L, 2 * FT, n, i, 4))
                        evacuated(L, b + 2 * j + 1, i, 8)
                        tt(fb[:, j, :], fb[:, j, :], fa[:, j, :], MUL).then_inc(f_h, 1)
                        lo(L, c + 2 * j + 1, i, 12)
                        dve.wait_ge(f_hh, lay(L, 2 * FT, n, i, 4))
                        tt(hl[:, par, j, :], fb[:, j, :], f32(hh[:, par, j, :]), SUB).then_inc(f_hl, 1)

                def y(c, s, i=None):
                    n = which * FSTEPS + s
                    dve.wait_ge(y_free, lay(L, 16 * FSTEPS, 8 * n + 4, i, 16))
                    for m in range(DT):
                        if m < DT - 1:
                            dve.wait_ge(y_done, lay(L, 14 * FSTEPS, 7 * n + m + 1, i, 14))
                        else:
                            used(L, c + 1, i, 12)
                        stt(x[:, m, :], ps[:, 4 + m % 4, :], 0.5, x[:, m, :], MUL, ADD).then_inc(y_free, 1)
                    lo(L, c, i, 12)
                    lo(L, c + 1, i, 12)

                norm(L, ev, gain, stat)
                mean(L, si, rstd[:, :], ps[:, 4, :])
                rooted(L, si)
                ab(u0, b0, 0, 0)
                with seq.loop("ffn", (FSTEPS - 1) // 2) as i:
                    for h in range(2):
                        ab(u0 + 4 + 6 * h, b0 + 4 + 4 * h, 1 + h, 1 - h, i)
                        y(u0 + 8 + 6 * h, h, i)
                y(u0 + 4 + 6 * (FSTEPS - 1), FSTEPS - 1)

            v.memset(att[:, 0:1], 0.0).then_inc(bank_free, SLOTS)
            v.memset(att[:, 1:2], 0.0).then_inc(y_free, 4)
            dve.wait_ge(x_in, 16)
            dve.wait_ge(const_in, 16)
            for u in range(SLOTS):
                dve.wait_ge(w_hi, u + 1)
                tt(wl[:, u, :], raw[:, u, :], f32(wh[:, u, :]), SUB).then_inc(w_split, 1)

            with seq.loop("layer", DEPTH) as L:
                dve.wait_ge(cols_in, lay(L, 16, 16))
                ffn(L, U_FFN1, B_FFN1, 0, 0, C_F1, 0, 0)
                barrier(dve, L, 0)

                norm(L, 1, C_MIX, 1)
                mean(L, 1, rstd[:, :], ps[:, 4, :])
                mean(L, 2, rstd_t[:, :], ps[:, 5, 0:TT])
                link(v.memset(ch[:, :, 0:CONV_K - 1], 0.0))
                rooted(L, 2)

                def taps(m, k0, k1):
                    for k in range(k0, k1):
                        w = col(m * CONV_K + (C_CW + k))
                        src = ch[:, m, k:k + T]
                        if k == 0:
                            link(ts(acc[:, m, :], src, w, col(m + C_CB), MUL, ADD))
                        else:
                            link(stt(acc[:, m, :], src, w, acc[:, m, :], MUL, ADD))

                FIRST, MID = 8, 15

                def pair(m, c, b, i=None):
                    scaled(cv[:, 0, :], L, c, b, i, 4, 4)
                    lo(L, c, i, 4)
                    scaled(cv[:, 1, :], L, c + 1, b + 1, i, 4, 4)
                    lo(L, c + 1, i, 4)
                    dve.wait_ge(c_sig, L * DT + m + 1)
                    link(stt(ch[:, m, CONV_K - 1:CONV_K - 1 + T], cv[:, 0, :], col(m + C_BA), cv[:, 1, :], ADD, MUL))
                    taps(m, 0, FIRST)

                for j in range(2):
                    pair(j, U_CONV + 2 * j, B_CONV + 2 * j)
                with seq.loop("conv", 3) as i:
                    for j in range(2):
                        pair(i * 2 + (2 + j), U_CONV + 4 + 2 * j, B_CONV + 4 + 2 * j, i)
                for j in range(4):
                    scaled(ctb[:, j, :], L, U_CT + j, B_CT + j)
                    lo(L, U_CT + j)
                    if j % 2:
                        taps(j // 2, FIRST, MID)
                dve.wait_ge(rows_in, lay(L, 16, 16))
                used(L, U_GATE)
                for t in range(TT):
                    ins = stt(gates[:, t, :], ps[:, B_GATE % SLOTS, t * 48:(t + 1) * 48], rstd_t[:, t:t + 1],
                              row[:, R_BG:R_KC], MUL, ADD)
                ins.then_inc(bank_free, 2)
                lo(L, U_GATE)

                def block_rest(jj):
                    dve.wait_ge(yc_h, lay(L, 32, jj + 1))
                    stt(ycl[:, jj % 8, :].rearrange("p (h n) -> p h n", h=NKV), at_pos(jj // 16, jj % 16),
                        col(C_POS + jj), f32(ych[:, jj % 8, :]).rearrange("p (h n) -> p h n", h=NKV),
                        ADD, SUB).then_inc(yc_l, 1)

                for jj in range(8):
                    block_rest(jj)
                for u in range(8):
                    used(L, U_CMP + u)
                    c = u // 4
                    if u % 4 == 3:
                        for m in range(2):
                            v.tensor_copy(hid[:, m, :], ps[:, (B_CMP + 2 * c + m) % SLOTS, 0:P]).then_inc(bank_free, 1)
                    lo(L, U_CMP + u)
                    if u < 6:
                        for jj in range(8 + 4 * u, 12 + 4 * u):
                            block_rest(jj)
                    if u % 4 == 1:
                        taps(2 + c, FIRST, MID)
                    if u % 4 == 3:
                        dve.wait_ge(hid_h, lay(L, 2, c + 1))
                        if c == 0:
                            tt(hkl[:, :, :], hid[:, :, :], f32(hkh[:, :, :]), SUB).then_inc(hid_l, 1)
                        else:
                            for m in range(2):
                                ins = tt(hvl[:, m, :].rearrange("p (g j n) -> p g j n", g=NKV, j=HPG), copies(m),
                                         f32(hvh[:, m, :]).rearrange("p (g j n) -> p g j n", g=NKV, j=HPG), SUB)
                            ins.then_inc(hid_l, 1)

                def rope(x1, x2, cos, sin, tmp):
                    tt(tmp[0], x1, cos, MUL)
                    tt(tmp[1], x2, sin, MUL)
                    tt(tmp[2], x2, cos, MUL)
                    link(tt(tmp[3], x1, sin, MUL))
                    tt(x1, tmp[0], tmp[1], SUB)
                    link(tt(x2, tmp[2], tmp[3], ADD))

                dve.wait_ge(kc_ready, lay(L, 1, 1))
                v.tensor_copy(kc[:, :], ps[:, B_W2 % SLOTS, 0:HD]).then_inc(bank_free, 1)
                used(L, U_W2)
                dve.wait_ge(vcb_zero, lay(L, 1, 1))
                for j in range(HPG):
                    r = slice(NCMP * j, NCMP * (j + 1))
                    ins = v.tensor_copy(vcb[r, :, j, :],
                                        ps[r, (B_W2 + 1) % SLOTS, 0:NKV * HD].rearrange("p (g d) -> p g d", g=NKV))
                ins.then_inc(bank_free, 1)
                lo(L, U_W2)
                evacuated(L, B_W2)
                link(tt(kcw[:, :], kc[:, :], kc[:, :], MUL))
                link(v.reduce_sum(small[:, 32:33], kcw[:, :], AX.X))
                link(ts(small[:, 32:33], small[:, 32:33], 1.0 / HD, EPS, MUL, ADD))
                v.reciprocal(small[:, 32:33], small[:, 32:33]).then_inc(t_rinv, 1)
                dve.wait_ge(t_rs, lay(L, 4, 1))
                link(stt(kc[:, :], kc[:, :], small[:, 32:33], row[:, R_KC:R_KC + HD], MUL, MUL))
                rope(kc[:, 0:HALF], kc[:, HALF:2 * HALF], con_[:, K_COSC:K_COSC + HALF], con_[:, K_SINC:K_SINC + HALF],
                     [kcw[:, n * HALF:(n + 1) * HALF] for n in range(4)])

                def tok_block(xt, n, m, i=None):
                    for j in range(4):
                        used(L, U_TOK + 4 * n + j, i, 4)
                        if j == 3:
                            bias = row[:, bass.ds(i * 512 + R_B, 512)] if i is not None \
                                else row[:, R_B + n * 512:R_B + (n + 1) * 512]
                            for t in range(TT):
                                stt(xt[:, t, :], ps[:, (B_TOK + t) % SLOTS, :], rstd_t[:, t:t + 1], bias,
                                    MUL, ADD).then_inc(bank_free, 1)
                        lo(L, U_TOK + 4 * n + j, i, 4)
                    taps(m, FIRST, MID)

                def table(c):
                    return con_[:, c:c + 32].rearrange("p (t o e) -> p t o e", t=TT, o=1)\
                        .broadcast_to([P, TT, 8, HALF])

                def head_norm(xt, n, i=None):
                    dve.wait_ge(t_sq, lay(L, 3, n + 1, i, 1))
                    link(v.reduce_sum(small[:, 0:32], sqt[:, :, :].rearrange("p t (h d) -> p (t h) d", d=HD), AX.X))
                    link(ts(small[:, 0:32], small[:, 0:32], 1.0 / HD, EPS, MUL, ADD))
                    v.reciprocal(small[:, 0:32], small[:, 0:32]).then_inc(t_rinv, 1)
                    gain = row[:, bass.ds(i * 512 + R_G, 512)] if i is not None \
                        else row[:, R_G + n * 512:R_G + (n + 1) * 512]
                    gain = gain.rearrange("p (o n) -> p o n", o=1)
                    link(tt(xt, xt, gain.broadcast_to([P, TT, 512]), MUL))
                    dve.wait_ge(t_rs, lay(L, 4, n + 2, i, 1))
                    xt = xt.rearrange("p t (h d) -> p t h d", d=HD)
                    rs = small[:, 0:32].rearrange("p (t h o) -> p t h o", h=8, o=1)
                    link(tt(xt, xt, rs.broadcast_to([P, TT, 8, HD]), MUL))
                    rope(xt[:, :, :, 0:HALF], xt[:, :, :, HALF:2 * HALF], table(K_COS), table(K_SIN),
                         [sqt[:, c, 0:256].rearrange("p (t h e) -> p t h e", t=TT, h=8) for c in range(4)])

                with seq.loop("tok", 2) as i:
                    xt = tq[:, :, bass.ds(i * 512, 512)]
                    tok_block(xt, 0, i + 4, i)
                    head_norm(xt, 0, i)
                tok_block(tkv[:, 0, :, :], 2, 6)
                head_norm(tkv[:, 0, :, :], 2)
                tok_block(tkv[:, 1, :, :], 3, 7)
                barrier(dve, L, 1)

                gc = gates[:, :, :].rearrange("p t (h c) -> p t h c", c=3)[:, :, :, 0]
                dve.wait_ge(g_sig, lay(L, 1, 1))
                link(tt(gc, gc, con_[:, K_VALID:K_VALID + TT].rearrange("p (t o) -> p t o", o=1)
                        .broadcast_to([P, TT, NH]), MUL))
                dve.wait_ge(kd_h, lay(L, TT + 1, 1))
                tt(kcd[:, 1, :, :], twice(kc[:, :]), f32(kcd[:, 0, :, :]), SUB).then_inc(kd_l, 1)
                for t in range(TT):
                    dve.wait_ge(kd_h, lay(L, TT + 1, t + 2))
                    tt(kdl[:, :, :, :], keys_twice(t), f32(kdh[:, :, :, :]), SUB).then_inc(kd_l, 1)
                dve.wait_ge(q_h, lay(L, 17, 1))
                tt(q2[:, :, 1, :], heads(0, 0), f32(q2[:, :, 0, :]), SUB).then_inc(q_l, 1)

                for q in range(TT):
                    W = (q + 1) * P
                    with seq.loop("att", NKV) as g:
                        def a_(c):
                            return lay(L, 16, 4 * q + c, g, 1)

                        def h_(c):
                            return lay(L, 64, 16 * q + c, g, 4)

                        def row_max(j):
                            r = j % 2
                            dve.wait_ge(s_done, h_(j + 1))
                            link(v.tensor_reduce(att[:, 8 + 2 * r:10 + 2 * r], ps[:, 2 * r:2 * r + 2, 0:W], AX.X, ALU.max))
                            ts(att[:, 16 + 2 * r:18 + 2 * r], att[:, 8 + 2 * r:10 + 2 * r], -SCALE, None, MUL)\
                                .then_inc(s_max, 1)

                        def turned(j):
                            dve.wait_ge(pt_tr, h_(j + 1))
                            v.tensor_copy(ptk[:, j % 2, 1, 0:q + 1, :],
                                          ps[:, 5, 0:W].rearrange("p (t k) -> p t k", k=P)).then_inc(pt_ev1, 1)

                        dve.wait_ge(sc_done, a_(1))
                        sc = ps[:, 7, 0:P].rearrange("p (j n) -> p j n", j=HPG)
                        link(v.tensor_reduce(att[:, 0:4], sc, AX.X, ALU.max))
                        tt(pcs[:, :, :], sc, att[:, 0:4].rearrange("p (j o) -> p j o", o=1)
                           .broadcast_to([P, HPG, NCMP]), SUB).then_inc(sc_sub, 1)
                        row_max(0)
                        row_max(1)
                        dve.wait_ge(ptc_tr, a_(1))
                        v.tensor_copy(ptc[:, :], ps[:, 7, P:2 * P]).then_inc(ptc_ev, 1)
                        link(v.reduce_sum(att[:, 24:28], pc[:, :].rearrange("p (j n) -> p j n", j=HPG), AX.X))
                        link(v.reciprocal(att[:, 52:56], att[:, 24:28]))

                        def gate(c, n):
                            return gates[:, q, bass.ds(g * 12, 12)].rearrange("p (j c) -> p c j", c=3)[:, c:c + n, :]

                        def weight(c):
                            return att[:, 40 + 4 * c:44 + 4 * c].rearrange("p (j o) -> p j o", o=1)\
                                .broadcast_to([P, HPG, HD])

                        def more_taps(n):
                            for k in range(n, n + 2):
                                for m in range(2 * q, 2 * q + 2):
                                    link(stt(acc[:, m, :], ch[:, m, bass.ds(g * 4 + (MID + k), T)],
                                             col(g * 4 + (C_CW + m * CONV_K + MID + k)), acc[:, m, :], MUL, ADD))

                        o = heads(q, g)
                        link(tt(att[:, 40:44], att[:, 52:56], gate(0, 1).rearrange("p c j -> p (c j)"), MUL))
                        dve.wait_ge(q_h, lay(L, 17, 4 * q + 2, g, 1))
                        tt(q2[:, :, 1, :], heads(q, g, 1), f32(q2[:, :, 0, :]), SUB).then_inc(q_l, 1)
                        turned(0)
                        row_max(2)
                        dve.wait_ge(oc_done, a_(1))
                        tt(o, ps[:, 7, 2 * P:4 * P].rearrange("p (j d) -> p j d", j=HPG), weight(0), MUL)\
                            .then_inc(oc_read, 1)
                        turned(1)
                        row_max(3)
                        more_taps(0)
                        turned(2)
                        more_taps(2)
                        turned(3)
                        link(v.reciprocal(att[:, 56:64], att[:, 28:36]))
                        link(tt(att[:, 44:52].rearrange("p (c j) -> p c j", c=2),
                                att[:, 56:64].rearrange("p (c j) -> p c j", c=2), gate(1, 2), MUL))
                        dve.wait_ge(pv_done, h_(4))
                        dve.wait_ge(oc_read, a_(1))
                        link(tt(ot[:, :, :], ps[:, 6, 0:256].rearrange("p (j d) -> p j d", j=HPG), weight(1), MUL))
                        link(tt(o, o, ot[:, :, :], ADD))
                        link(tt(ot[:, :, :], ps[:, 6, 256:512].rearrange("p (j d) -> p j d", j=HPG), weight(2), MUL))
                        link(tt(o, o, ot[:, :, :], ADD))
                barrier(dve, L, 2)

                def branch_gate(j, c, i=None):
                    scaled(mt[:, j, :], L, U_MERGE + c + j, B_MERGE + c + j, i, 4, 4)
                    lo(L, U_MERGE + c + j, i, 4)

                def branch_out(m, c, i=None):
                    dve.wait_ge(m_sig, lay(L, 2 * DT, 2 + c // 2, i, 2))
                    for j in range(2, 4):
                        used(L, U_MERGE + c + j, i, 4)
                        tt(mt[:, j, :], ps[:, (B_MERGE + j) % SLOTS, :], mt[:, 3 - j, :], MUL).then_inc(bank_free, 1)
                        lo(L, U_MERGE + c + j, i, 4)
                    evacuated(L, B_MERGE + c + 3, i, 4)
                    link(tt(yf[:, m, :], mt[:, 2, :], mt[:, 3, :], ADD))

                norm(L, 2, C_MIX, None)
                dve.wait_ge(ln_mu, lay(L, 1, 1))
                for m in range(DT):
                    stt(acc[:, m, :], ps[:, 4, :], -1.0 / D, acc[:, m, :], MUL, ADD).then_inc(ln_d, 1)
                for m in range(DT):
                    dve.wait_ge(ot_h, lay(L, 8, m + 1))
                    tt(ol[:, m, :], ps[:, 6 + m % 2, :], f32(oh[:, m, :]), SUB).then_inc(ot_l, 1)
                dve.wait_ge(ln_var, lay(L, 8, 8))
                link(ts(ssq[:, :], ps[:, 5, :], 1.0 / D, EPS, MUL, ADD))
                v.reciprocal(ssq[:, :], ssq[:, :]).then_inc(ln_rinv, 1)
                branch_gate(0, 0)
                dve.wait_ge(ln_rs, lay(L, 1, 1))
                dve.wait_ge(ln_d, lay(L, 8, 8))
                for m in range(DT):
                    tt(acc[:, m, :], acc[:, m, :], ssq[:, :], MUL).then_inc(ln_e, 1)
                for m in range(DT):
                    dve.wait_ge(ln_hi, lay(L, 8, m + 1))
                    tt(cvl[:, m, :], acc[:, m, :], f32(cvh[:, m, :]), SUB).then_inc(ln_lo, 1)
                branch_gate(1, 0)
                branch_out(0, 0)
                with seq.loop("merge", DT - 1) as i:
                    branch_gate(0, 4, i)
                    branch_gate(1, 4, i)
                    branch_out(i + 1, 4, i)
                barrier(dve, L, 3)
                for k in range(DT):
                    dve.wait_ge(s_xh, lay(L, 48, 24 + k + 1))
                    tt(xl[:, k, :], yf[:, k, :], f32(xh[:, k, :]), SUB).then_inc(s_xl, 1)
                for m in range(DT):
                    used(L, U_OUT + m)
                    tt(x[:, m, :], ps[:, (B_OUT + m) % SLOTS, :], x[:, m, :], ADD).then_inc(bank_free, 1)
                    lo(L, U_OUT + m)
                barrier(dve, L, 4)
                ffn(L, U_FFN2, B_FFN2, 1, 4, C_F2, 2, 3)
                barrier(dve, L, 5)

                for k in range(2):
                    dve.wait_ge(p_hi_, lay(L, 2, k + 1))
                    tt(pl[:, k, :], pf[:, k, :], f32(ph[:, k, :]), SUB).then_inc(p_lo_, 1)
                norm(L, 5, C_PLE, 3)
                mean(L, 4, rstd[:, :], ps[:, 4, :])
                for j in range(2):
                    used(L, U_PROJ + j)
                    for m in range(4 * j, 4 * j + 4):
                        v.tensor_copy(pe_[:, m, :], ps[:, (B_PROJ + m) % SLOTS, :]).then_inc(bank_free, 1)
                    lo(L, U_PROJ + j)
                for m in range(DT):
                    add_square(L, 4, m)
                rooted(L, 4)
                for m in range(DT):
                    scaled(fa[:, m % 2, :], L, U_PLE + m, B_PLE + m)
                    lo(L, U_PLE + m)
                    if m == 0:
                        mean(L, 5, ssq[:, :], ps[:, 4, :])
                        rooted(L, 5)
                        for k in range(DT):
                            ins = stt(pe_[:, k, :], pe_[:, k, :], col(C_POST + k), ssq[:, :], MUL, MUL)
                        link(ins)
                    dve.wait_ge(g_s, lay(L, DT, m + 1))
                    link(tt(fb[:, m % 2, :], fb[:, m % 2, :], pe_[:, m, :], MUL))
                    link(tt(x[:, m, :], x[:, m, :], fb[:, m % 2, :], ADD))
                barrier(dve, L, 6)


_OUT = "out_0_dram"


def kernel(**inputs):
    import concourse.bacc as bacc
    from concourse.bass_utils import run_bass_kernel_spmd

    i = {k: np.asarray(a) for k, a in inputs.items()}
    stream, cols, rows = pack(i)
    con, masks = constants()
    arrays = {
        "stream": stream, "cols": cols, "rows": rows, "const": con, "masks": masks,
        "xT": np.ascontiguousarray(i["x"][0].T.reshape(DT, P, T).transpose(1, 0, 2)),
        "pT": np.ascontiguousarray(i["p"][:, 0].transpose(0, 2, 1).reshape(DEPTH, 2, P, T).transpose(0, 2, 1, 3)),
    }
    nc = bacc.Bacc("TRN2", target_bir_lowering=False, num_devices=1)
    args = [nc.dram_tensor(n, a.shape, F32, kind="ExternalInput").ap() for n, a in arrays.items()]
    out = nc.dram_tensor(_OUT, (P, DT, T), F32, kind="ExternalOutput").ap()
    build(nc, *args, out)
    got = run_bass_kernel_spmd(nc, [arrays], core_ids=[0]).results[0][_OUT]
    return np.ascontiguousarray(np.asarray(got).transpose(2, 1, 0).reshape(1, T, D))
```

```python
from contextlib import ExitStack

import numpy as np

import concourse.bass as bass
from concourse import mybir

F32 = mybir.dt.float32
F32R = mybir.dt.float32r
ALU = mybir.AluOpType
ACT = mybir.ActivationFunctionType
AX = mybir.AxisListType

P = 128
D, T, DEPTH = 1024, 512, 2
DT = D // P
TT = T // P
FF = 2816
FT = FF // P
FSTEPS = FT // 2
PLE = 256
CONV_K = 31
NH, NKV, HPG, HD = 16, 4, 4, 64
HALF = 8
ROPE_THETA = 500000.0
CMP_LEN, CMP_STRIDE, CMP_HID = 32, 16, 256
NCMP = T // CMP_STRIDE
KVW = NKV * HD
OFF_Q = 2 * D
OFF_KV = OFF_Q + NH * HD
OFF_GATE = OFF_KV + 6 * KVW
OFF_MERGE = OFF_GATE + 3 * NH
NEG = -1e30
EPS = 1e-6
SCALE = HD ** -0.5
XTOK = T + CMP_STRIDE

SLOTS = 4
U_FFN1 = 0
U_CONV = U_FFN1 + 3 * FT
U_CT = U_CONV + 2 * DT
U_GATE = U_CT + 4
U_CMP = U_GATE + 1
U_W2 = U_CMP + 8
U_TOK = U_W2 + 1
U_MERGE = U_TOK + 16
U_OUT = U_MERGE + 4 * DT
U_FFN2 = U_OUT + DT
U_PROJ = U_FFN2 + 3 * FT
U_PLE = U_PROJ + 2
UNITS = U_PLE + DT
assert UNITS % SLOTS == 0
B_FFN1 = 0
B_CONV = B_FFN1 + 2 * FT
B_CT = B_CONV + 2 * DT
B_GATE = B_CT + 4
B_CMP = B_GATE + 2
B_W2 = B_CMP + 4
B_TOK = B_W2 + 2
B_MERGE = B_TOK + 16
B_OUT = B_MERGE + 4 * DT
B_FFN2 = B_OUT + DT
B_PROJ = B_FFN2 + 2 * FT
B_PLE = B_PROJ + DT
BANKS = B_PLE + DT
assert BANKS % SLOTS == 0
BARRIERS = 7
STATS = 4
NSPLIT = 7

C_F1, C_MIX, C_F2, C_PLE, C_POST, C_BA, C_BG, C_BGC, C_BGN = range(0, 72, 8)
C_BCT, C_CB, C_LG, C_LB, C_POS, C_B1, C_CW = 72, 76, 84, 92, 100, 132, 136
NCOL = C_CW + DT * CONV_K
R_B, R_G, R_BG, R_KC = 0, 2048, 3584, 3632
NROW = R_KC + HD
K_ID, K_ONE, K_COS, K_SIN, K_COSC, K_SINC, K_VALID, NCON = 0, 128, 256, 288, 320, 328, 336, 340
K_MASK, K_CM, NMASK = 0, 128, 640


def constants():
    c = np.zeros((P, NCON), np.float32)
    masks = np.zeros((P, NMASK), np.float32)
    c[:, K_ID:K_ID + P] = np.eye(P)
    r = np.arange(P)
    masks[:, K_MASK:K_MASK + P] = np.where(r[None, :] <= r[:, None], 0.0, NEG)
    c[:, K_ONE:K_ONE + P] = 1.0
    inv = (np.float32(ROPE_THETA) ** (-np.arange(HALF, dtype=np.float32) / np.float32(HALF))).astype(np.float32)
    n = np.arange(NCMP)
    for q in range(TT):
        t = q * P + r
        seen = (n[None, :] * CMP_STRIDE + CMP_LEN - 1 <= t[:, None]) & (n[None, :] < NCMP - 1)
        masks[:, K_CM + q * P:K_CM + (q + 1) * P] = np.tile(np.where(seen, 0.0, NEG), (1, 4))
        ang = (t.astype(np.float32)[:, None] * inv[None, :]).astype(np.float32)
        c[:, K_COS + q * HALF:K_COS + (q + 1) * HALF] = np.cos(ang)
        c[:, K_SIN + q * HALF:K_SIN + (q + 1) * HALF] = np.sin(ang)
        c[:, K_VALID + q] = t >= CMP_LEN - 1
    pos = ((r % NCMP) * CMP_STRIDE + CMP_LEN - 1).astype(np.float32)
    ang = (pos[:, None] * inv[None, :]).astype(np.float32)
    c[:, K_COSC:K_COSC + HALF] = np.cos(ang)
    c[:, K_SINC:K_SINC + HALF] = np.sin(ang)
    return c, masks


def pack(i):
    stream = np.zeros((DEPTH * UNITS + SLOTS, P, 1024), np.float32)
    cols = np.zeros((DEPTH + 1, P, NCOL), np.float32)
    rows = np.zeros((DEPTH, NROW), np.float32)

    def tiles(w):
        return w.reshape(w.shape[0] // P, P, w.shape[1]).transpose(1, 0, 2).reshape(P, -1)

    def cm(v):
        return v.reshape(-1, P).T

    for l in range(DEPTH):
        out = stream[l * UNITS:(l + 1) * UNITS]

        def ffn(u, w1, w2):
            for s in range(FSTEPS + 1):
                if s < FSTEPS:
                    for j in range(2):
                        for c in range(2):
                            m = c * FF + (2 * s + j) * P
                            out[u] = tiles(w1[:, m:m + P])
                            u += 1
                if s > 0:
                    for j in range(2):
                        f = (2 * (s - 1) + j) * P
                        out[u] = w2[f:f + P]
                        u += 1

        def cols_of(u, w, n):
            for m in range(n):
                out[u + m] = tiles(w[:, m * P:(m + 1) * P])

        ffn(U_FFN1, i["ffn1_w_in"][l], i["ffn1_w_out"][l])
        ffn(U_FFN2, i["ffn2_w_in"][l], i["ffn2_w_out"][l])
        w, b = i["w_in"][l], i["b_in"][l]
        kv = [slice(OFF_KV + j * KVW, OFF_KV + (j + 1) * KVW) for j in range(6)]
        for m in range(DT):
            out[U_CONV + 2 * m] = tiles(w[:, m * P:(m + 1) * P])
            out[U_CONV + 2 * m + 1] = tiles(w[:, D + m * P:D + (m + 1) * P])
            u = U_MERGE + 4 * m
            out[u] = tiles(w[:, OFF_MERGE + m * P:OFF_MERGE + (m + 1) * P])
            out[u + 1] = tiles(w[:, OFF_MERGE + D + m * P:OFF_MERGE + D + (m + 1) * P])
            out[u + 2] = tiles(i["nsa_w_out"][l][:, m * P:(m + 1) * P])
            out[u + 3] = tiles(i["conv_w_out"][l][:, m * P:(m + 1) * P])
        cols_of(U_CT, w[:, kv[0].start:kv[1].stop], 4)
        out[U_GATE][:, :8 * 48] = tiles(w[:, OFF_GATE:OFF_MERGE])
        for c in range(2):
            w1 = tiles(i["cmp_w1"][l, c]).reshape(P, 4, 1024)
            for j in range(4):
                out[U_CMP + 4 * c + j] = w1[:, j]
            out[U_W2][:, c * 128:(c + 1) * 128] = tiles(i["cmp_w2"][l, c])
        blocks = [(w[:, OFF_Q:OFF_Q + 512], b[OFF_Q:OFF_Q + 512]),
                  (w[:, OFF_Q + 512:OFF_KV], b[OFF_Q + 512:OFF_KV]),
                  (np.concatenate([w[:, kv[2]], w[:, kv[4]]], 1), np.concatenate([b[kv[2]], b[kv[4]]])),
                  (np.concatenate([w[:, kv[3]], w[:, kv[5]]], 1), np.concatenate([b[kv[3]], b[kv[5]]]))]
        for n, (wb, bb) in enumerate(blocks):
            wb = tiles(wb)
            for j in range(4):
                out[U_TOK + 4 * n + j] = wb[:, j * 1024:(j + 1) * 1024]
            rows[l, R_B + n * 512:R_B + (n + 1) * 512] = bb
        cols_of(U_OUT, i["w_out"][l], DT)
        for j in range(2):
            out[U_PROJ + j] = tiles(i["ple_w_proj"][l][:, j * 512:(j + 1) * 512])
        cols_of(U_PLE, i["ple_w_gate"][l], DT)

        for c, v in ((C_F1, i["ffn1_norm"][l]), (C_MIX, i["mix_norm"][l]), (C_F2, i["ffn2_norm"][l]),
                     (C_PLE, i["ple_norm"][l]), (C_POST, i["ple_post_norm"][l]), (C_BA, b[:D]), (C_BG, b[D:2 * D]),
                     (C_BGC, b[OFF_MERGE:OFF_MERGE + D]), (C_BGN, b[OFF_MERGE + D:]),
                     (C_BCT, b[kv[0].start:kv[1].stop]), (C_CB, i["conv_b"][l]), (C_LG, i["conv_ln_g"][l]),
                     (C_LB, i["conv_ln_b"][l]), (C_B1, i["cmp_b1"][l].reshape(-1))):
            v = cm(v)
            cols[l][:, c:c + v.shape[1]] = v
        for c in range(2):
            cols[l][:, C_POS + 16 * c:C_POS + 16 * (c + 1)] = cm(i["cmp_pos"][l, c].reshape(-1))
        cols[l][:, C_CW:] = i["conv_w"][l].reshape(CONV_K, DT, P).transpose(2, 1, 0).reshape(P, -1)
        g = [i["q_norm"][l]] * 16 + [i["k_norm"][l, 1]] * 4 + [i["k_norm"][l, 2]] * 4
        rows[l, R_G:R_BG] = np.concatenate(g)
        rows[l, R_BG:R_KC] = b[OFF_GATE:OFF_MERGE]
        rows[l, R_KC:] = i["k_norm"][l, 0]
    return stream, cols, rows


LINKS = {'act.layer': 2, 'dve.conv': 18, 'dve.tok': 13, 'dve.att': 16, 'dve.merge': 1, 'dve.layer': 442}


class Chain:

    def __init__(self, eng, sem, name, settle):
        self.eng, self.sem, self.name, self.n, self.terms, self.settle = eng, sem, name, 0, [], settle

    def link(self, ins):
        ins.then_inc(self.sem, 1)
        self.n += 1
        v = self.n
        for reg, per in self.terms:
            v = reg * per + v
        self.eng.wait_ge(self.sem, v)

    def loop(self, key, trips):
        return _Loop(self, self.name + key, trips)


class _Loop:
    def __init__(self, chain, key, trips):
        self.c, self.key, self.trips = chain, key, trips

    def __enter__(self):
        self.c.settle(self.c.eng)
        self.fori = self.c.eng.Fori(0, self.trips)
        reg = self.fori.__enter__()
        self.start = self.c.n
        self.per = LINKS.get(self.key, 0)
        self.c.terms.append((reg, self.per))
        return reg

    def __exit__(self, *exc):
        if exc[0] is None:
            got = self.c.n - self.start
            assert got == self.per, f"LINKS[{self.key!r}] = {got}"
            self.c.terms.pop()
            self.c.n = self.start + self.per * self.trips
        return self.fori.__exit__(*exc)


def build(nc, stream, cols_d, rows_d, const_d, mask_d, x_d, p_d, out_d):
    ctx = ExitStack()
    with ctx:
        base = 16512
        end = [base]

        def region(nbytes):
            at = end[0]
            end[0] += (nbytes + 31) // 32 * 32
            return at

        def sb(name, shape, dt, at):
            n = 4
            for s in shape[1:]:
                n *= s
            return nc.alloc_sbuf_tensor_at(name, shape, dt, offset=at), at + n

        def one(name, shape, dt=F32):
            n = 4
            for s in shape[1:]:
                n *= s
            return sb(name, shape, dt, region(n))[0]

        x = one("x", [P, DT, T])
        raw = one("raw", [P, SLOTS, 1024])
        wh = one("w_hi", [P, SLOTS, 1024], F32R)
        wl = one("w_lo", [P, SLOTS, 1024], F32R)
        con = one("con", [P, NCON])
        ident_r = one("ident_r", [P, P], F32R)
        mask_r = one("mask_r", [P, P], F32R)
        cmask_r = one("cmask_r", [P, TT, P], F32R)
        cols = one("cols", [P, NCOL])
        rstd = one("rstd", [P, T])
        rstd_t = one("rstd_t", [P, TT])
        ssq = one("ssq", [P, T])
        sq = one("sq", [P, 2, T])
        gates = one("gates", [P, TT, 3 * NH])
        small = one("small", [P, 64])
        att = one("att", [P, 64])
        rB, rT, rA = region(32768), region(32768), region(4 * DT * (T + CONV_K - 1) + 16384)
        rD = end[0]
        D_BYTES = 229368 - rD

        xh, a = sb("x_hi", [P, DT, T], F32R, rB)
        xl, _ = sb("x_lo", [P, DT, T], F32R, a)
        kT, _ = sb("kT", [P, 2, 2, NKV, T], F32R, rB)
        tok = sb("tok", [P, 2 * TT * D], F32, rT)[0][:, :]
        tq = tok[:, 0:TT * D].rearrange("p (t n) -> p t n", t=TT)
        tkv = tok[:, TT * D:2 * TT * D].rearrange("p (c t n) -> p c t n", c=2, t=TT)
        xc, a = sb("xc", [P, 2, NKV, XTOK], F32, rT)
        ych, a = sb("yc_hi", [P, 8, P], F32R, a)
        ycl, a = sb("yc_lo", [P, 8, P], F32R, a)
        yf, a = sb("yf", [P, DT, T], F32, rT)
        mt, _ = sb("mt", [P, 4, T], F32, a)
        pe_, a = sb("emb", [P, DT, T], F32, rT)
        pf, a = sb("pf", [P, 2, T], F32, a)
        ph, a = sb("p_hi", [P, 2, T], F32R, a)
        pl, a = sb("p_lo", [P, 2, T], F32R, a)
        acc, ch_at = sb("conv_acc", [P, DT, T], F32, rA)
        ch, _ = sb("conv_in", [P, DT, T + CONV_K - 1], F32, ch_at)
        cvl, _ = sb("cv_lo", [P, DT, T], F32R, rA)
        cvh, o_at = sb("cv_hi", [P, DT, T], F32R, ch_at)
        hh, a = sb("h_hi", [P, 2, 2, T], F32R, rD)
        hl, a = sb("h_lo", [P, 2, 2, T], F32R, a)
        fa, a = sb("fa", [P, 2, T], F32, a)
        fb, a = sb("fb", [P, 2, T], F32, a)
        row, a = sb("rows", [P, NROW], F32, rD)
        sqt, a2 = sb("sqt", [P, TT, 512], F32, a)
        ctb, _ = sb("ctb", [P, 4, T], F32, a)
        hvh, a3 = sb("hv_hi", [P, 2, 512], F32R, a)
        hvl, _ = sb("hv_lo", [P, 2, 512], F32R, a3)
        vcb, a = sb("vcb", [P, NKV, HPG, HD], F32, a2)
        kcT, a = sb("kcT", [P, 2, P], F32R, a)
        free_at = a
        cv, _ = sb("cv", [P, 2, T], F32, a)
        hid, a = sb("hid", [P, 2, P], F32, a)
        hkh, a = sb("hk_hi", [P, 2, P], F32R, a)
        hkl, a = sb("hk_lo", [P, 2, P], F32R, a)
        kc, a = sb("kc", [P, HD], F32, a)
        kcw, a = sb("kcw", [P, HD], F32, a)
        assert a <= 229368, (a - rD, D_BYTES)
        k2, _ = sb("k2", [P, 2, 8, 2, HD], F32, rD)
        kc2, _ = sb("kc2", [P, 1, 2, HD], F32, rD + 16384)
        pr, a = sb("probs", [P, 2, 2, T], F32, rD)
        ptk, a = sb("probsT", [P, 2, 2, TT, P], F32, a)
        q2, a = sb("q2", [P, HPG, 2, HD], F32, a)
        q2T, a = sb("q2T", [P, HPG, P], F32R, a)
        pcs, a = sb("pcs", [P, HPG, NCMP], F32, a)
        pc, a = sb("pc", [P, P], F32, a)
        ptc, a = sb("ptc", [P, P], F32, a)
        ot, _ = sb("ot", [P, 2, HPG, HD], F32, free_at)
        assert a <= rD + NROW * 4 + 8192, "the attention's buffers reach into vcb"
        oh, a = sb("o_hi", [P, DT, T], F32R, o_at)
        ol, a = sb("o_lo", [P, DT, T], F32R, a)
        assert a <= 229368, a - 229368
        masks, _ = sb("masks", [P, NMASK], F32, rD)

        con_ = con[:, :]
        ident = con_[:, K_ID:K_ID + P]
        ones = con_[:, K_ONE:K_ONE + P]

        ps = ctx.enter_context(nc.psum_tensor("ps", [P, 8, 512], F32))

        def sem(name):
            return ctx.enter_context(nc.semaphore(name))

        raw_in = [sem(f"raw_in{s}") for s in range(SLOTS)]
        w_hi, w_split, w_used = sem("s_w_hi"), sem("s_w_split"), sem("s_w_used")
        bank_free = sem("bank_free")
        bar = sem("bar")
        mask_in, settled = sem("mask_in"), sem("settled")
        const_in, x_in, cols_in, rows_in, p_in = (sem(n) for n in ("const_in", "x_in", "cols_in", "rows_in", "p_in"))
        xc_zero, ct_ready, xc_in, vcb_zero = sem("xc_zero"), sem("ct_ready"), sem("xc_in"), sem("vcb_zero")
        con_r = sem("con_r")
        s_xh, s_xl = sem("s_xh"), sem("s_xl")
        s_sq, s_ssq, s_sum, s_rinv, s_rstd = sem("s_sq"), sem("s_ssq"), sem("s_sum"), sem("s_rinv"), sem("s_rstd")
        f_silu, f_h, f_hh, f_hl = sem("f_silu"), sem("f_h"), sem("f_hh"), sem("f_hl")
        y_done, y_free = sem("y_done"), sem("y_free")
        c_sig, c_pad = sem("c_sig"), sem("c_pad")
        g_pre = sem("g_pre")
        g_sig = sem("g_sig")
        yc_h, yc_l = sem("yc_h"), sem("yc_l")
        hid_pre, hid_h, hid_l, kc_ready = sem("hid_pre"), sem("hid_h"), sem("hid_l"), sem("kc_ready")
        t_ev, t_sq, t_rinv, t_rs, t_done = sem("t_ev"), sem("t_sq"), sem("t_rinv"), sem("t_rs"), sem("t_done")
        ln_mu, ln_d, ln_sq, ln_var, ln_rinv, ln_rs = (sem(n) for n in ("ln_mu", "ln_d", "ln_sq", "ln_var", "ln_rinv",
                                                                   "ln_rs"))
        ln_e, ln_f, ln_hi, ln_lo = sem("ln_e"), sem("ln_f"), sem("ln_hi"), sem("ln_lo")
        k_two, k_tr, k_hi, k_lo = sem("k_two"), sem("k_tr"), sem("k_hi"), sem("k_lo")
        q_two, q_tr, q_hi, q_lo = sem("q_two"), sem("q_tr"), sem("q_hi"), sem("q_lo")
        sc_done, sc_sub, pc_exp, ptc_tr, ptc_ev, oc_done = (sem(n) for n in ("sc_done", "sc_sub", "pc_exp", "ptc_tr",
                                                                           "ptc_ev", "oc_done"))
        s_done, s_max, p_exp, pt_tr, pt_ev, pv_done = (sem(n) for n in ("s_done", "s_max", "p_exp", "pt_tr", "pt_ev",
                                                                       "pv_done"))
        oc_read, o_read = sem("oc_read"), sem("o_read")
        ot_tr, ot_h, ot_l = sem("ot_tr"), sem("ot_h"), sem("ot_l")
        m_pre, m_sig = sem("m_pre"), sem("m_sig")
        p_hi_, p_lo_ = sem("s_p_hi"), sem("s_p_lo")
        e_ev = sem("e_ev")
        g_t, g_s = sem("g_t"), sem("g_s")
        dve_seq, act_seq = sem("dve_seq"), sem("act_seq")
        out_done = sem("out_done")

        def unit(L, c, i=None, pi=0):
            v = L * UNITS + c
            return v if i is None else i * pi + v

        def lay(L, per, c, i=None, pi=0):
            v = L * per + c
            return v if i is None else i * pi + v

        def col(c):
            return cols[:, c:c + 1] if isinstance(c, int) else cols[:, bass.ds(c, 1)]

        def at_pos(c, j):
            n = 2 * j // CMP_STRIDE
            return xc[:, c, :, :].rearrange("p h (n s) -> p h n s", s=CMP_STRIDE)[:, :, n:n + NCMP, 2 * j % CMP_STRIDE]

        def copies(m):
            return hid[:, m, :].rearrange("p (g o n) -> p g o n", g=NKV, o=1).broadcast_to([P, NKV, HPG, NCMP])

        def twice(ap, h):
            return ap.rearrange("p (h o d) -> p h o d", h=h, o=1).broadcast_to([P, h, 2, HD])

        def flat(ap):
            return ap.rearrange("p a d -> p (a d)")

        def heads(q, g):
            return tok[:, bass.ds(g * 256 + q * D, 256)]

        def steps(step, loop):
            for q in range(TT):
                with loop(NKV - 1) as g:
                    step(q, g, q, g + 1)
                step(q, NKV - 1, q + 1, 0)

        def settle(eng):
            eng.sem_inc(settled, 1)

        def barrier(eng, L, k):
            settle(eng)
            eng.drain().then_inc(bar, 1)
            eng.wait_ge(bar, lay(L, 3 * BARRIERS, 3 * (k + 1)))
            settle(eng)

        block = ctx.enter_context(nc.Block())

        @block.sync
        def _(sp):
            for u in range(SLOTS):
                sp.dma_start(raw[:, u, :], stream[u]).then_inc(raw_in[u], 16)
            with sp.Fori(0, DEPTH * UNITS // SLOTS) as i:
                for s in range(SLOTS):
                    sp.wait_ge(w_split, i * SLOTS + s + 1)
                    sp.dma_start(raw[:, s, :], stream[i * SLOTS + s + SLOTS]).then_inc(raw_in[s], 16)
            for s in range(SLOTS):
                sp.wait_ge(raw_in[s], 16 * (DEPTH * UNITS // SLOTS + 1))
            sp.wait_ge(bar, 3 * BARRIERS * DEPTH)
            sp.dma_start(out_d, x[:, :, :]).then_inc(out_done, 16)
            sp.wait_ge(out_done, 16)

        @block.gpsimd
        def _(pool):
            pool.dma_start(con[:, :], const_d).then_inc(const_in, 16)
            pool.dma_start(masks[:, :], mask_d).then_inc(mask_in, 16)
            pool.dma_start(x[:, :, :], x_d).then_inc(x_in, 16)
            pool.dma_start(cols[:, :], cols_d[0]).then_inc(cols_in, 16)
            with pool.Fori(0, DEPTH) as L:
                pool.wait_ge(bar, lay(L, 3 * BARRIERS, 3))
                settle(pool)
                pool.dma_start(row[:, :], rows_d[L].partition_broadcast(P)).then_inc(rows_in, 16)
                pool.memset(xc[:, :, :, :], 0.0).then_inc(xc_zero, 1)
                pool.memset(vcb[:, :, :, :], 0.0).then_inc(vcb_zero, 1)
                pool.wait_ge(xc_zero, lay(L, 1, 1))
                settle(pool)
                for c in range(4):
                    pool.wait_ge(ct_ready, lay(L, 4, c + 1))
                    settle(pool)
                    for half in range(2):
                        h = 2 * (c % 2) + half
                        src = ctb[64 * half:64 * half + 64, c, :]
                        pool.dma_start(xc[0:64, c // 2, h, 0:T], src).then_inc(xc_in, 16)
                        pool.dma_start(xc[64:128, c // 2, h, 0:T - 1], src[:, 1:T]).then_inc(xc_in, 16)
                pool.wait_ge(bar, lay(L, 3 * BARRIERS, 3 * 4))
                settle(pool)
                pool.dma_start(pf[:, :, :], p_d[L]).then_inc(p_in, 16)
                pool.wait_ge(bar, lay(L, 3 * BARRIERS, 3 * BARRIERS))
                settle(pool)
                pool.dma_start(cols[:, :], cols_d[L + 1]).then_inc(cols_in, 16)
            pool.wait_ge(cols_in, 16 * (DEPTH + 1))

        @block.tensor
        def _(pe):
            mm = nc.tensor.matmul

            def mm3(out, ah, al, bh, bl, start, stop, **kw):
                mm(out, ah, bh, start=start, stop=False, **kw)
                mm(out, ah, bl, start=False, stop=False, **kw)
                return mm(out, al, bh, start=False, stop=stop, **kw)

            def bank(b):
                return ps[:, b % SLOTS, :]

            def product(L, c, b, rh, rl, i=None, pi=0, bi=0, first=None, ready=None):
                s = c % SLOTS
                pe.wait_ge(w_split, unit(L, c + 1, i, pi))
                pe.wait_ge(bank_free, lay(L, BANKS, b + 1, i, bi))
                for k in range(DT):
                    if first is not None:
                        pe.wait_ge(s_xl, lay(L, 8 * 6, first + k + 1))
                    if ready is not None:
                        pe.wait_ge(ready, lay(L, DT, k + 1))
                    last = mm3(bank(b), wh[:, s, k * P:(k + 1) * P], wl[:, s, k * P:(k + 1) * P],
                               rh[:, k, :], rl[:, k, :], k == 0, k == DT - 1)
                last.then_inc(w_used, 1)

            def stat_sum(L, s):
                pe.wait_ge(s_ssq, lay(L, 8 * 5, 8 * s + 8))
                mm(ps[:, 4, :], ones, ssq[:, :], start=True, stop=True).then_inc(s_sum, 1)

            def ffn(L, u0, b0, which, split, stat):
                def ab(c, b, i=None, first=None):
                    for j in range(4):
                        product(L, c + j, b + j, xh, xl, i, 12, 8, first if j == 0 else None)
                        if j == 0 and first is not None:
                            stat_sum(L, stat)

                def y(c, s, par, i=None):
                    pe.wait_ge(w_split, unit(L, c + 2, i, 12))
                    pe.wait_ge(f_hl, lay(L, 2 * FT, which * FT + 2 * s + 2, i, 4))
                    for m in range(DT):
                        pe.wait_ge(y_free, lay(L, 16 * FSTEPS, (which * FSTEPS + s) * 8 + m + 1, i, 16))
                        for j in range(2):
                            sl = (c + j) % SLOTS
                            last = mm3(ps[:, 4 + m % 4, :], wh[:, sl, m * P:(m + 1) * P], wl[:, sl, m * P:(m + 1) * P],
                                       hh[:, par, j, :], hl[:, par, j, :], j == 0, j == 1)
                            if m == DT - 1:
                                last.then_inc(w_used, 1)
                        if m < DT - 1:
                            last.then_inc(y_done, 1)

                ab(u0, b0, first=split)
                with pe.Fori(0, (FSTEPS - 1) // 2) as i:
                    for h in range(2):
                        ab(u0 + 4 + 6 * h, b0 + 4 + 4 * h, i)
                        y(u0 + 8 + 6 * h, h, h, i)
                y(u0 + 4 + 6 * (FSTEPS - 1), FSTEPS - 1, 0)

            with pe.Fori(0, DEPTH) as L:
                pe.wait_ge(const_in, 16)
                ffn(L, U_FFN1, B_FFN1, 0, 0, 0)
                barrier(pe, L, 0)

                product(L, U_CONV, B_CONV, xh, xl, first=8)
                stat_sum(L, 1)
                for t in range(TT):
                    last = mm(ps[:, 5, t:t + 1], ssq[:, t * P:(t + 1) * P], ones[:, 0:1], start=True, stop=True)
                last.then_inc(s_sum, 1)
                for j in range(1, 4):
                    product(L, U_CONV + j, B_CONV + j, xh, xl)
                with pe.Fori(0, 3) as i:
                    for j in range(4):
                        product(L, U_CONV + 4 + j, B_CONV + 4 + j, xh, xl, i, 4, 4)
                for j in range(4):
                    product(L, U_CT + j, B_CT + j, xh, xl)
                s = U_GATE % SLOTS
                pe.wait_ge(w_split, unit(L, U_GATE + 1))
                pe.wait_ge(bank_free, lay(L, BANKS, B_GATE + 1))
                for t in range(TT):
                    for k in range(DT):
                        tk = slice(t * P, (t + 1) * P)
                        last = mm3(bank(B_GATE)[:, t * 48:(t + 1) * 48], xh[:, k, tk], xl[:, k, tk],
                                   wh[:, s, k * 48:(k + 1) * 48], wl[:, s, k * 48:(k + 1) * 48],
                                   t == 0 and k == 0, t == TT - 1 and k == DT - 1, skip_group_check=True)
                last.then_inc(w_used, 1)
                for c in range(2):
                    for j in range(4):
                        u = U_CMP + 4 * c + j
                        pe.wait_ge(w_split, unit(L, u + 1))
                        pe.wait_ge(yc_l, lay(L, 32, 16 * c + 4 * j + 4))
                        for m in range(2):
                            if j == 0:
                                pe.wait_ge(bank_free, lay(L, BANKS, B_CMP + 2 * c + m + 1))
                            for kk in range(4):
                                w = slice(kk * 256 + m * P, kk * 256 + (m + 1) * P)
                                r = (4 * j + kk) % 8
                                last = mm3(bank(B_CMP + 2 * c + m)[:, 0:P], wh[:, u % SLOTS, w], wl[:, u % SLOTS, w],
                                           ych[:, r, :], ycl[:, r, :], j == 0 and kk == 0, j == 3 and kk == 3)
                        last.then_inc(w_used, 1)
                s = U_W2 % SLOTS
                pe.wait_ge(w_split, unit(L, U_W2 + 1))
                pe.wait_ge(hid_l, lay(L, 2, 2))
                pe.wait_ge(bank_free, lay(L, BANKS, B_W2 + 2))
                for m in range(2):
                    w = slice(m * HD, (m + 1) * HD)
                    last = mm3(bank(B_W2)[:, 0:HD], hkh[:, m, :], hkl[:, m, :], wh[:, s, w], wl[:, s, w], m == 0, m == 1)
                last.then_inc(kc_ready, 1)
                for g in range(NKV):
                    for m in range(2):
                        w, r = slice(P + m * HD, P + (m + 1) * HD), slice(g * P, (g + 1) * P)
                        last = mm3(bank(B_W2 + 1)[:, g * HD:(g + 1) * HD], hvh[:, m, r], hvl[:, m, r], wh[:, s, w],
                                   wl[:, s, w], g == 0 and m == 0, g == 3 and m == 1, skip_group_check=True)
                last.then_inc(w_used, 1)

                def tok_block(i=None, c=0, b=0):
                    for j in range(4):
                        s = (U_TOK + j) % SLOTS
                        pe.wait_ge(w_split, unit(L, U_TOK + c + j + 1, i, 4))
                        for t in range(TT):
                            if j == 0:
                                pe.wait_ge(bank_free, lay(L, BANKS, B_TOK + b + t + 1, i, 4))
                            tk = slice(t * P, (t + 1) * P)
                            for kk in range(2):
                                w = slice(kk * 512, (kk + 1) * 512)
                                last = mm3(bank(B_TOK + t), xh[:, 2 * j + kk, tk], xl[:, 2 * j + kk, tk], wh[:, s, w],
                                           wl[:, s, w], j == 0 and kk == 0, j == 3 and kk == 1)
                        last.then_inc(w_used, 1)

                with pe.Fori(0, 2) as i:
                    tok_block(i)
                tok_block(None, 8, 8)
                tok_block(None, 12, 12)
                barrier(pe, L, 1)

                pe.wait_ge(k_two, lay(L, 5, 1))
                nc.tensor.transpose(ps[:, 6, 0:P], flat(kc2[:, 0, :, :]), ident).then_inc(k_tr, 1)
                for t in range(TT):
                    pe.wait_ge(k_two, lay(L, 5, t + 2))
                    for kind in range(2):
                        n = 2 * t + kind
                        if n >= 4:
                            pe.wait_ge(k_lo, lay(L, 9, n - 2))
                        for g in range(NKV):
                            last = nc.tensor.transpose(ps[:, n % 4, g * P:(g + 1) * P],
                                                       flat(k2[:, t % 2, kind * NKV + g, :, :]), ident)
                        last.then_inc(k_tr, 1)

                def steps_done(q, g, c):
                    return lay(L, 16, 4 * q + c, g, 1)

                def heads_done(q, g, c):
                    return lay(L, 64, 16 * q + c, g, 4)

                def turn_q(q, g):
                    pe.wait_ge(q_two, steps_done(q, g, 1))
                    for j in range(HPG):
                        last = nc.tensor.transpose(ps[:, 7, j * P:(j + 1) * P], flat(q2[:, j, :, :]), ident)
                    last.then_inc(q_tr, 1)

                def compressed(q, g):
                    pe.wait_ge(q_lo, steps_done(q, g, 1))
                    mm(ps[:, 7, 0:P], ident_r[:, :], cmask_r[:, q, :], start=True, stop=False, skip_group_check=True)
                    for j in range(HPG):
                        for c in range(2):
                            last = mm(ps[:, 7, j * NCMP:(j + 1) * NCMP], q2T[:, j, :],
                                      kcT[:, c, bass.ds(g * NCMP, NCMP)], start=False,
                                      stop=j == 3 and c == 1, skip_group_check=True)
                    last.then_inc(sc_done, 1)

                def scores(q, g, j, first=False):
                    W = (q + 1) * P
                    if not first:
                        pe.wait_ge(p_exp, heads_done(q, g, j - 1))
                    for kind in range(2):
                        o = ps[:, 2 * (j % 2) + kind, 0:W]
                        mm(o, q2T[:, j, :], kT[:, kind, 0, g, 0:W], start=True, stop=False)
                        mm(o, q2T[:, j, :], kT[:, kind, 1, g, 0:W], start=False, stop=False)
                        last = mm(o[:, W - P:W], ident_r[:, :], mask_r[:, :], start=False, stop=True)
                    last.then_inc(s_done, 1)

                def turn(q, g, j, first=False):
                    pe.wait_ge(p_exp, heads_done(q, g, j + 1))
                    if not first:
                        pe.wait_ge(pt_ev, heads_done(q, g, j))
                    for kind in range(2):
                        for k in range(q + 1):
                            last = nc.tensor.transpose(ps[:, 4 + kind, k * P:(k + 1) * P],
                                                       pr[:, j % 2, kind, k * P:(k + 1) * P], ident)
                    last.then_inc(pt_tr, 1)

                def values(q, g, j):
                    pe.wait_ge(pt_ev, heads_done(q, g, j + 1))
                    for kind in range(2):
                        for k in range(q + 1):
                            v = tkv[:, 1, k, bass.ds(g * HD + kind * KVW, HD)]
                            last = mm(ps[:, 6, (kind * 4 + j) * HD:(kind * 4 + j + 1) * HD],
                                      ptk[:, j % 2, kind, k, :], v, start=k == 0, stop=k == q)
                    last.then_inc(pv_done, 1)

                def step(q, g, Q, G):
                    more = Q < TT
                    scores(q, g, 2)
                    pe.wait_ge(pc_exp, steps_done(q, g, 1))
                    nc.tensor.transpose(ps[:, 7, P:2 * P], pc[:, :], ident).then_inc(ptc_tr, 1)
                    turn(q, g, 1)
                    pe.wait_ge(ptc_ev, steps_done(q, g, 1))
                    mm(ps[:, 7, 2 * P:4 * P], ptc[:, :],
                       vcb[:, g, :, :].rearrange("p j d -> p (j d)"), start=True, stop=True).then_inc(oc_done, 1)
                    pe.wait_ge(o_read, lay(L, 17, 4 * q + 1, g, 1))
                    values(q, g, 0)
                    scores(q, g, 3)
                    if more:
                        pe.wait_ge(oc_read, steps_done(q, g, 1))
                        turn_q(Q, G)
                    turn(q, g, 2)
                    values(q, g, 1)
                    if more:
                        compressed(Q, G)
                        scores(Q, G, 0)
                    turn(q, g, 3)
                    values(q, g, 2)
                    if more:
                        scores(Q, G, 1)
                        turn(Q, G, 0)
                    values(q, g, 3)

                turn_q(0, 0)
                pe.wait_ge(k_lo, lay(L, 9, 9))
                compressed(0, 0)
                scores(0, 0, 0, True)
                scores(0, 0, 1, True)
                turn(0, 0, 0, True)
                settle(pe)
                steps(step, lambda n: pe.Fori(0, n))
                barrier(pe, L, 2)

                for m in range(DT):
                    last = mm(ps[:, 4, :], ones, acc[:, m, :], start=m == 0, stop=m == DT - 1)
                last.then_inc(ln_mu, 1)
                product(L, U_MERGE, B_MERGE, xh, xl, first=16)
                for m in range(DT):
                    if m >= 2:
                        pe.wait_ge(ot_l, lay(L, 8, m - 1))
                    for t in range(TT):
                        last = nc.tensor.transpose(ps[:, 6 + m % 2, t * P:(t + 1) * P], tq[:, t, m * P:(m + 1) * P],
                                                   ident)
                    last.then_inc(ot_tr, 1)
                    pe.wait_ge(ln_sq, lay(L, 8, m + 1))
                    mm(ps[:, 5, :], ones, sq[:, m % 2, :], start=m == 0, stop=m == DT - 1).then_inc(ln_var, 1)
                product(L, U_MERGE + 1, B_MERGE + 1, xh, xl)
                product(L, U_MERGE + 2, B_MERGE + 2, oh, ol, ready=ot_l)
                product(L, U_MERGE + 3, B_MERGE + 3, cvh, cvl, ready=ln_lo)
                with pe.Fori(0, DT - 1) as i:
                    for j, (rh, rl) in enumerate(((xh, xl), (xh, xl), (oh, ol), (cvh, cvl))):
                        product(L, U_MERGE + 4 + j, B_MERGE + 4 + j, rh, rl, i, 4, 4)
                barrier(pe, L, 3)
                product(L, U_OUT, B_OUT, xh, xl, first=24)
                for j in range(1, 4):
                    product(L, U_OUT + j, B_OUT + j, xh, xl)
                for j in range(4):
                    product(L, U_OUT + 4 + j, B_OUT + 4 + j, xh, xl)
                barrier(pe, L, 4)
                ffn(L, U_FFN2, B_FFN2, 1, 32, 2)
                barrier(pe, L, 5)

                def proj(j):
                    u = U_PROJ + j
                    pe.wait_ge(w_split, unit(L, u + 1))
                    for m in range(4):
                        b = B_PROJ + 4 * j + m
                        pe.wait_ge(bank_free, lay(L, BANKS, b + 1))
                        for k in range(2):
                            if j == 0 and m == 0:
                                pe.wait_ge(p_lo_, lay(L, 2, k + 1))
                            w = slice(k * 512 + m * P, k * 512 + (m + 1) * P)
                            last = mm3(bank(b), wh[:, u % SLOTS, w], wl[:, u % SLOTS, w], ph[:, k, :], pl[:, k, :],
                                       k == 0, k == 1)
                    last.then_inc(w_used, 1)

                proj(0)
                stat_sum(L, 3)
                proj(1)
                product(L, U_PLE, B_PLE, xh, xl, first=40)
                stat_sum(L, 4)
                for j in range(1, 4):
                    product(L, U_PLE + j, B_PLE + j, xh, xl)
                for j in range(4):
                    product(L, U_PLE + 4 + j, B_PLE + 4 + j, xh, xl)
                barrier(pe, L, 6)

        @block.scalar
        def _(act):
            seq = Chain(act, act_seq, "act.", settle)
            f = nc.scalar.activation

            def hi(L, c, i=None, pi=0):
                s = c % SLOTS
                act.wait_ge(w_used, unit(L, c + 1, i, pi))
                n = lay(L, UNITS // SLOTS, c // SLOTS + 2, i, pi // SLOTS)
                act.wait_ge(raw_in[s], n * 16)
                f(wh[:, s, :], raw[:, s, :], ACT.Copy).then_inc(w_hi, 1)

            def evacuated(L, b, i=None, bi=0):
                act.wait_ge(bank_free, lay(L, BANKS, b + 5, i, bi))

            def norm(L, ev, gain, stat):
                for k in range(DT):
                    f(xh[:, k, :], x[:, k, :], ACT.Copy, scale=col(gain + k)).then_inc(s_xh, 1)
                    if stat is not None:
                        if k >= 2:
                            act.wait_ge(s_ssq, lay(L, 40, 8 * stat + k - 1))
                        f(sq[:, k % 2, :], x[:, k, :], ACT.Square).then_inc(s_sq, 1)

            def root(L, si, t):
                act.wait_ge(s_rinv, lay(L, 6, si + 1))
                f(t, t, ACT.Sqrt).then_inc(s_rstd, 1)

            def ffn(L, u0, b0, which, ev, gain, stat, si):
                def ab(c, b, s, par, i=None):
                    for j in range(2):
                        hi(L, c + 2 * j, i, 12)
                        evacuated(L, b + 2 * j, i, 8)
                        f(fa[:, j, :], fa[:, j, :], ACT.Silu).then_inc(f_silu, 1)
                        hi(L, c + 2 * j + 1, i, 12)
                        act.wait_ge(f_h, lay(L, 2 * FT, which * FT + 2 * s + j + 1, i, 4))
                        f(hh[:, par, j, :], fb[:, j, :], ACT.Copy).then_inc(f_hh, 1)

                norm(L, ev, gain, stat)
                root(L, si, rstd[:, :])
                ab(u0, b0, 0, 0)
                with seq.loop("ffn", (FSTEPS - 1) // 2) as i:
                    for h in range(2):
                        ab(u0 + 4 + 6 * h, b0 + 4 + 4 * h, 1 + h, 1 - h, i)
                        hi(L, u0 + 8 + 6 * h, i, 12)
                        hi(L, u0 + 9 + 6 * h, i, 12)
                hi(L, u0 + 4 + 6 * (FSTEPS - 1))
                hi(L, u0 + 5 + 6 * (FSTEPS - 1))

            act.wait_ge(const_in, 16)
            f(ident_r[:, :], ident, ACT.Copy)
            act.wait_ge(mask_in, 16)
            f(mask_r[:, :], masks[:, K_MASK:K_MASK + P], ACT.Copy)
            f(cmask_r[:, :, :], masks[:, K_CM:K_CM + TT * P].rearrange("p (t k) -> p t k", t=TT),
              ACT.Copy).then_inc(con_r, 1)
            act.wait_ge(x_in, 16)
            for u in range(SLOTS):
                act.wait_ge(raw_in[u], 16)
                f(wh[:, u, :], raw[:, u, :], ACT.Copy).then_inc(w_hi, 1)

            with seq.loop("layer", DEPTH) as L:
                act.wait_ge(cols_in, lay(L, 16, 16))
                ffn(L, U_FFN1, B_FFN1, 0, 0, C_F1, 0, 0)
                barrier(act, L, 0)

                norm(L, 1, C_MIX, 1)
                root(L, 1, rstd[:, :])
                root(L, 2, rstd_t[:, :])

                def pair(m, c, b, i=None):
                    hi(L, c, i, 4)
                    hi(L, c + 1, i, 4)
                    evacuated(L, b + 1, i, 4)
                    f(cv[:, 1, :], cv[:, 1, :], ACT.Sigmoid, bias=col(m + C_BG)).then_inc(c_sig, 1)

                for j in range(2):
                    pair(j, U_CONV + 2 * j, B_CONV + 2 * j)
                with seq.loop("conv", 3) as i:
                    for j in range(2):
                        pair(i * 2 + (2 + j), U_CONV + 4 + 2 * j, B_CONV + 4 + 2 * j, i)
                for j in range(4):
                    hi(L, U_CT + j)
                    evacuated(L, B_CT + j)
                    f(ctb[:, j, :], ctb[:, j, :], ACT.Identity, bias=col(C_BCT + j)).then_inc(ct_ready, 1)
                hi(L, U_GATE)
                evacuated(L, B_GATE + 1)
                f(gates[:, :, :], gates[:, :, :], ACT.Sigmoid).then_inc(g_sig, 1)

                def block_in(jj):
                    c, j = jj // 16, jj % 16
                    if jj >= 8:
                        act.wait_ge(w_used, unit(L, U_CMP + (jj - 8) // 4 + 1))
                    f(ych[:, jj % 8, :].rearrange("p (h n) -> p h n", h=NKV), at_pos(c, j), ACT.Identity,
                      bias=col(C_POS + jj)).then_inc(yc_h, 1)

                act.wait_ge(xc_in, lay(L, 256, 256))
                for jj in range(8):
                    block_in(jj)
                for u in range(8):
                    hi(L, U_CMP + u)
                    if u % 4 == 3:
                        c = u // 4
                        evacuated(L, B_CMP + 2 * c + 1)
                        for m in range(2):
                            ins = f(hid[:, m, :], hid[:, m, :], ACT.Gelu_apprx_tanh, bias=col(C_B1 + 2 * c + m))
                        seq.link(ins)
                        if c == 0:
                            f(hkh[:, :, :], hid[:, :, :], ACT.Copy).then_inc(hid_h, 1)
                        else:
                            for m in range(2):
                                ins = f(hvh[:, m, :].rearrange("p (g j n) -> p g j n", g=NKV, j=HPG), copies(m), ACT.Copy)
                            ins.then_inc(hid_h, 1)
                    if u < 6:
                        for jj in range(8 + 4 * u, 12 + 4 * u):
                            block_in(jj)
                hi(L, U_W2)
                act.wait_ge(t_rinv, lay(L, 4, 1))
                f(small[:, 32:33], small[:, 32:33], ACT.Sqrt).then_inc(t_rs, 1)

                def tok_turns(i=None, c=0, b=0):
                    for j in range(4):
                        hi(L, U_TOK + c + j, i, 4)

                def head_norm(xt, n, i=None):
                    evacuated(L, B_TOK + 4 * n + 3, i, 4)
                    f(sqt[:, :, :], xt, ACT.Square).then_inc(t_sq, 1)
                    act.wait_ge(t_rinv, lay(L, 4, n + 2, i, 1))
                    f(small[:, 0:32], small[:, 0:32], ACT.Sqrt).then_inc(t_rs, 1)

                with seq.loop("tok", 2) as i:
                    tok_turns(i)
                    head_norm(tq[:, :, bass.ds(i * 512, 512)], 0, i)
                tok_turns(None, 8)
                head_norm(tkv[:, 0, :, :], 2)
                tok_turns(None, 12)
                barrier(act, L, 1)

                def two_keys(t):
                    f(k2[:, t % 2, :, :, :], twice(tkv[:, 0, t, :], 8), ACT.Copy).then_inc(k_two, 1)

                def two_q(q, g):
                    f(q2[:, :, :, :], twice(heads(q, g), HPG), ACT.Copy).then_inc(q_two, 1)

                f(kc2[:, :, :, :], twice(kc[:, :], 1), ACT.Copy).then_inc(k_two, 1)
                two_keys(0)
                two_keys(1)
                act.wait_ge(k_tr, lay(L, 9, 1))
                f(kcT[:, 0, :], ps[:, 6, 0:P], ACT.Copy).then_inc(k_hi, 1)
                for n in range(2 * TT):
                    if n in (2, 4):
                        act.wait_ge(k_tr, lay(L, 9, n + 1))
                        two_keys(n // 2 + 1)
                    act.wait_ge(k_tr, lay(L, 9, n + 2))
                    f(kT[:, n % 2, 0, :, n // 2 * P:(n // 2 + 1) * P],
                      ps[:, n % 4, :].rearrange("p (g k) -> p g k", g=NKV), ACT.Copy).then_inc(k_hi, 1)

                def round_q(q, g):
                    act.wait_ge(q_tr, lay(L, 16, 4 * q + 1, g, 1))
                    f(q2T[:, :, :], ps[:, 7, :].rearrange("p (j k) -> p j k", j=HPG), ACT.Copy).then_inc(q_hi, 1)

                def exp_c(q, g):
                    act.wait_ge(sc_sub, lay(L, 16, 4 * q + 1, g, 1))
                    f(pc[:, :], pcs[:, :, :].rearrange("p j n -> p (j n)"), ACT.Exp, scale=SCALE).then_inc(pc_exp, 1)

                def exps(q, g, j):
                    W = (q + 1) * P
                    act.wait_ge(s_max, lay(L, 64, 16 * q + j + 1, g, 4))
                    for kind in range(2):
                        n = 28 + 4 * kind + j
                        ins = f(pr[:, j % 2, kind, 0:W], ps[:, 2 * (j % 2) + kind, 0:W], ACT.Exp, scale=SCALE,
                                bias=att[:, 16 + 2 * (j % 2) + kind:17 + 2 * (j % 2) + kind],
                                accum_out=att[:, n:n + 1])
                    ins.then_inc(p_exp, 1)

                def turned(q, g, j):
                    act.wait_ge(pt_tr, lay(L, 64, 16 * q + j + 1, g, 4))
                    for kind in range(2):
                        ins = f(ptk[:, j % 2, kind, 0:q + 1, :],
                                ps[:, 4 + kind, 0:(q + 1) * P].rearrange("p (t k) -> p t k", k=P), ACT.Copy)
                    ins.then_inc(pt_ev, 1)

                def step(q, g, Q, G):
                    more = Q < TT
                    if more:
                        two_q(Q, G)
                    exps(q, g, 2)
                    turned(q, g, 1)
                    if more:
                        round_q(Q, G)
                    exps(q, g, 3)
                    turned(q, g, 2)
                    if more:
                        exp_c(Q, G)
                        exps(Q, G, 0)
                    turned(q, g, 3)
                    if more:
                        exps(Q, G, 1)
                        turned(Q, G, 0)

                act.wait_ge(k_tr, lay(L, 9, 9))
                two_q(0, 0)
                round_q(0, 0)
                exp_c(0, 0)
                exps(0, 0, 0)
                exps(0, 0, 1)
                turned(0, 0, 0)
                steps(step, lambda n: seq.loop("att", n))
                barrier(act, L, 2)

                norm(L, 2, C_MIX, None)
                for m in range(DT):
                    act.wait_ge(ln_d, lay(L, 8, m + 1))
                    if m >= 2:
                        act.wait_ge(ln_var, lay(L, 8, m - 1))
                    f(sq[:, m % 2, :], acc[:, m, :], ACT.Square).then_inc(ln_sq, 1)
                    act.wait_ge(ot_tr, lay(L, 8, m + 1))
                    f(oh[:, m, :], ps[:, 6 + m % 2, :], ACT.Copy).then_inc(ot_h, 1)
                hi(L, U_MERGE)
                act.wait_ge(ln_rinv, lay(L, 1, 1))
                f(ssq[:, :], ssq[:, :], ACT.Sqrt).then_inc(ln_rs, 1)
                for m in range(DT):
                    act.wait_ge(ln_e, lay(L, 8, m + 1))
                    f(acc[:, m, :], acc[:, m, :], ACT.Silu, bias=col(C_LB + m), scale=col(C_LG + m)).then_inc(ln_f, 1)
                    if m:
                        act.wait_ge(ln_f, lay(L, 8, m))
                        f(cvh[:, m - 1, :], acc[:, m - 1, :], ACT.Copy).then_inc(ln_hi, 1)
                act.wait_ge(ln_f, lay(L, 8, 8))
                f(cvh[:, DT - 1, :], acc[:, DT - 1, :], ACT.Copy).then_inc(ln_hi, 1)

                def merge(m, c, i=None):
                    for j in range(4):
                        if c + j:
                            hi(L, U_MERGE + c + j, i, 4)
                        if j < 2:
                            evacuated(L, B_MERGE + c + j, i, 4)
                            f(mt[:, j, :], mt[:, j, :], ACT.Sigmoid, bias=col(m + (C_BGN if j else C_BGC)))\
                                .then_inc(m_sig, 1)

                merge(0, 0)
                with seq.loop("merge", DT - 1) as i:
                    merge(i + 1, 4, i)
                barrier(act, L, 3)
                for k in range(DT):
                    f(xh[:, k, :], yf[:, k, :], ACT.Copy).then_inc(s_xh, 1)
                for j in range(DT):
                    hi(L, U_OUT + j)
                barrier(act, L, 4)
                ffn(L, U_FFN2, B_FFN2, 1, 4, C_F2, 2, 3)
                barrier(act, L, 5)

                act.wait_ge(p_in, lay(L, 16, 16))
                for k in range(2):
                    f(ph[:, k, :], pf[:, k, :], ACT.Copy).then_inc(p_hi_, 1)
                norm(L, 5, C_PLE, 3)
                root(L, 4, rstd[:, :])
                for j in range(2):
                    hi(L, U_PROJ + j)
                for m in range(DT):
                    evacuated(L, B_PROJ + m)
                    if m >= 2:
                        act.wait_ge(s_ssq, lay(L, 40, 32 + m - 1))
                    f(sq[:, m % 2, :], pe_[:, m, :], ACT.Square).then_inc(s_sq, 1)
                for m in range(DT):
                    hi(L, U_PLE + m)
                    if m == 0:
                        root(L, 5, ssq[:, :])
                    evacuated(L, B_PLE + m)
                    f(fb[:, m % 2, :], fa[:, m % 2, :], ACT.Sigmoid).then_inc(g_s, 1)
                barrier(act, L, 6)

        @block.vector
        def _(dve):
            seq = Chain(dve, dve_seq, "dve.", settle)
            link = seq.link
            v = nc.vector
            tt, ts, stt = v.tensor_tensor, v.tensor_scalar, v.scalar_tensor_tensor
            MUL, ADD, SUB = ALU.mult, ALU.add, ALU.subtract

            def f32(ap):
                return ap.bitcast(F32)

            def lo(L, c, i=None, pi=0):
                s = c % SLOTS
                dve.wait_ge(w_hi, unit(L, c + 5, i, pi))
                tt(wl[:, s, :], raw[:, s, :], f32(wh[:, s, :]), SUB).then_inc(w_split, 1)

            def used(L, c, i=None, pi=0):
                dve.wait_ge(w_used, unit(L, c + 1, i, pi))

            def evacuated(L, b, i=None, bi=0):
                dve.wait_ge(bank_free, lay(L, BANKS, b + 5, i, bi))

            def scaled(dst, L, c, b, i=None, pi=0, bi=0):
                used(L, c, i, pi)
                tt(dst, ps[:, b % SLOTS, :], rstd[:, :], MUL).then_inc(bank_free, 1)

            def norm(L, ev, gain, stat):
                for k in range(DT):
                    dve.wait_ge(s_xh, lay(L, 48, 8 * ev + k + 1))
                    stt(xl[:, k, :], x[:, k, :], col(gain + k), f32(xh[:, k, :]), MUL, SUB).then_inc(s_xl, 1)
                    if stat is not None:
                        add_square(L, stat, k)

            def add_square(L, stat, k):
                dve.wait_ge(s_sq, lay(L, 40, 8 * stat + k + 1))
                if k == 0:
                    v.tensor_copy(ssq[:, :], sq[:, 0, :]).then_inc(s_ssq, 1)
                else:
                    dve.wait_ge(s_ssq, lay(L, 40, 8 * stat + k))
                    tt(ssq[:, :], ssq[:, :], sq[:, k % 2, :], ADD).then_inc(s_ssq, 1)

            def mean(L, si, dst, src):
                dve.wait_ge(s_sum, lay(L, 6, si + 1))
                link(ts(dst, src, 1.0 / D, EPS, MUL, ADD))
                v.reciprocal(dst, dst).then_inc(s_rinv, 1)

            def rooted(L, si):
                dve.wait_ge(s_rstd, lay(L, 6, si + 1))

            def ffn(L, u0, b0, which, ev, gain, stat, si):
                def ab(c, b, s, par, i=None):
                    for j in range(2):
                        scaled(fa[:, j, :], L, c + 2 * j, b + 2 * j, i, 12, 8)
                        lo(L, c + 2 * j, i, 12)
                        scaled(fb[:, j, :], L, c + 2 * j + 1, b + 2 * j + 1, i, 12, 8)
                        n = which * FT + 2 * s + j + 1
                        dve.wait_ge(f_silu, lay(L, 2 * FT, n, i, 4))
                        evacuated(L, b + 2 * j + 1, i, 8)
                        tt(fb[:, j, :], fb[:, j, :], fa[:, j, :], MUL).then_inc(f_h, 1)
                        lo(L, c + 2 * j + 1, i, 12)
                        dve.wait_ge(f_hh, lay(L, 2 * FT, n, i, 4))
                        tt(hl[:, par, j, :], fb[:, j, :], f32(hh[:, par, j, :]), SUB).then_inc(f_hl, 1)

                def y(c, s, i=None):
                    n = which * FSTEPS + s
                    dve.wait_ge(y_free, lay(L, 16 * FSTEPS, 8 * n + 4, i, 16))
                    for m in range(DT):
                        if m < DT - 1:
                            dve.wait_ge(y_done, lay(L, 14 * FSTEPS, 7 * n + m + 1, i, 14))
                        else:
                            used(L, c + 1, i, 12)
                        stt(x[:, m, :], ps[:, 4 + m % 4, :], 0.5, x[:, m, :], MUL, ADD).then_inc(y_free, 1)
                    lo(L, c, i, 12)
                    lo(L, c + 1, i, 12)

                norm(L, ev, gain, stat)
                mean(L, si, rstd[:, :], ps[:, 4, :])
                rooted(L, si)
                ab(u0, b0, 0, 0)
                with seq.loop("ffn", (FSTEPS - 1) // 2) as i:
                    for h in range(2):
                        ab(u0 + 4 + 6 * h, b0 + 4 + 4 * h, 1 + h, 1 - h, i)
                        y(u0 + 8 + 6 * h, h, i)
                y(u0 + 4 + 6 * (FSTEPS - 1), FSTEPS - 1)

            v.memset(att[:, 0:1], 0.0).then_inc(bank_free, SLOTS)
            v.memset(att[:, 1:2], 0.0).then_inc(y_free, 4)
            dve.wait_ge(x_in, 16)
            dve.wait_ge(const_in, 16)
            for u in range(SLOTS):
                dve.wait_ge(w_hi, u + 1)
                tt(wl[:, u, :], raw[:, u, :], f32(wh[:, u, :]), SUB).then_inc(w_split, 1)

            with seq.loop("layer", DEPTH) as L:
                dve.wait_ge(cols_in, lay(L, 16, 16))
                ffn(L, U_FFN1, B_FFN1, 0, 0, C_F1, 0, 0)
                barrier(dve, L, 0)

                norm(L, 1, C_MIX, 1)
                mean(L, 1, rstd[:, :], ps[:, 4, :])
                mean(L, 2, rstd_t[:, :], ps[:, 5, 0:TT])
                link(v.memset(ch[:, :, 0:CONV_K - 1], 0.0))
                rooted(L, 2)

                def taps(m, k0, k1):
                    for k in range(k0, k1):
                        w = col(m * CONV_K + (C_CW + k))
                        src = ch[:, m, k:k + T]
                        if k == 0:
                            link(ts(acc[:, m, :], src, w, col(m + C_CB), MUL, ADD))
                        else:
                            link(stt(acc[:, m, :], src, w, acc[:, m, :], MUL, ADD))

                FIRST, MID = 8, 15

                def pair(m, c, b, i=None):
                    scaled(cv[:, 0, :], L, c, b, i, 4, 4)
                    lo(L, c, i, 4)
                    scaled(cv[:, 1, :], L, c + 1, b + 1, i, 4, 4)
                    lo(L, c + 1, i, 4)
                    dve.wait_ge(c_sig, L * DT + m + 1)
                    link(stt(ch[:, m, CONV_K - 1:CONV_K - 1 + T], cv[:, 0, :], col(m + C_BA), cv[:, 1, :], ADD, MUL))
                    taps(m, 0, FIRST)

                for j in range(2):
                    pair(j, U_CONV + 2 * j, B_CONV + 2 * j)
                with seq.loop("conv", 3) as i:
                    for j in range(2):
                        pair(i * 2 + (2 + j), U_CONV + 4 + 2 * j, B_CONV + 4 + 2 * j, i)
                for j in range(4):
                    scaled(ctb[:, j, :], L, U_CT + j, B_CT + j)
                    lo(L, U_CT + j)
                    if j % 2:
                        taps(j // 2, FIRST, MID)
                dve.wait_ge(rows_in, lay(L, 16, 16))
                used(L, U_GATE)
                for t in range(TT):
                    ins = stt(gates[:, t, :], ps[:, B_GATE % SLOTS, t * 48:(t + 1) * 48], rstd_t[:, t:t + 1],
                              row[:, R_BG:R_KC], MUL, ADD)
                ins.then_inc(bank_free, 2)
                lo(L, U_GATE)

                def block_rest(jj):
                    dve.wait_ge(yc_h, lay(L, 32, jj + 1))
                    stt(ycl[:, jj % 8, :].rearrange("p (h n) -> p h n", h=NKV), at_pos(jj // 16, jj % 16),
                        col(C_POS + jj), f32(ych[:, jj % 8, :]).rearrange("p (h n) -> p h n", h=NKV),
                        ADD, SUB).then_inc(yc_l, 1)

                for jj in range(8):
                    block_rest(jj)
                for u in range(8):
                    used(L, U_CMP + u)
                    c = u // 4
                    if u % 4 == 3:
                        for m in range(2):
                            v.tensor_copy(hid[:, m, :], ps[:, (B_CMP + 2 * c + m) % SLOTS, 0:P]).then_inc(bank_free, 1)
                    lo(L, U_CMP + u)
                    if u < 6:
                        for jj in range(8 + 4 * u, 12 + 4 * u):
                            block_rest(jj)
                    if u % 4 == 1:
                        taps(2 + c, FIRST, MID)
                    if u % 4 == 3:
                        dve.wait_ge(hid_h, lay(L, 2, c + 1))
                        if c == 0:
                            tt(hkl[:, :, :], hid[:, :, :], f32(hkh[:, :, :]), SUB).then_inc(hid_l, 1)
                        else:
                            for m in range(2):
                                ins = tt(hvl[:, m, :].rearrange("p (g j n) -> p g j n", g=NKV, j=HPG), copies(m),
                                         f32(hvh[:, m, :]).rearrange("p (g j n) -> p g j n", g=NKV, j=HPG), SUB)
                            ins.then_inc(hid_l, 1)

                def rope(x1, x2, cos, sin, tmp):
                    tt(tmp[0], x1, cos, MUL)
                    tt(tmp[1], x2, sin, MUL)
                    tt(tmp[2], x2, cos, MUL)
                    link(tt(tmp[3], x1, sin, MUL))
                    tt(x1, tmp[0], tmp[1], SUB)
                    link(tt(x2, tmp[2], tmp[3], ADD))

                dve.wait_ge(kc_ready, lay(L, 1, 1))
                v.tensor_copy(kc[:, :], ps[:, B_W2 % SLOTS, 0:HD]).then_inc(bank_free, 1)
                used(L, U_W2)
                dve.wait_ge(vcb_zero, lay(L, 1, 1))
                for j in range(HPG):
                    r = slice(NCMP * j, NCMP * (j + 1))
                    ins = v.tensor_copy(vcb[r, :, j, :],
                                        ps[r, (B_W2 + 1) % SLOTS, 0:NKV * HD].rearrange("p (g d) -> p g d", g=NKV))
                ins.then_inc(bank_free, 1)
                lo(L, U_W2)
                evacuated(L, B_W2)
                link(tt(kcw[:, :], kc[:, :], kc[:, :], MUL))
                link(v.reduce_sum(small[:, 32:33], kcw[:, :], AX.X))
                link(ts(small[:, 32:33], small[:, 32:33], 1.0 / HD, EPS, MUL, ADD))
                v.reciprocal(small[:, 32:33], small[:, 32:33]).then_inc(t_rinv, 1)
                dve.wait_ge(t_rs, lay(L, 4, 1))
                link(stt(kc[:, :], kc[:, :], small[:, 32:33], row[:, R_KC:R_KC + HD], MUL, MUL))
                rope(kc[:, 0:HALF], kc[:, HALF:2 * HALF], con_[:, K_COSC:K_COSC + HALF], con_[:, K_SINC:K_SINC + HALF],
                     [kcw[:, n * HALF:(n + 1) * HALF] for n in range(4)])

                def tok_block(xt, n, m, i=None):
                    for j in range(4):
                        used(L, U_TOK + 4 * n + j, i, 4)
                        if j == 3:
                            bias = row[:, bass.ds(i * 512 + R_B, 512)] if i is not None \
                                else row[:, R_B + n * 512:R_B + (n + 1) * 512]
                            for t in range(TT):
                                stt(xt[:, t, :], ps[:, (B_TOK + t) % SLOTS, :], rstd_t[:, t:t + 1], bias,
                                    MUL, ADD).then_inc(bank_free, 1)
                        lo(L, U_TOK + 4 * n + j, i, 4)
                    taps(m, FIRST, MID)

                def table(c):
                    return con_[:, c:c + 32].rearrange("p (t o e) -> p t o e", t=TT, o=1)\
                        .broadcast_to([P, TT, 8, HALF])

                def head_norm(xt, n, i=None):
                    dve.wait_ge(t_sq, lay(L, 3, n + 1, i, 1))
                    link(v.reduce_sum(small[:, 0:32], sqt[:, :, :].rearrange("p t (h d) -> p (t h) d", d=HD), AX.X))
                    link(ts(small[:, 0:32], small[:, 0:32], 1.0 / HD, EPS, MUL, ADD))
                    v.reciprocal(small[:, 0:32], small[:, 0:32]).then_inc(t_rinv, 1)
                    gain = row[:, bass.ds(i * 512 + R_G, 512)] if i is not None \
                        else row[:, R_G + n * 512:R_G + (n + 1) * 512]
                    gain = gain.rearrange("p (o n) -> p o n", o=1)
                    link(tt(xt, xt, gain.broadcast_to([P, TT, 512]), MUL))
                    dve.wait_ge(t_rs, lay(L, 4, n + 2, i, 1))
                    xt = xt.rearrange("p t (h d) -> p t h d", d=HD)
                    rs = small[:, 0:32].rearrange("p (t h o) -> p t h o", h=8, o=1)
                    link(tt(xt, xt, rs.broadcast_to([P, TT, 8, HD]), MUL))
                    rope(xt[:, :, :, 0:HALF], xt[:, :, :, HALF:2 * HALF], table(K_COS), table(K_SIN),
                         [sqt[:, c, 0:256].rearrange("p (t h e) -> p t h e", t=TT, h=8) for c in range(4)])

                with seq.loop("tok", 2) as i:
                    xt = tq[:, :, bass.ds(i * 512, 512)]
                    tok_block(xt, 0, i + 4, i)
                    head_norm(xt, 0, i)
                tok_block(tkv[:, 0, :, :], 2, 6)
                head_norm(tkv[:, 0, :, :], 2)
                tok_block(tkv[:, 1, :, :], 3, 7)
                barrier(dve, L, 1)

                gc = gates[:, :, :].rearrange("p t (h c) -> p t h c", c=3)[:, :, :, 0]
                dve.wait_ge(g_sig, lay(L, 1, 1))
                link(tt(gc, gc, con_[:, K_VALID:K_VALID + TT].rearrange("p (t o) -> p t o", o=1)
                        .broadcast_to([P, TT, NH]), MUL))
                v.memset(att[:, 0:1], 0.0).then_inc(o_read, 1)
                dve.wait_ge(k_hi, lay(L, 9, 1))
                tt(kcT[:, 1, :], ps[:, 6, 0:P], f32(kcT[:, 0, :]), SUB).then_inc(k_lo, 1)
                for n in range(2 * TT):
                    dve.wait_ge(k_hi, lay(L, 9, n + 2))
                    k = slice(n // 2 * P, (n // 2 + 1) * P)
                    tt(kT[:, n % 2, 1, :, k], ps[:, n % 4, :].rearrange("p (g k) -> p g k", g=NKV),
                       f32(kT[:, n % 2, 0, :, k]), SUB).then_inc(k_lo, 1)

                def steps_done(q, g, c):
                    return lay(L, 16, 4 * q + c, g, 1)

                def rest_q(q, g):
                    dve.wait_ge(q_hi, steps_done(q, g, 1))
                    tt(q2T[HD:P, :, :], ps[HD:P, 7, :].rearrange("p (j k) -> p j k", j=HPG), f32(q2T[HD:P, :, :]), SUB)\
                        .then_inc(q_lo, 1)

                def sub_max(q, g):
                    dve.wait_ge(sc_done, steps_done(q, g, 1))
                    sc = ps[:, 7, 0:P].rearrange("p (j n) -> p j n", j=HPG)
                    link(v.tensor_reduce(att[:, 0:4], sc, AX.X, ALU.max))
                    tt(pcs[:, :, :], sc, att[:, 0:4].rearrange("p (j o) -> p j o", o=1)
                       .broadcast_to([P, HPG, NCMP]), SUB).then_inc(sc_sub, 1)

                def row_max(q, g, j):
                    r = j % 2
                    dve.wait_ge(s_done, lay(L, 64, 16 * q + j + 1, g, 4))
                    link(v.tensor_reduce(att[:, 8 + 2 * r:10 + 2 * r], ps[:, 2 * r:2 * r + 2, 0:(q + 1) * P], AX.X,
                                         ALU.max))
                    ts(att[:, 16 + 2 * r:18 + 2 * r], att[:, 8 + 2 * r:10 + 2 * r], -SCALE, None, MUL)\
                        .then_inc(s_max, 1)

                def inverse(j):
                    def pair_of(c):
                        return att[:, c:c + 8].rearrange("p (c j) -> p c j", c=2)[:, :, j:j + 2]
                    return v.reciprocal(pair_of(56), pair_of(28))

                def more_taps(q, g, n):
                    for m in range(2 * q, 2 * q + 2):
                        ins = stt(acc[:, m, :], ch[:, m, bass.ds(g * 4 + (MID + n), T)],
                                  col(g * 4 + (C_CW + m * CONV_K + MID + n)), acc[:, m, :], MUL, ADD)
                    link(ins)

                def weight(c):
                    return att[:, 40 + 4 * c:44 + 4 * c].rearrange("p (j o) -> p j o", o=1).broadcast_to([P, HPG, HD])

                def step(q, g, Q, G):
                    more = Q < TT
                    o = heads(q, g).rearrange("p (j d) -> p j d", j=HPG)

                    def gate(c, n):
                        return gates[:, q, bass.ds(g * 12, 12)].rearrange("p (j c) -> p c j", c=3)[:, c:c + n, :]

                    dve.wait_ge(ptc_tr, steps_done(q, g, 1))
                    v.tensor_copy(ptc[:, :], ps[:, 7, P:2 * P]).then_inc(ptc_ev, 1)
                    link(v.reduce_sum(att[:, 24:28], pc[:, :].rearrange("p (j n) -> p j n", j=HPG), AX.X))
                    row_max(q, g, 2)
                    link(v.reciprocal(att[:, 52:56], att[:, 24:28]))
                    link(tt(att[:, 40:44], att[:, 52:56], gate(0, 1).rearrange("p c j -> p (c j)"), MUL))
                    dve.wait_ge(oc_done, steps_done(q, g, 1))
                    tt(o, ps[:, 7, 2 * P:4 * P].rearrange("p (j d) -> p j d", j=HPG), weight(0), MUL)\
                        .then_inc(oc_read, 1)
                    more_taps(q, g, 0)
                    row_max(q, g, 3)
                    inverse(0)
                    if more:
                        rest_q(Q, G)
                    more_taps(q, g, 1)
                    if more:
                        sub_max(Q, G)
                        row_max(Q, G, 0)
                        more_taps(q, g, 2)
                        row_max(Q, G, 1)
                    else:
                        more_taps(q, g, 2)
                        dve.wait_ge(p_exp, lay(L, 64, 64))
                    link(inverse(2))
                    more_taps(q, g, 3)
                    link(tt(att[:, 44:52].rearrange("p (c j) -> p c j", c=2),
                            att[:, 56:64].rearrange("p (c j) -> p c j", c=2), gate(1, 2), MUL))
                    dve.wait_ge(pv_done, lay(L, 64, 16 * q + 4, g, 4))
                    dve.wait_ge(oc_read, steps_done(q, g, 1))
                    tt(ot[:, 0, :, :], ps[:, 6, 0:256].rearrange("p (j d) -> p j d", j=HPG), weight(1), MUL)
                    tt(ot[:, 1, :, :], ps[:, 6, 256:512].rearrange("p (j d) -> p j d", j=HPG), weight(2), MUL)\
                        .then_inc(o_read, 1)
                    dve.wait_ge(o_read, lay(L, 17, 4 * q + 2, g, 1))
                    link(tt(o, o, ot[:, 0, :, :], ADD))
                    link(tt(o, o, ot[:, 1, :, :], ADD))

                rest_q(0, 0)
                sub_max(0, 0)
                row_max(0, 0, 0)
                row_max(0, 0, 1)
                steps(step, lambda n: seq.loop("att", n))
                barrier(dve, L, 2)

                def branch_gate(j, c, i=None):
                    scaled(mt[:, j, :], L, U_MERGE + c + j, B_MERGE + c + j, i, 4, 4)
                    lo(L, U_MERGE + c + j, i, 4)

                def branch_out(m, c, i=None):
                    dve.wait_ge(m_sig, lay(L, 2 * DT, 2 + c // 2, i, 2))
                    for j in range(2, 4):
                        used(L, U_MERGE + c + j, i, 4)
                        tt(mt[:, j, :], ps[:, (B_MERGE + j) % SLOTS, :], mt[:, 3 - j, :], MUL).then_inc(bank_free, 1)
                        lo(L, U_MERGE + c + j, i, 4)
                    evacuated(L, B_MERGE + c + 3, i, 4)
                    link(tt(yf[:, m, :], mt[:, 2, :], mt[:, 3, :], ADD))

                norm(L, 2, C_MIX, None)
                dve.wait_ge(ln_mu, lay(L, 1, 1))
                for m in range(DT):
                    stt(acc[:, m, :], ps[:, 4, :], -1.0 / D, acc[:, m, :], MUL, ADD).then_inc(ln_d, 1)
                for m in range(DT):
                    dve.wait_ge(ot_h, lay(L, 8, m + 1))
                    tt(ol[:, m, :], ps[:, 6 + m % 2, :], f32(oh[:, m, :]), SUB).then_inc(ot_l, 1)
                dve.wait_ge(ln_var, lay(L, 8, 8))
                link(ts(ssq[:, :], ps[:, 5, :], 1.0 / D, EPS, MUL, ADD))
                v.reciprocal(ssq[:, :], ssq[:, :]).then_inc(ln_rinv, 1)
                branch_gate(0, 0)
                dve.wait_ge(ln_rs, lay(L, 1, 1))
                dve.wait_ge(ln_d, lay(L, 8, 8))
                for m in range(DT):
                    tt(acc[:, m, :], acc[:, m, :], ssq[:, :], MUL).then_inc(ln_e, 1)
                for m in range(DT):
                    dve.wait_ge(ln_hi, lay(L, 8, m + 1))
                    tt(cvl[:, m, :], acc[:, m, :], f32(cvh[:, m, :]), SUB).then_inc(ln_lo, 1)
                branch_gate(1, 0)
                branch_out(0, 0)
                with seq.loop("merge", DT - 1) as i:
                    branch_gate(0, 4, i)
                    branch_gate(1, 4, i)
                    branch_out(i + 1, 4, i)
                barrier(dve, L, 3)
                for k in range(DT):
                    dve.wait_ge(s_xh, lay(L, 48, 24 + k + 1))
                    tt(xl[:, k, :], yf[:, k, :], f32(xh[:, k, :]), SUB).then_inc(s_xl, 1)
                for m in range(DT):
                    used(L, U_OUT + m)
                    tt(x[:, m, :], ps[:, (B_OUT + m) % SLOTS, :], x[:, m, :], ADD).then_inc(bank_free, 1)
                    lo(L, U_OUT + m)
                barrier(dve, L, 4)
                ffn(L, U_FFN2, B_FFN2, 1, 4, C_F2, 2, 3)
                barrier(dve, L, 5)

                for k in range(2):
                    dve.wait_ge(p_hi_, lay(L, 2, k + 1))
                    tt(pl[:, k, :], pf[:, k, :], f32(ph[:, k, :]), SUB).then_inc(p_lo_, 1)
                norm(L, 5, C_PLE, 3)
                mean(L, 4, rstd[:, :], ps[:, 4, :])
                for j in range(2):
                    used(L, U_PROJ + j)
                    for m in range(4 * j, 4 * j + 4):
                        v.tensor_copy(pe_[:, m, :], ps[:, (B_PROJ + m) % SLOTS, :]).then_inc(bank_free, 1)
                    lo(L, U_PROJ + j)
                for m in range(DT):
                    add_square(L, 4, m)
                rooted(L, 4)
                for m in range(DT):
                    scaled(fa[:, m % 2, :], L, U_PLE + m, B_PLE + m)
                    lo(L, U_PLE + m)
                    if m == 0:
                        mean(L, 5, ssq[:, :], ps[:, 4, :])
                        rooted(L, 5)
                        for k in range(DT):
                            ins = stt(pe_[:, k, :], pe_[:, k, :], col(C_POST + k), ssq[:, :], MUL, MUL)
                        link(ins)
                    dve.wait_ge(g_s, lay(L, DT, m + 1))
                    link(tt(fb[:, m % 2, :], fb[:, m % 2, :], pe_[:, m, :], MUL))
                    link(tt(x[:, m, :], x[:, m, :], fb[:, m % 2, :], ADD))
                barrier(dve, L, 6)


_OUT = "out_0_dram"


def kernel(**inputs):
    import concourse.bacc as bacc
    from concourse.bass_utils import run_bass_kernel_spmd

    i = {k: np.asarray(a) for k, a in inputs.items()}
    stream, cols, rows = pack(i)
    con, masks = constants()
    arrays = {
        "stream": stream, "cols": cols, "rows": rows, "const": con, "masks": masks,
        "xT": np.ascontiguousarray(i["x"][0].T.reshape(DT, P, T).transpose(1, 0, 2)),
        "pT": np.ascontiguousarray(i["p"][:, 0].transpose(0, 2, 1).reshape(DEPTH, 2, P, T).transpose(0, 2, 1, 3)),
    }
    nc = bacc.Bacc("TRN2", target_bir_lowering=False, num_devices=1)
    args = [nc.dram_tensor(n, a.shape, F32, kind="ExternalInput").ap() for n, a in arrays.items()]
    out = nc.dram_tensor(_OUT, (P, DT, T), F32, kind="ExternalOutput").ap()
    build(nc, *args, out)
    got = run_bass_kernel_spmd(nc, [arrays], core_ids=[0]).results[0][_OUT]
    return np.ascontiguousarray(np.asarray(got).transpose(2, 1, 0).reshape(1, T, D))
```

```python
from contextlib import ExitStack

import numpy as np

import concourse.bass as bass
from concourse import mybir

F32 = mybir.dt.float32
F32R = mybir.dt.float32r
ALU = mybir.AluOpType
ACT = mybir.ActivationFunctionType
AX = mybir.AxisListType

P = 128
D, T, DEPTH = 1024, 512, 2
DT = D // P
TT = T // P
FF = 2816
FT = FF // P
FSTEPS = FT // 2
PLE = 256
CONV_K = 31
NH, NKV, HPG, HD = 16, 4, 4, 64
HALF = 8
ROPE_THETA = 500000.0
CMP_LEN, CMP_STRIDE, CMP_HID = 32, 16, 256
NCMP = T // CMP_STRIDE
KVW = NKV * HD
OFF_Q = 2 * D
OFF_KV = OFF_Q + NH * HD
OFF_GATE = OFF_KV + 6 * KVW
OFF_MERGE = OFF_GATE + 3 * NH
NEG = -1e30
EPS = 1e-6
SCALE = HD ** -0.5
XTOK = T + CMP_STRIDE

SBUF_BASE, SBUF_END = 16512, 229368

SLOTS = 4
U_FFN1 = 0
U_CONV = U_FFN1 + 3 * FT
U_CT = U_CONV + 2 * DT
U_GATE = U_CT + 4
U_K = U_GATE + 1
U_CMP = U_K + 4
U_Q0 = U_CMP + 8
U_W2 = U_Q0 + 4
U_Q1 = U_W2 + 1
U_V = U_Q1 + 4
U_MERGE = U_V + 4
U_OUT = U_MERGE + 4 * DT
U_FFN2 = U_OUT + DT
U_PROJ = U_FFN2 + 3 * FT
U_PLE = U_PROJ + 2
UNITS = U_PLE + DT
assert UNITS % SLOTS == 0
B_FFN1 = 0
B_CONV = B_FFN1 + 2 * FT
B_CT = B_CONV + 2 * DT
B_GATE = B_CT + 4
B_K = B_GATE + 1
B_GATE_T = B_K + TT
B_CMP = B_GATE_T + 1
B_Q0 = B_CMP + 4
B_W2 = B_Q0 + TT
B_Q1 = B_W2 + 2
B_V = B_Q1 + TT
B_MERGE = B_V + TT
B_OUT = B_MERGE + 4 * DT
B_FFN2 = B_OUT + DT
B_PROJ = B_FFN2 + 2 * FT
B_PLE = B_PROJ + DT
BANKS = B_PLE + DT
assert BANKS % SLOTS == 0
BARRIERS = 7

C_F1, C_MIX, C_F2, C_PLE, C_POST, C_BA, C_BG, C_BGC, C_BGN = range(0, 72, 8)
C_BCT, C_CB, C_LG, C_LB, C_POS, C_BB, C_CW = 72, 76, 84, 92, 100, 132, 133
NCOL = C_CW + DT * CONV_K
R_B, R_G, R_KC, R_B1 = 0, 2048, 3072, 3136
NROW = R_B1 + 2 * CMP_HID
K_ID, K_ONE, K_COS, K_SIN, K_COSC, K_SINC, K_VALID, NCON = 0, 128, 256, 288, 320, 328, 336, 340
K_MASK, K_CM, NMASK = 0, 128, 640


FIRST = 7
MID = CONV_K - 4 * TT

def constants():
    c = np.zeros((P, NCON), np.float32)
    masks = np.zeros((P, NMASK), np.float32)
    c[:, K_ID:K_ID + P] = np.eye(P)
    r = np.arange(P)
    masks[:, K_MASK:K_MASK + P] = np.where(r[None, :] <= r[:, None], 0.0, NEG)
    c[:, K_ONE:K_ONE + P] = 1.0
    inv = (np.float32(ROPE_THETA) ** (-np.arange(HALF, dtype=np.float32) / np.float32(HALF))).astype(np.float32)
    n = np.arange(NCMP)
    for q in range(TT):
        t = q * P + r
        seen = (n[None, :] * CMP_STRIDE + CMP_LEN - 1 <= t[:, None]) & (n[None, :] < NCMP - 1)
        masks[:, K_CM + q * P:K_CM + (q + 1) * P] = np.tile(np.where(seen, 0.0, NEG), (1, 4))
        ang = (t.astype(np.float32)[:, None] * inv[None, :]).astype(np.float32)
        c[:, K_COS + q * HALF:K_COS + (q + 1) * HALF] = np.cos(ang)
        c[:, K_SIN + q * HALF:K_SIN + (q + 1) * HALF] = np.sin(ang)
        c[:, K_VALID + q] = t >= CMP_LEN - 1
    pos = ((r % NCMP) * CMP_STRIDE + CMP_LEN - 1).astype(np.float32)
    ang = (pos[:, None] * inv[None, :]).astype(np.float32)
    c[:, K_COSC:K_COSC + HALF] = np.cos(ang)
    c[:, K_SINC:K_SINC + HALF] = np.sin(ang)
    return c, masks


def pack(i):
    stream = np.zeros((DEPTH * UNITS + SLOTS, P, 1024), np.float32)
    cols = np.zeros((DEPTH + 1, P, NCOL), np.float32)
    rows = np.zeros((DEPTH, NROW), np.float32)

    def tiles(w):
        return w.reshape(w.shape[0] // P, P, w.shape[1]).transpose(1, 0, 2).reshape(P, -1)

    def cm(v):
        return v.reshape(-1, P).T

    for l in range(DEPTH):
        out = stream[l * UNITS:(l + 1) * UNITS]

        def ffn(u, w1, w2):
            for s in range(FSTEPS + 1):
                if s < FSTEPS:
                    for j in range(2):
                        for c in range(2):
                            m = c * FF + (2 * s + j) * P
                            out[u] = tiles(w1[:, m:m + P])
                            u += 1
                if s > 0:
                    for j in range(2):
                        f = (2 * (s - 1) + j) * P
                        out[u] = w2[f:f + P]
                        u += 1

        def cols_of(u, w, n):
            for m in range(n):
                out[u + m] = tiles(w[:, m * P:(m + 1) * P])

        ffn(U_FFN1, i["ffn1_w_in"][l], i["ffn1_w_out"][l])
        ffn(U_FFN2, i["ffn2_w_in"][l], i["ffn2_w_out"][l])
        w, b = i["w_in"][l], i["b_in"][l]
        kv = [slice(OFF_KV + j * KVW, OFF_KV + (j + 1) * KVW) for j in range(6)]
        for m in range(DT):
            out[U_CONV + 2 * m] = tiles(w[:, m * P:(m + 1) * P])
            out[U_CONV + 2 * m + 1] = tiles(w[:, D + m * P:D + (m + 1) * P])
            u = U_MERGE + 4 * m
            out[u] = tiles(w[:, OFF_MERGE + m * P:OFF_MERGE + (m + 1) * P])
            out[u + 1] = tiles(w[:, OFF_MERGE + D + m * P:OFF_MERGE + D + (m + 1) * P])
            out[u + 2] = tiles(i["nsa_w_out"][l][:, m * P:(m + 1) * P])
            out[u + 3] = tiles(i["conv_w_out"][l][:, m * P:(m + 1) * P])
        cols_of(U_CT, w[:, kv[0].start:kv[1].stop], 4)
        out[U_GATE][:, :DT * 3 * NH] = tiles(w[:, OFF_GATE:OFF_MERGE])
        for c in range(2):
            w1 = tiles(i["cmp_w1"][l, c]).reshape(P, 4, 1024)
            for j in range(4):
                out[U_CMP + 4 * c + j] = w1[:, j]
            out[U_W2][:, c * 128:(c + 1) * 128] = tiles(i["cmp_w2"][l, c])
        blocks = [(w[:, OFF_Q:OFF_Q + 512], b[OFF_Q:OFF_Q + 512]),
                  (w[:, OFF_Q + 512:OFF_KV], b[OFF_Q + 512:OFF_KV]),
                  (np.concatenate([w[:, kv[2]], w[:, kv[4]]], 1), np.concatenate([b[kv[2]], b[kv[4]]])),
                  (np.concatenate([w[:, kv[3]], w[:, kv[5]]], 1), np.concatenate([b[kv[3]], b[kv[5]]]))]
        for n, (wb, bb) in enumerate(blocks):
            wb = tiles(wb)
            for j in range(4):
                out[(U_Q0, U_Q1, U_K, U_V)[n] + j] = wb[:, j * 1024:(j + 1) * 1024]
            rows[l, R_B + n * 512:R_B + (n + 1) * 512] = bb
        cols_of(U_OUT, i["w_out"][l], DT)
        for j in range(2):
            out[U_PROJ + j] = tiles(i["ple_w_proj"][l][:, j * 512:(j + 1) * 512])
        cols_of(U_PLE, i["ple_w_gate"][l], DT)

        for c, v in ((C_F1, i["ffn1_norm"][l]), (C_MIX, i["mix_norm"][l]), (C_F2, i["ffn2_norm"][l]),
                     (C_PLE, i["ple_norm"][l]), (C_POST, i["ple_post_norm"][l]), (C_BA, b[:D]), (C_BG, b[D:2 * D]),
                     (C_BGC, b[OFF_MERGE:OFF_MERGE + D]), (C_BGN, b[OFF_MERGE + D:]),
                     (C_BCT, b[kv[0].start:kv[1].stop]), (C_CB, i["conv_b"][l]), (C_LG, i["conv_ln_g"][l]),
                     (C_LB, i["conv_ln_b"][l])):
            v = cm(v)
            cols[l][:, c:c + v.shape[1]] = v
        for c in range(2):
            cols[l][:, C_POS + 16 * c:C_POS + 16 * (c + 1)] = cm(i["cmp_pos"][l, c].reshape(-1))
        cols[l][:, C_CW:] = i["conv_w"][l].reshape(CONV_K, DT, P).transpose(2, 1, 0).reshape(P, -1)
        g = [i["q_norm"][l]] * 8 + [i["k_norm"][l, 1]] * 4 + [i["k_norm"][l, 2]] * 4
        rows[l, R_G:R_KC] = np.concatenate(g)
        cols[l][0:3 * NH, C_BB] = b[OFF_GATE:OFF_MERGE]
        rows[l, R_KC:R_B1] = i["k_norm"][l, 0]
        rows[l, R_B1:] = i["cmp_b1"][l].reshape(-1)
    return stream, cols, rows


LINKS = {'dve.conv': 9, 'dve.att': 12, 'dve.merge': 1, 'dve.layer': 317}


class Chain:

    def __init__(self, eng, sem, name, settle):
        self.eng, self.sem, self.name, self.n, self.terms, self.settle = eng, sem, name, 0, [], settle

    def link(self, ins):
        ins.then_inc(self.sem, 1)
        self.n += 1
        v = self.n
        for reg, per in self.terms:
            v = reg * per + v
        self.eng.wait_ge(self.sem, v)

    def loop(self, key, trips):
        return _Loop(self, self.name + key, trips)


class _Loop:
    def __init__(self, chain, key, trips):
        self.c, self.key, self.trips = chain, key, trips

    def __enter__(self):
        self.c.settle(self.c.eng)
        self.fori = self.c.eng.Fori(0, self.trips)
        reg = self.fori.__enter__()
        self.start = self.c.n
        self.per = LINKS.get(self.key, 0)
        self.c.terms.append((reg, self.per))
        return reg

    def __exit__(self, *exc):
        if exc[0] is None:
            got = self.c.n - self.start
            assert got == self.per, f"LINKS[{self.key!r}] = {got}"
            self.c.terms.pop()
            self.c.n = self.start + self.per * self.trips
        return self.fori.__exit__(*exc)


def build(nc, stream, cols_d, rows_d, const_d, mask_d, x_d, p_d, out_d):
    ctx = ExitStack()
    with ctx:
        end = [SBUF_BASE]

        def region(nbytes):
            at = end[0]
            end[0] += (nbytes + 31) // 32 * 32
            return at

        def sb(name, shape, dt, at):
            n = 4
            for s in shape[1:]:
                n *= s
            return nc.alloc_sbuf_tensor_at(name, shape, dt, offset=at), at + n

        def one(name, shape, dt=F32):
            n = 4
            for s in shape[1:]:
                n *= s
            return sb(name, shape, dt, region(n))[0]

        x = one("x", [P, DT, T])
        raw = one("raw", [P, SLOTS, 1024])
        wh = one("w_hi", [P, SLOTS, 1024], F32R)
        wl = one("w_lo", [P, SLOTS, 1024], F32R)
        con = one("con", [P, NCON])
        ident_r = one("ident_r", [P, P], F32R)
        mask_r = one("mask_r", [P, P], F32R)
        cmask_r = one("cmask_r", [P, TT, P], F32R)
        cols = one("cols", [P, NCOL])
        rstd = one("rstd", [P, T])
        rstd_t = one("rstd_t", [P, TT])
        ssq = one("ssq", [P, T])
        sq = one("sq", [P, 2, T])
        gates = one("gates", [P, TT, 3 * NH])
        small = one("small", [P, 64])
        att = one("att", [P, 64])
        rB, rT, rA = region(32768), region(32768 + 512), region(4 * DT * (T + CONV_K - 1) + 16384)
        rD = end[0]

        xh, a = sb("x_hi", [P, DT, T], F32R, rB)
        xl, _ = sb("x_lo", [P, DT, T], F32R, a)
        kT, _ = sb("kT", [P, 2, 2, NKV, T], F32R, rB)
        tok = sb("tok", [P, 2 * TT * D], F32, rT + 512)[0][:, :]
        tq = tok[:, 0:TT * D].rearrange("p (t n) -> p t n", t=TT)
        tkv = tok[:, TT * D:2 * TT * D].rearrange("p (c t n) -> p c t n", c=2, t=TT)
        tv, tk = tkv[:, 0], tkv[:, 1]
        xc, a = sb("xc", [P, 2, NKV, XTOK], F32, rT)
        ych, a = sb("yc_hi", [P, 8, P], F32R, a)
        ycl, a = sb("yc_lo", [P, 8, P], F32R, a)
        assert a <= rT + 512 + 4 * (TT * D + TT * 512), "the compressor's input reaches into k"
        yf, a = sb("yf", [P, DT, T], F32, rT)
        mt, _ = sb("mt", [P, 4, T], F32, a)
        pe_, a = sb("emb", [P, DT, T], F32, rT)
        pf, a = sb("pf", [P, 2, T], F32, a)
        ph, a = sb("p_hi", [P, 2, T], F32R, a)
        pl, a = sb("p_lo", [P, 2, T], F32R, a)
        acc, ch_at = sb("conv_acc", [P, DT, T], F32, rA)
        ch, _ = sb("conv_in", [P, DT, T + CONV_K - 1], F32, ch_at)
        cvl, _ = sb("cv_lo", [P, DT, T], F32R, rA)
        cvh, o_at = sb("cv_hi", [P, DT, T], F32R, ch_at)
        hh, a = sb("h_hi", [P, 2, 2, T], F32R, rD)
        hl, a = sb("h_lo", [P, 2, 2, T], F32R, a)
        fa, a = sb("fa", [P, 2, T], F32, a)
        fb, a = sb("fb", [P, 2, T], F32, a)
        row, a = sb("rows", [P, NROW], F32, rD)
        sqt, a2 = sb("sqt", [P, TT, 512], F32, a)
        ctb, _ = sb("ctb", [P, 4, T], F32, a)
        hvh, a3 = sb("hv_hi", [P, 2, 512], F32R, a)
        hvl, _ = sb("hv_lo", [P, 2, 512], F32R, a3)
        vcb, a = sb("vcb", [P, NKV, HPG, HD], F32, a2)
        kcT, a = sb("kcT", [P, 2, P], F32R, a)
        free_at = a
        cv, _ = sb("cv", [P, 2, T], F32, a)
        hid, a = sb("hid", [P, CMP_HID], F32, a)
        hkh, a = sb("hk_hi", [P, 2, P], F32R, a)
        hkl, a = sb("hk_lo", [P, 2, P], F32R, a)
        kc, a = sb("kc", [P, HD], F32, a)
        kcw, a = sb("kcw", [P, HD], F32, a)
        assert a <= SBUF_END
        k2, _ = sb("k2", [P, 2, 8, 2, HD], F32, rD)
        kc2, _ = sb("kc2", [P, 1, 2, HD], F32, rD + 16384)
        pr, a = sb("probs", [P, 2, 2, T], F32, rD)
        ptk, a = sb("probsT", [P, 2, 2, TT, P], F32, a)
        q2, a = sb("q2", [P, HPG, 2, HD], F32, a)
        q2T, a = sb("q2T", [P, HPG, P], F32R, a)
        pcs, a = sb("pcs", [P, HPG, NCMP], F32, a)
        pc, a = sb("pc", [P, P], F32, a)
        ptc, a = sb("ptc", [P, P], F32, a)
        ot, _ = sb("ot", [P, 2, HPG, HD], F32, free_at)
        assert a <= rD + NROW * 4 + 8192, "the attention's buffers reach into vcb"
        oh, a = sb("o_hi", [P, DT, T], F32R, o_at)
        ol, a = sb("o_lo", [P, DT, T], F32R, a)
        assert a <= SBUF_END
        masks, _ = sb("masks", [P, NMASK], F32, rD)

        con_ = con[:, :]
        ident = con_[:, K_ID:K_ID + P]
        ones = con_[:, K_ONE:K_ONE + P]

        ps = ctx.enter_context(nc.psum_tensor("ps", [P, 8, 512], F32))

        def sem(name):
            return ctx.enter_context(nc.semaphore(name))

        raw_in = [sem(f"raw_in{s}") for s in range(SLOTS)]
        w_hi, w_split, w_used = sem("s_w_hi"), sem("s_w_split"), sem("s_w_used")
        bank_free = sem("bank_free")
        bar = sem("bar")
        mask_in, settled = sem("mask_in"), sem("settled")
        const_in, x_in, cols_in, rows_in, p_in = (sem(n) for n in ("const_in", "x_in", "cols_in", "rows_in", "p_in"))
        xc_zero, ct_ready, xc_in, vcb_zero = sem("xc_zero"), sem("ct_ready"), sem("xc_in"), sem("vcb_zero")
        con_r = sem("con_r")
        s_xh, s_xl = sem("s_xh"), sem("s_xl")
        s_sq, s_ssq, s_sum, s_rinv, s_rstd = sem("s_sq"), sem("s_ssq"), sem("s_sum"), sem("s_rinv"), sem("s_rstd")
        f_silu, f_h, f_hh, f_hl = sem("f_silu"), sem("f_h"), sem("f_hh"), sem("f_hl")
        y_done, y_free = sem("y_done"), sem("y_free")
        c_sig = sem("c_sig")
        g_sig, g_tr = sem("g_sig"), sem("g_tr")
        yc_h, yc_l = sem("yc_h"), sem("yc_l")
        hid_act, hid_tr, hid_h, hid_l = sem("hid_act"), sem("hid_tr"), sem("hid_h"), sem("hid_l")
        kc_ready = sem("kc_ready")
        t_sq, t_rinv, t_rs = sem("t_sq"), sem("t_rinv"), sem("t_rs")
        ln_mu, ln_d, ln_sq, ln_var, ln_rinv, ln_rs = (sem(n) for n in ("ln_mu", "ln_d", "ln_sq", "ln_var", "ln_rinv",
                                                                   "ln_rs"))
        ln_e, ln_f, ln_hi, ln_lo = sem("ln_e"), sem("ln_f"), sem("ln_hi"), sem("ln_lo")
        k_two, k_tr, k_hi, k_lo = sem("k_two"), sem("k_tr"), sem("k_hi"), sem("k_lo")
        q_two, q_tr, q_hi, q_lo = sem("q_two"), sem("q_tr"), sem("q_hi"), sem("q_lo")
        sc_done, sc_sub, pc_exp, ptc_tr, ptc_ev, oc_done = (sem(n) for n in ("sc_done", "sc_sub", "pc_exp", "ptc_tr",
                                                                           "ptc_ev", "oc_done"))
        s_done, s_max, p_exp, pt_tr, pt_ev, pv_done = (sem(n) for n in ("s_done", "s_max", "p_exp", "pt_tr", "pt_ev",
                                                                       "pv_done"))
        oc_read, o_read = sem("oc_read"), sem("o_read")
        ot_tr, ot_h, ot_l = sem("ot_tr"), sem("ot_h"), sem("ot_l")
        m_sig = sem("m_sig")
        p_hi_, p_lo_ = sem("s_p_hi"), sem("s_p_lo")
        g_s = sem("g_s")
        dve_seq, act_seq = sem("dve_seq"), sem("act_seq")
        out_done = sem("out_done")

        def unit(L, c, i=None, pi=0):
            v = L * UNITS + c
            return v if i is None else i * pi + v

        def lay(L, per, c, i=None, pi=0):
            v = L * per + c
            return v if i is None else i * pi + v

        def col(c):
            return cols[:, c:c + 1] if isinstance(c, int) else cols[:, bass.ds(c, 1)]

        def at_pos(c, j):
            n = 2 * j // CMP_STRIDE
            return xc[:, c, :, :].rearrange("p h (n s) -> p h n s", s=CMP_STRIDE)[:, :, n:n + NCMP, 2 * j % CMP_STRIDE]

        def copies(b, m):
            return ps[:, b, m * P:(m + 1) * P].rearrange("p (g o n) -> p g o n", g=NKV, o=1)\
                .broadcast_to([P, NKV, HPG, NCMP])

        def twice(ap, h):
            return ap.rearrange("p (h o d) -> p h o d", h=h, o=1).broadcast_to([P, h, 2, HD])

        def flat(ap):
            return ap.rearrange("p a d -> p (a d)")

        def heads(q, g):
            return tok[:, bass.ds(g * 256 + q * D, 256)]

        def side(b, q):
            W = (q + 1) * P
            if 2 * W <= 512:
                return ps[:, b, 0:2 * W].rearrange("p (c k) -> p c k", c=2)
            return ps[:, b:b + 2, 0:W]

        def steps(step, loop):
            for q in range(TT):
                with loop(NKV - 1) as g:
                    step(q, g, q, g + 1)
                step(q, NKV - 1, q + 1, 0)

        def settle(eng):
            eng.sem_inc(settled, 1)

        def barrier(eng, L, k):
            settle(eng)
            eng.drain().then_inc(bar, 1)
            eng.wait_ge(bar, lay(L, 3 * BARRIERS, 3 * (k + 1)))
            settle(eng)

        block = ctx.enter_context(nc.Block())

        @block.sync
        def _(sp):
            sp.dma_start(con[:, :], const_d).then_inc(const_in, 16)
            sp.dma_start(masks[:, :], mask_d).then_inc(mask_in, 16)
            for u in range(SLOTS):
                sp.dma_start(raw[:, u, :], stream[u]).then_inc(raw_in[u], 16)
                if u == 0:
                    sp.dma_start(x[:, :, :], x_d).then_inc(x_in, 16)
            with sp.Fori(0, DEPTH * UNITS // SLOTS) as i:
                for s in range(SLOTS):
                    sp.wait_ge(w_split, i * SLOTS + s + 1)
                    sp.dma_start(raw[:, s, :], stream[i * SLOTS + s + SLOTS]).then_inc(raw_in[s], 16)
            for s in range(SLOTS):
                sp.wait_ge(raw_in[s], 16 * (DEPTH * UNITS // SLOTS + 1))
            sp.wait_ge(bar, 3 * BARRIERS * DEPTH)
            sp.dma_start(out_d, x[:, :, :]).then_inc(out_done, 16)
            sp.wait_ge(out_done, 16)

        @block.gpsimd
        def _(pool):
            pool.dma_start(cols[:, :], cols_d[0]).then_inc(cols_in, 16)
            with pool.Fori(0, DEPTH) as L:
                pool.wait_ge(bar, lay(L, 3 * BARRIERS, 3))
                settle(pool)
                pool.dma_start(row[:, :], rows_d[L].partition_broadcast(P)).then_inc(rows_in, 16)
                pool.memset(xc[:, :, :, :], 0.0).then_inc(xc_zero, 1)
                pool.memset(vcb[:, :, :, :], 0.0).then_inc(vcb_zero, 1)
                pool.wait_ge(bar, lay(L, 3 * BARRIERS, 3 * 4))
                settle(pool)
                pool.dma_start(pf[:, :, :], p_d[L]).then_inc(p_in, 16)
                pool.wait_ge(bar, lay(L, 3 * BARRIERS, 3 * BARRIERS))
                settle(pool)
                pool.dma_start(cols[:, :], cols_d[L + 1]).then_inc(cols_in, 16)
            pool.wait_ge(cols_in, 16 * (DEPTH + 1))

        @block.tensor
        def _(pe):
            mm = nc.tensor.matmul

            def mm3(out, ah, al, bh, bl, start, stop, **kw):
                mm(out, ah, bh, start=start, stop=False, **kw)
                mm(out, ah, bl, start=False, stop=False, **kw)
                return mm(out, al, bh, start=False, stop=stop, **kw)

            def bank(b):
                return ps[:, b % SLOTS, :]

            def product(L, c, b, rh, rl, i=None, pi=0, bi=0, first=None, ready=None):
                s = c % SLOTS
                pe.wait_ge(w_split, unit(L, c + 1, i, pi))
                pe.wait_ge(bank_free, lay(L, BANKS, b + 1, i, bi))
                for k in range(DT):
                    if first is not None:
                        pe.wait_ge(s_xl, lay(L, 8 * 6, first + k + 1))
                    if ready is not None:
                        pe.wait_ge(ready, lay(L, DT, k + 1))
                    last = mm3(bank(b), wh[:, s, k * P:(k + 1) * P], wl[:, s, k * P:(k + 1) * P],
                               rh[:, k, :], rl[:, k, :], k == 0, k == DT - 1)
                last.then_inc(w_used, 1)

            def stat_sum(L, s):
                pe.wait_ge(s_ssq, lay(L, 8 * 5, 8 * s + 8))
                mm(ps[:, 4, :], ones, ssq[:, :], start=True, stop=True).then_inc(s_sum, 1)

            def ffn(L, u0, b0, which, split, stat):
                def ab(c, b, i=None, first=None):
                    for j in range(4):
                        product(L, c + j, b + j, xh, xl, i, 12, 8, first if j == 0 else None)
                        if j == 1 and first is not None:
                            stat_sum(L, stat)

                def y(c, s, par, i=None):
                    pe.wait_ge(w_split, unit(L, c + 2, i, 12))
                    pe.wait_ge(f_hl, lay(L, 2 * FT, which * FT + 2 * s + 2, i, 4))
                    for m in range(DT):
                        pe.wait_ge(y_free, lay(L, 16 * FSTEPS, (which * FSTEPS + s) * 8 + m + 1, i, 16))
                        for j in range(2):
                            sl = (c + j) % SLOTS
                            last = mm3(ps[:, 4 + m % 4, :], wh[:, sl, m * P:(m + 1) * P], wl[:, sl, m * P:(m + 1) * P],
                                       hh[:, par, j, :], hl[:, par, j, :], j == 0, j == 1)
                            if m == DT - 1:
                                last.then_inc(w_used, 1)
                        if m < DT - 1:
                            last.then_inc(y_done, 1)

                ab(u0, b0, first=split)
                with pe.Fori(0, (FSTEPS - 1) // 2) as i:
                    for h in range(2):
                        ab(u0 + 4 + 6 * h, b0 + 4 + 4 * h, i)
                        y(u0 + 8 + 6 * h, h, h, i)
                y(u0 + 4 + 6 * (FSTEPS - 1), FSTEPS - 1, 0)

            with pe.Fori(0, DEPTH) as L:
                pe.wait_ge(const_in, 16)
                pe.wait_ge(con_r, 1)
                ffn(L, U_FFN1, B_FFN1, 0, 0, 0)
                barrier(pe, L, 0)

                product(L, U_CONV, B_CONV, xh, xl, first=8)
                product(L, U_CONV + 1, B_CONV + 1, xh, xl)
                stat_sum(L, 1)
                for t in range(TT):
                    last = mm(ps[:, 5, t:t + 1], ssq[:, t * P:(t + 1) * P], ones[:, 0:1], start=True, stop=True)
                last.then_inc(s_sum, 1)
                for j in range(2, 4):
                    product(L, U_CONV + j, B_CONV + j, xh, xl)
                with pe.Fori(0, 3) as i:
                    for j in range(4):
                        product(L, U_CONV + 4 + j, B_CONV + 4 + j, xh, xl, i, 4, 4)
                for j in range(4):
                    product(L, U_CT + j, B_CT + j, xh, xl)
                s = U_GATE % SLOTS
                pe.wait_ge(w_split, unit(L, U_GATE + 1))
                pe.wait_ge(bank_free, lay(L, BANKS, B_GATE + 1))
                for k in range(DT):
                    w = slice(k * 3 * NH, (k + 1) * 3 * NH)
                    last = mm3(bank(B_GATE)[0:3 * NH, :], wh[:, s, w], wl[:, s, w], xh[:, k, :], xl[:, k, :], k == 0,
                               k == DT - 1)
                last.then_inc(w_used, 1)

                def tok_block(u, b, between=None):
                    for j in range(4):
                        s = (u + j) % SLOTS
                        pe.wait_ge(w_split, unit(L, u + j + 1))
                        for t in range(TT):
                            if j == 0:
                                pe.wait_ge(bank_free, lay(L, BANKS, b + t + 1))
                            tk = slice(t * P, (t + 1) * P)
                            for kk in range(2):
                                w = slice(kk * 512, (kk + 1) * 512)
                                last = mm3(bank(b + t), xh[:, 2 * j + kk, tk], xl[:, 2 * j + kk, tk], wh[:, s, w],
                                           wl[:, s, w], j == 0 and kk == 0, j == 3 and kk == 1)
                        last.then_inc(w_used, 1)
                        if between is not None and j == 1:
                            between()

                tok_block(U_K, B_K)
                pe.wait_ge(g_sig, lay(L, 1, 1))
                pe.wait_ge(bank_free, lay(L, BANKS, B_GATE_T + 1))
                for t in range(TT):
                    last = nc.tensor.transpose(bank(B_GATE_T)[:, t * P:(t + 1) * P],
                                               cv[:, 0, t * P:(t + 1) * P], ident)
                last.then_inc(g_tr, 1)
                def turn_hid(c):
                    pe.wait_ge(hid_act, lay(L, 2, c + 1))
                    for m in range(2):
                        last = nc.tensor.transpose(ps[:, 6 + c, m * P:(m + 1) * P], hid[:, m * P:(m + 1) * P], ident)
                    last.then_inc(hid_tr, 1)

                for u in range(8):
                    c, j = u // 4, u % 4
                    s = (U_CMP + u) % SLOTS
                    pe.wait_ge(w_split, unit(L, U_CMP + u + 1))
                    pe.wait_ge(yc_l, lay(L, 32, 4 * u + 4))
                    if j == 0:
                        pe.wait_ge(bank_free, lay(L, BANKS, B_CMP + 2 * c + 1))
                    for kk in range(4):
                        w = slice(kk * CMP_HID, (kk + 1) * CMP_HID)
                        r = (4 * j + kk) % 8
                        last = mm3(bank(B_CMP + 2 * c)[:, 0:CMP_HID], ych[:, r, :], ycl[:, r, :], wh[:, s, w],
                                   wl[:, s, w], j == 0 and kk == 0, j == 3 and kk == 3)
                    last.then_inc(w_used, 1)
                    if u == 5:
                        turn_hid(0)
                tok_block(U_Q0, B_Q0, lambda: turn_hid(1))
                s = U_W2 % SLOTS
                pe.wait_ge(w_split, unit(L, U_W2 + 1))
                pe.wait_ge(hid_l, lay(L, 2, 2))
                pe.wait_ge(bank_free, lay(L, BANKS, B_W2 + 2))
                for m in range(2):
                    w = slice(m * HD, (m + 1) * HD)
                    last = mm3(bank(B_W2)[:, 0:HD], hkh[:, m, :], hkl[:, m, :], wh[:, s, w], wl[:, s, w], m == 0,
                               m == 1)
                last.then_inc(kc_ready, 1)
                for g in range(NKV):
                    for m in range(2):
                        w, r = slice(P + m * HD, P + (m + 1) * HD), slice(g * P, (g + 1) * P)
                        last = mm3(bank(B_W2 + 1)[:, g * HD:(g + 1) * HD], hvh[:, m, r], hvl[:, m, r], wh[:, s, w],
                                   wl[:, s, w], g == 0 and m == 0, g == 3 and m == 1, skip_group_check=True)
                last.then_inc(w_used, 1)

                tok_block(U_Q1, B_Q1)
                tok_block(U_V, B_V)
                barrier(pe, L, 1)

                pe.wait_ge(k_two, lay(L, 5, 1))
                nc.tensor.transpose(ps[:, 6, 0:P], flat(kc2[:, 0, :, :]), ident).then_inc(k_tr, 1)
                for t in range(TT):
                    pe.wait_ge(k_two, lay(L, 5, t + 2))
                    for kind in range(2):
                        n = 2 * t + kind
                        if n >= 4:
                            pe.wait_ge(k_lo, lay(L, 9, n - 2))
                        for g in range(NKV):
                            last = nc.tensor.transpose(ps[:, n % 4, g * P:(g + 1) * P],
                                                       flat(k2[:, t % 2, kind * NKV + g, :, :]), ident)
                        last.then_inc(k_tr, 1)

                def steps_done(q, g, c):
                    return lay(L, 16, 4 * q + c, g, 1)

                def heads_done(q, g, c):
                    return lay(L, 64, 16 * q + c, g, 4)

                def turn_q(q, g):
                    pe.wait_ge(q_two, steps_done(q, g, 1))
                    for j in range(HPG):
                        last = nc.tensor.transpose(ps[:, 7, j * P:(j + 1) * P], flat(q2[:, j, :, :]), ident)
                    last.then_inc(q_tr, 1)

                def compressed(q, g):
                    pe.wait_ge(q_lo, steps_done(q, g, 1))
                    mm(ps[:, 7, 0:P], ident_r[:, :], cmask_r[:, q, :], start=True, stop=False, skip_group_check=True)
                    for j in range(HPG):
                        for c in range(2):
                            last = mm(ps[:, 7, j * NCMP:(j + 1) * NCMP], q2T[:, j, :],
                                      kcT[:, c, bass.ds(g * NCMP, NCMP)], start=False,
                                      stop=j == 3 and c == 1, skip_group_check=True)
                    last.then_inc(sc_done, 1)

                both = mask_r[:, :].rearrange("p (o k) -> p o k", o=1).broadcast_to([P, 2, P])

                def scores(q, g, j, first=False):
                    W = (q + 1) * P
                    if not first:
                        pe.wait_ge(p_exp, heads_done(q, g, j - 1))
                    o = side(2 * (j % 2), q)
                    if 2 * W <= 512:
                        mm(o, q2T[:, j, :], kT[:, :, 0, g, 0:W], start=True, stop=False)
                        mm(o, q2T[:, j, :], kT[:, :, 1, g, 0:W], start=False, stop=False)
                        last = mm(o[:, :, W - P:W], ident_r[:, :], both, start=False, stop=True)
                    else:
                        for kind in range(2):
                            mm(o[:, kind, :], q2T[:, j, :], kT[:, kind, 0, g, 0:W], start=True, stop=False)
                            mm(o[:, kind, :], q2T[:, j, :], kT[:, kind, 1, g, 0:W], start=False, stop=False)
                            last = mm(o[:, kind, W - P:W], ident_r[:, :], mask_r[:, :], start=False, stop=True)
                    last.then_inc(s_done, 1)

                def turn(q, g, j, first=False):
                    pe.wait_ge(p_exp, heads_done(q, g, j + 1))
                    if not first:
                        pe.wait_ge(pt_ev, heads_done(q, g, j))
                    for kind in range(2):
                        for k in range(q + 1):
                            last = nc.tensor.transpose(side(4, q)[:, kind, k * P:(k + 1) * P],
                                                       pr[:, j % 2, kind, k * P:(k + 1) * P], ident)
                    last.then_inc(pt_tr, 1)

                def values(q, g, j):
                    pe.wait_ge(pt_ev, heads_done(q, g, j + 1))
                    for kind in range(2):
                        for k in range(q + 1):
                            v = tv[:, k, bass.ds(g * HD + kind * KVW, HD)]
                            last = mm(ps[:, 6, (kind * 4 + j) * HD:(kind * 4 + j + 1) * HD],
                                      ptk[:, j % 2, kind, k, :], v, start=k == 0, stop=k == q)
                    last.then_inc(pv_done, 1)

                def step(q, g, Q, G):
                    more = Q < TT
                    scores(q, g, 2)
                    pe.wait_ge(pc_exp, steps_done(q, g, 1))
                    nc.tensor.transpose(ps[:, 7, P:2 * P], pc[:, :], ident).then_inc(ptc_tr, 1)
                    turn(q, g, 1)
                    pe.wait_ge(ptc_ev, steps_done(q, g, 1))
                    mm(ps[:, 7, 2 * P:4 * P], ptc[:, :],
                       vcb[:, g, :, :].rearrange("p j d -> p (j d)"), start=True, stop=True).then_inc(oc_done, 1)
                    pe.wait_ge(o_read, lay(L, 17, 4 * q + 1, g, 1))
                    values(q, g, 0)
                    scores(q, g, 3)
                    if more:
                        pe.wait_ge(oc_read, steps_done(q, g, 1))
                        turn_q(Q, G)
                    turn(q, g, 2)
                    values(q, g, 1)
                    if more:
                        compressed(Q, G)
                        scores(Q, G, 0)
                    turn(q, g, 3)
                    values(q, g, 2)
                    if more:
                        scores(Q, G, 1)
                        turn(Q, G, 0)
                    values(q, g, 3)

                turn_q(0, 0)
                pe.wait_ge(k_lo, lay(L, 9, 9))
                compressed(0, 0)
                scores(0, 0, 0, True)
                scores(0, 0, 1, True)
                turn(0, 0, 0, True)
                settle(pe)
                steps(step, lambda n: pe.Fori(0, n))
                barrier(pe, L, 2)

                for m in range(DT):
                    last = mm(ps[:, 4, :], ones, acc[:, m, :], start=m == 0, stop=m == DT - 1)
                last.then_inc(ln_mu, 1)
                product(L, U_MERGE, B_MERGE, xh, xl, first=16)
                for m in range(DT):
                    if m >= 2:
                        pe.wait_ge(ot_l, lay(L, 8, m - 1))
                    for t in range(TT):
                        last = nc.tensor.transpose(ps[:, 6 + m % 2, t * P:(t + 1) * P], tq[:, t, m * P:(m + 1) * P],
                                                   ident)
                    last.then_inc(ot_tr, 1)
                    pe.wait_ge(ln_sq, lay(L, 8, m + 1))
                    mm(ps[:, 5, :], ones, sq[:, m % 2, :], start=m == 0, stop=m == DT - 1).then_inc(ln_var, 1)
                product(L, U_MERGE + 1, B_MERGE + 1, xh, xl)
                product(L, U_MERGE + 2, B_MERGE + 2, oh, ol, ready=ot_l)
                product(L, U_MERGE + 3, B_MERGE + 3, cvh, cvl, ready=ln_lo)
                with pe.Fori(0, DT - 1) as i:
                    for j, (rh, rl) in enumerate(((xh, xl), (xh, xl), (oh, ol), (cvh, cvl))):
                        product(L, U_MERGE + 4 + j, B_MERGE + 4 + j, rh, rl, i, 4, 4)
                barrier(pe, L, 3)
                product(L, U_OUT, B_OUT, xh, xl, first=24)
                for j in range(1, 4):
                    product(L, U_OUT + j, B_OUT + j, xh, xl)
                for j in range(4):
                    product(L, U_OUT + 4 + j, B_OUT + 4 + j, xh, xl)
                barrier(pe, L, 4)
                ffn(L, U_FFN2, B_FFN2, 1, 32, 2)
                barrier(pe, L, 5)

                def proj(j):
                    u = U_PROJ + j
                    pe.wait_ge(w_split, unit(L, u + 1))
                    for m in range(4):
                        b = B_PROJ + 4 * j + m
                        pe.wait_ge(bank_free, lay(L, BANKS, b + 1))
                        for k in range(2):
                            if j == 0 and m == 0:
                                pe.wait_ge(p_lo_, lay(L, 2, k + 1))
                            w = slice(k * 512 + m * P, k * 512 + (m + 1) * P)
                            last = mm3(bank(b), wh[:, u % SLOTS, w], wl[:, u % SLOTS, w], ph[:, k, :], pl[:, k, :],
                                       k == 0, k == 1)
                    last.then_inc(w_used, 1)

                proj(0)
                proj(1)
                product(L, U_PLE, B_PLE, xh, xl, first=40)
                stat_sum(L, 3)
                product(L, U_PLE + 1, B_PLE + 1, xh, xl)
                stat_sum(L, 4)
                for j in range(2, 4):
                    product(L, U_PLE + j, B_PLE + j, xh, xl)
                for j in range(4):
                    product(L, U_PLE + 4 + j, B_PLE + 4 + j, xh, xl)
                barrier(pe, L, 6)

        @block.scalar
        def _(act):
            seq = Chain(act, act_seq, "act.", settle)
            f = nc.scalar.activation

            def hi(L, c, i=None, pi=0):
                s = c % SLOTS
                act.wait_ge(w_used, unit(L, c + 1, i, pi))
                n = lay(L, UNITS // SLOTS, c // SLOTS + 2, i, pi // SLOTS)
                act.wait_ge(raw_in[s], n * 16)
                f(wh[:, s, :], raw[:, s, :], ACT.Copy).then_inc(w_hi, 1)

            def evacuated(L, b, i=None, bi=0):
                act.wait_ge(bank_free, lay(L, BANKS, b + 5, i, bi))

            def norm(L, ev, gain, stat):
                for k in range(DT):
                    f(xh[:, k, :], x[:, k, :], ACT.Copy, scale=col(gain + k)).then_inc(s_xh, 1)
                if stat is not None:
                    for k in range(DT):
                        if k >= 2:
                            act.wait_ge(s_ssq, lay(L, 40, 8 * stat + k - 1))
                        f(sq[:, k % 2, :], x[:, k, :], ACT.Square).then_inc(s_sq, 1)

            def root(L, si, t):
                act.wait_ge(s_rinv, lay(L, 6, si + 1))
                f(t, t, ACT.Sqrt).then_inc(s_rstd, 1)

            def ffn(L, u0, b0, which, ev, gain, stat, si):
                def ab(c, b, s, par, i=None):
                    for j in range(2):
                        hi(L, c + 2 * j, i, 12)
                        evacuated(L, b + 2 * j, i, 8)
                        f(fa[:, j, :], fa[:, j, :], ACT.Silu).then_inc(f_silu, 1)
                        hi(L, c + 2 * j + 1, i, 12)
                        act.wait_ge(f_h, lay(L, 2 * FT, which * FT + 2 * s + j + 1, i, 4))
                        f(hh[:, par, j, :], fb[:, j, :], ACT.Copy).then_inc(f_hh, 1)

                norm(L, ev, gain, stat)
                root(L, si, rstd[:, :])
                ab(u0, b0, 0, 0)
                with seq.loop("ffn", (FSTEPS - 1) // 2) as i:
                    for h in range(2):
                        ab(u0 + 4 + 6 * h, b0 + 4 + 4 * h, 1 + h, 1 - h, i)
                        hi(L, u0 + 8 + 6 * h, i, 12)
                        hi(L, u0 + 9 + 6 * h, i, 12)
                hi(L, u0 + 4 + 6 * (FSTEPS - 1))
                hi(L, u0 + 5 + 6 * (FSTEPS - 1))

            act.wait_ge(const_in, 16)
            f(ident_r[:, :], ident, ACT.Copy)
            act.wait_ge(mask_in, 16)
            f(mask_r[:, :], masks[:, K_MASK:K_MASK + P], ACT.Copy)
            f(cmask_r[:, :, :], masks[:, K_CM:K_CM + TT * P].rearrange("p (t k) -> p t k", t=TT),
              ACT.Copy).then_inc(con_r, 1)
            for u in range(SLOTS):
                act.wait_ge(raw_in[u], 16)
                f(wh[:, u, :], raw[:, u, :], ACT.Copy).then_inc(w_hi, 1)

            with seq.loop("layer", DEPTH) as L:
                act.wait_ge(cols_in, lay(L, 16, 16))
                act.wait_ge(x_in, 16)
                ffn(L, U_FFN1, B_FFN1, 0, 0, C_F1, 0, 0)
                barrier(act, L, 0)

                norm(L, 1, C_MIX, 1)
                root(L, 1, rstd[:, :])
                root(L, 2, rstd_t[:, :])

                def pair(m, c, b, i=None):
                    hi(L, c, i, 4)
                    hi(L, c + 1, i, 4)
                    evacuated(L, b + 1, i, 4)
                    f(cv[:, 1, :], cv[:, 1, :], ACT.Sigmoid, bias=col(m + C_BG)).then_inc(c_sig, 1)

                for j in range(2):
                    pair(j, U_CONV + 2 * j, B_CONV + 2 * j)
                with seq.loop("conv", 3) as i:
                    for j in range(2):
                        pair(i * 2 + (2 + j), U_CONV + 4 + 2 * j, B_CONV + 4 + 2 * j, i)
                for j in range(4):
                    hi(L, U_CT + j)
                    evacuated(L, B_CT + j)
                    f(ctb[:, j, :], ctb[:, j, :], ACT.Identity, bias=col(C_BCT + j)).then_inc(ct_ready, 1)
                    act.wait_ge(ct_ready, lay(L, 4, j + 1))
                    if j == 0:
                        act.wait_ge(xc_zero, lay(L, 1, 1))
                    settle(act)
                    for half in range(2):
                        h = 2 * (j % 2) + half
                        src = ctb[64 * half:64 * half + 64, j, :]
                        act.dma_start(xc[0:64, j // 2, h, 0:T], src).then_inc(xc_in, 16)
                        act.dma_start(xc[64:128, j // 2, h, 0:T - 1], src[:, 1:T]).then_inc(xc_in, 16)
                hi(L, U_GATE)
                evacuated(L, B_GATE)
                f(cv[0:3 * NH, 0, :], cv[0:3 * NH, 0, :], ACT.Sigmoid, bias=cols[0:3 * NH, C_BB:C_BB + 1])\
                    .then_inc(g_sig, 1)

                def roots(n, c):
                    act.wait_ge(t_rinv, lay(L, 4, n))
                    f(small[:, 0:c], small[:, 0:c], ACT.Sqrt).then_inc(t_rs, 1)

                def head_norm(xt, b, n):
                    evacuated(L, b + TT - 1)
                    f(sqt[:, :, :], xt, ACT.Square).then_inc(t_sq, 1)
                    roots(n, 32)

                def block_in(jj):
                    c, j = jj // 16, jj % 16
                    if jj >= 8:
                        act.wait_ge(w_used, unit(L, U_CMP + (jj - 8) // 4 + 1))
                    f(ych[:, jj % 8, :].rearrange("p (h n) -> p h n", h=NKV), at_pos(c, j), ACT.Identity,
                      bias=col(C_POS + jj)).then_inc(yc_h, 1)

                for j in range(4):
                    hi(L, U_K + j)
                    if j == 1:
                        act.wait_ge(xc_in, lay(L, 256, 256))
                        for jj in range(8):
                            block_in(jj)
                for u in range(8):
                    hi(L, U_CMP + u)
                    if u % 4 == 3:
                        evacuated(L, B_CMP + u // 4 * 2 + 1)
                        f(hid[:, :], hid[:, :], ACT.Gelu_apprx_tanh).then_inc(hid_act, 1)
                    if u == 5:
                        act.wait_ge(hid_tr, lay(L, 2, 1))
                        f(hkh[:, :, :], ps[:, 6, 0:2 * P].rearrange("p (m k) -> p m k", m=2), ACT.Copy)\
                            .then_inc(hid_h, 1)
                    if u < 6:
                        for jj in range(8 + 4 * u, 12 + 4 * u):
                            block_in(jj)
                head_norm(tk, B_K, 1)
                for j in range(4):
                    hi(L, U_Q0 + j)
                    if j == 1:
                        act.wait_ge(hid_tr, lay(L, 2, 2))
                        act.wait_ge(w_split, unit(L, U_Q0 + SLOTS + 1))
                        for m in range(2):
                            ins = f(hvh[:, m, :].rearrange("p (g j n) -> p g j n", g=NKV, j=HPG),
                                    copies(7, m), ACT.Copy)
                        ins.then_inc(hid_h, 1)
                hi(L, U_W2)
                roots(2, 1)
                head_norm(tq[:, :, 0:512], B_Q0, 3)
                for j in range(4):
                    hi(L, U_Q1 + j)
                head_norm(tq[:, :, 512:D], B_Q1, 4)
                for j in range(4):
                    hi(L, U_V + j)
                barrier(act, L, 1)

                def two_keys(t):
                    f(k2[:, t % 2, :, :, :], twice(tk[:, t, :], 8), ACT.Copy).then_inc(k_two, 1)

                def two_q(q, g):
                    f(q2[:, :, :, :], twice(heads(q, g), HPG), ACT.Copy).then_inc(q_two, 1)

                f(kc2[:, :, :, :], twice(kc[:, :], 1), ACT.Copy).then_inc(k_two, 1)
                two_keys(0)
                two_keys(1)
                act.wait_ge(k_tr, lay(L, 9, 1))
                f(kcT[:, 0, :], ps[:, 6, 0:P], ACT.Copy).then_inc(k_hi, 1)
                for n in range(2 * TT):
                    if n in (2, 4):
                        act.wait_ge(k_tr, lay(L, 9, n + 1))
                        two_keys(n // 2 + 1)
                    act.wait_ge(k_tr, lay(L, 9, n + 2))
                    f(kT[:, n % 2, 0, :, n // 2 * P:(n // 2 + 1) * P],
                      ps[:, n % 4, :].rearrange("p (g k) -> p g k", g=NKV), ACT.Copy).then_inc(k_hi, 1)

                def round_q(q, g):
                    act.wait_ge(q_tr, lay(L, 16, 4 * q + 1, g, 1))
                    f(q2T[:, :, :], ps[:, 7, :].rearrange("p (j k) -> p j k", j=HPG), ACT.Copy).then_inc(q_hi, 1)

                def exp_c(q, g):
                    act.wait_ge(sc_sub, lay(L, 16, 4 * q + 1, g, 1))
                    f(pc[:, :], pcs[:, :, :].rearrange("p j n -> p (j n)"), ACT.Exp, scale=SCALE).then_inc(pc_exp, 1)

                def exps(q, g, j):
                    W = (q + 1) * P
                    act.wait_ge(s_max, lay(L, 64, 16 * q + j + 1, g, 4))
                    for kind in range(2):
                        n = 28 + 4 * kind + j
                        ins = f(pr[:, j % 2, kind, 0:W], side(2 * (j % 2), q)[:, kind, :], ACT.Exp, scale=SCALE,
                                bias=att[:, 16 + 2 * (j % 2) + kind:17 + 2 * (j % 2) + kind],
                                accum_out=att[:, n:n + 1])
                    ins.then_inc(p_exp, 1)

                def turned(q, g, j):
                    act.wait_ge(pt_tr, lay(L, 64, 16 * q + j + 1, g, 4))
                    for kind in range(2):
                        ins = f(ptk[:, j % 2, kind, 0:q + 1, :],
                                side(4, q)[:, kind, :].rearrange("p (t k) -> p t k", k=P), ACT.Copy)
                    ins.then_inc(pt_ev, 1)

                def step(q, g, Q, G):
                    more = Q < TT
                    if more:
                        two_q(Q, G)
                    exps(q, g, 2)
                    turned(q, g, 1)
                    if more:
                        round_q(Q, G)
                    exps(q, g, 3)
                    turned(q, g, 2)
                    if more:
                        exp_c(Q, G)
                        exps(Q, G, 0)
                    turned(q, g, 3)
                    if more:
                        exps(Q, G, 1)
                        turned(Q, G, 0)

                act.wait_ge(k_tr, lay(L, 9, 9))
                two_q(0, 0)
                round_q(0, 0)
                exp_c(0, 0)
                exps(0, 0, 0)
                exps(0, 0, 1)
                turned(0, 0, 0)
                steps(step, lambda n: seq.loop("att", n))
                barrier(act, L, 2)

                norm(L, 2, C_MIX, None)
                for m in range(DT):
                    act.wait_ge(ln_d, lay(L, 8, m + 1))
                    if m >= 2:
                        act.wait_ge(ln_var, lay(L, 8, m - 1))
                    f(sq[:, m % 2, :], acc[:, m, :], ACT.Square).then_inc(ln_sq, 1)
                    act.wait_ge(ot_tr, lay(L, 8, m + 1))
                    f(oh[:, m, :], ps[:, 6 + m % 2, :], ACT.Copy).then_inc(ot_h, 1)
                hi(L, U_MERGE)
                act.wait_ge(ln_rinv, lay(L, 1, 1))
                f(ssq[:, :], ssq[:, :], ACT.Sqrt).then_inc(ln_rs, 1)
                for m in range(DT):
                    act.wait_ge(ln_e, lay(L, 8, m + 1))
                    f(acc[:, m, :], acc[:, m, :], ACT.Silu, bias=col(C_LB + m), scale=col(C_LG + m)).then_inc(ln_f, 1)
                    if m:
                        act.wait_ge(ln_f, lay(L, 8, m))
                        f(cvh[:, m - 1, :], acc[:, m - 1, :], ACT.Copy).then_inc(ln_hi, 1)
                act.wait_ge(ln_f, lay(L, 8, 8))
                f(cvh[:, DT - 1, :], acc[:, DT - 1, :], ACT.Copy).then_inc(ln_hi, 1)

                def merge(m, c, i=None):
                    for j in range(4):
                        if c + j:
                            hi(L, U_MERGE + c + j, i, 4)
                        if j < 2:
                            evacuated(L, B_MERGE + c + j, i, 4)
                            f(mt[:, j, :], mt[:, j, :], ACT.Sigmoid, bias=col(m + (C_BGN if j else C_BGC)))\
                                .then_inc(m_sig, 1)

                merge(0, 0)
                with seq.loop("merge", DT - 1) as i:
                    merge(i + 1, 4, i)
                barrier(act, L, 3)
                for k in range(DT):
                    f(xh[:, k, :], yf[:, k, :], ACT.Copy).then_inc(s_xh, 1)
                for j in range(DT):
                    hi(L, U_OUT + j)
                barrier(act, L, 4)
                ffn(L, U_FFN2, B_FFN2, 1, 4, C_F2, 2, 3)
                barrier(act, L, 5)

                act.wait_ge(p_in, lay(L, 16, 16))
                for k in range(2):
                    f(ph[:, k, :], pf[:, k, :], ACT.Copy).then_inc(p_hi_, 1)
                norm(L, 5, C_PLE, 3)
                for j in range(2):
                    hi(L, U_PROJ + j)
                root(L, 4, rstd[:, :])
                for m in range(DT):
                    evacuated(L, B_PROJ + m)
                    if m >= 2:
                        act.wait_ge(s_ssq, lay(L, 40, 32 + m - 1))
                    f(sq[:, m % 2, :], pe_[:, m, :], ACT.Square).then_inc(s_sq, 1)
                for m in range(DT):
                    hi(L, U_PLE + m)
                    if m == 0:
                        root(L, 5, ssq[:, :])
                    evacuated(L, B_PLE + m)
                    f(fb[:, m % 2, :], fa[:, m % 2, :], ACT.Sigmoid).then_inc(g_s, 1)
                barrier(act, L, 6)

        @block.vector
        def _(dve):
            seq = Chain(dve, dve_seq, "dve.", settle)
            link = seq.link
            v = nc.vector
            tt, ts, stt = v.tensor_tensor, v.tensor_scalar, v.scalar_tensor_tensor
            MUL, ADD, SUB = ALU.mult, ALU.add, ALU.subtract

            def f32(ap):
                return ap.bitcast(F32)

            def lo(L, c, i=None, pi=0):
                s = c % SLOTS
                dve.wait_ge(w_hi, unit(L, c + 5, i, pi))
                tt(wl[:, s, :], raw[:, s, :], f32(wh[:, s, :]), SUB).then_inc(w_split, 1)

            def used(L, c, i=None, pi=0):
                dve.wait_ge(w_used, unit(L, c + 1, i, pi))

            def evacuated(L, b, i=None, bi=0):
                dve.wait_ge(bank_free, lay(L, BANKS, b + 5, i, bi))

            def scaled(dst, L, c, b, i=None, pi=0, bi=0):
                used(L, c, i, pi)
                tt(dst, ps[:, b % SLOTS, :], rstd[:, :], MUL).then_inc(bank_free, 1)

            def norm(L, ev, gain, stat):
                for k in range(DT):
                    dve.wait_ge(s_xh, lay(L, 48, 8 * ev + k + 1))
                    stt(xl[:, k, :], x[:, k, :], col(gain + k), f32(xh[:, k, :]), MUL, SUB).then_inc(s_xl, 1)
                if stat is not None:
                    for k in range(DT):
                        add_square(L, stat, k)

            def add_square(L, stat, k):
                dve.wait_ge(s_sq, lay(L, 40, 8 * stat + k + 1))
                if k == 0:
                    v.tensor_copy(ssq[:, :], sq[:, 0, :]).then_inc(s_ssq, 1)
                else:
                    dve.wait_ge(s_ssq, lay(L, 40, 8 * stat + k))
                    tt(ssq[:, :], ssq[:, :], sq[:, k % 2, :], ADD).then_inc(s_ssq, 1)

            def mean(L, si, dst, src):
                dve.wait_ge(s_sum, lay(L, 6, si + 1))
                link(ts(dst, src, 1.0 / D, EPS, MUL, ADD))
                v.reciprocal(dst, dst).then_inc(s_rinv, 1)

            def rooted(L, si):
                dve.wait_ge(s_rstd, lay(L, 6, si + 1))

            def ffn(L, u0, b0, which, ev, gain, stat, si):
                def ab(c, b, s, par, i=None):
                    for j in range(2):
                        scaled(fa[:, j, :], L, c + 2 * j, b + 2 * j, i, 12, 8)
                        lo(L, c + 2 * j, i, 12)
                        scaled(fb[:, j, :], L, c + 2 * j + 1, b + 2 * j + 1, i, 12, 8)
                        n = which * FT + 2 * s + j + 1
                        dve.wait_ge(f_silu, lay(L, 2 * FT, n, i, 4))
                        evacuated(L, b + 2 * j + 1, i, 8)
                        tt(fb[:, j, :], fb[:, j, :], fa[:, j, :], MUL).then_inc(f_h, 1)
                        lo(L, c + 2 * j + 1, i, 12)
                        dve.wait_ge(f_hh, lay(L, 2 * FT, n, i, 4))
                        tt(hl[:, par, j, :], fb[:, j, :], f32(hh[:, par, j, :]), SUB).then_inc(f_hl, 1)

                def y(c, s, i=None):
                    n = which * FSTEPS + s
                    dve.wait_ge(y_free, lay(L, 16 * FSTEPS, 8 * n + 4, i, 16))
                    for m in range(DT):
                        if m < DT - 1:
                            dve.wait_ge(y_done, lay(L, 14 * FSTEPS, 7 * n + m + 1, i, 14))
                        else:
                            used(L, c + 1, i, 12)
                        stt(x[:, m, :], ps[:, 4 + m % 4, :], 0.5, x[:, m, :], MUL, ADD).then_inc(y_free, 1)
                    lo(L, c, i, 12)
                    lo(L, c + 1, i, 12)

                norm(L, ev, gain, stat)
                mean(L, si, rstd[:, :], ps[:, 4, :])
                rooted(L, si)
                ab(u0, b0, 0, 0)
                with seq.loop("ffn", (FSTEPS - 1) // 2) as i:
                    for h in range(2):
                        ab(u0 + 4 + 6 * h, b0 + 4 + 4 * h, 1 + h, 1 - h, i)
                        y(u0 + 8 + 6 * h, h, i)
                y(u0 + 4 + 6 * (FSTEPS - 1), FSTEPS - 1)

            v.memset(att[:, 0:1], 0.0).then_inc(bank_free, SLOTS)
            v.memset(att[:, 1:2], 0.0).then_inc(y_free, 4)
            dve.wait_ge(const_in, 16)
            for u in range(SLOTS):
                dve.wait_ge(w_hi, u + 1)
                tt(wl[:, u, :], raw[:, u, :], f32(wh[:, u, :]), SUB).then_inc(w_split, 1)

            with seq.loop("layer", DEPTH) as L:
                dve.wait_ge(cols_in, lay(L, 16, 16))
                dve.wait_ge(x_in, 16)
                ffn(L, U_FFN1, B_FFN1, 0, 0, C_F1, 0, 0)
                barrier(dve, L, 0)

                norm(L, 1, C_MIX, 1)
                mean(L, 1, rstd[:, :], ps[:, 4, :])
                mean(L, 2, rstd_t[:, :], ps[:, 5, 0:TT])
                v.memset(ch[:, :, 0:CONV_K - 1], 0.0)
                rooted(L, 2)

                def taps(m, k0, k1, i=None):
                    for k in range(k0, k1):
                        for t in range(m, m + 2):
                            c, cb = C_CW + t * CONV_K + k, C_CB + t
                            if i is not None:
                                t, c, cb = i * 2 + t, i * (2 * CONV_K) + c, i * 2 + cb
                            if k == 0:
                                ins = ts(acc[:, t, :], ch[:, t, k:k + T], col(c), col(cb), MUL, ADD)
                            else:
                                ins = stt(acc[:, t, :], ch[:, t, k:k + T], col(c), acc[:, t, :], MUL, ADD)
                        link(ins)

                def pair(m, c, b, i=None):
                    scaled(cv[:, 0, :], L, c, b, i, 4, 4)
                    lo(L, c, i, 4)
                    scaled(cv[:, 1, :], L, c + 1, b + 1, i, 4, 4)
                    lo(L, c + 1, i, 4)
                    dve.wait_ge(c_sig, L * DT + m + 1)
                    link(stt(ch[:, m, CONV_K - 1:CONV_K - 1 + T], cv[:, 0, :], col(m + C_BA), cv[:, 1, :], ADD, MUL))

                for j in range(2):
                    pair(j, U_CONV + 2 * j, B_CONV + 2 * j)
                taps(0, 0, FIRST)
                with seq.loop("conv", 3) as i:
                    for j in range(2):
                        pair(i * 2 + (2 + j), U_CONV + 4 + 2 * j, B_CONV + 4 + 2 * j, i)
                    taps(2, 0, FIRST, i)
                for j in range(4):
                    scaled(ctb[:, j, :], L, U_CT + j, B_CT + j)
                    lo(L, U_CT + j)
                    taps(0, FIRST + 2 * j, FIRST + 2 * (j + 1))
                dve.wait_ge(rows_in, lay(L, 16, 16))
                used(L, U_GATE)
                tt(cv[0:3 * NH, 0, :], ps[0:3 * NH, B_GATE % SLOTS, :], rstd[0:3 * NH, :], MUL).then_inc(bank_free, 1)
                lo(L, U_GATE)

                def block_rest(jj):
                    dve.wait_ge(yc_h, lay(L, 32, jj + 1))
                    stt(ycl[:, jj % 8, :].rearrange("p (h n) -> p h n", h=NKV), at_pos(jj // 16, jj % 16),
                        col(C_POS + jj), f32(ych[:, jj % 8, :]).rearrange("p (h n) -> p h n", h=NKV),
                        ADD, SUB).then_inc(yc_l, 1)

                def tok_block(xt, u, b, n, m=None):
                    for j in range(4):
                        used(L, u + j)
                        if j == 3:
                            for t in range(TT):
                                stt(xt[:, t, :], ps[:, (b + t) % SLOTS, :], rstd_t[:, t:t + 1],
                                    row[:, R_B + n * 512:R_B + (n + 1) * 512], MUL, ADD).then_inc(bank_free, 1)
                        lo(L, u + j)
                        if n == 2 and j == 1:
                            for jj in range(8):
                                block_rest(jj)
                        if n == 0 and j == 1:
                            rest_hid()
                        if m is not None:
                            taps(m, FIRST + 2 * j, FIRST + 2 * (j + 1))

                def rope(x1, x2, cos, sin, tmp):
                    tt(tmp[0], x1, cos, MUL)
                    tt(tmp[1], x2, sin, MUL)
                    tt(tmp[2], x2, cos, MUL)
                    link(tt(tmp[3], x1, sin, MUL))
                    tt(x1, tmp[0], tmp[1], SUB)
                    link(tt(x2, tmp[2], tmp[3], ADD))

                def table(c):
                    return con_[:, c:c + 32].rearrange("p (t o e) -> p t o e", t=TT, o=1)\
                        .broadcast_to([P, TT, 8, HALF])

                def head_norm(xt, n, m, gains):
                    dve.wait_ge(t_sq, lay(L, 3, m))
                    link(v.reduce_sum(small[:, 0:32], sqt[:, :, :].rearrange("p t (h d) -> p (t h) d", d=HD), AX.X))
                    link(ts(small[:, 0:32], small[:, 0:32], 1.0 / HD, EPS, MUL, ADD))
                    v.reciprocal(small[:, 0:32], small[:, 0:32]).then_inc(t_rinv, 1)
                    gain = row[:, R_G + gains:R_G + gains + 512].rearrange("p (o n) -> p o n", o=1)
                    link(tt(xt, xt, gain.broadcast_to([P, TT, 512]), MUL))
                    dve.wait_ge(t_rs, lay(L, 4, n))
                    xt = xt.rearrange("p t (h d) -> p t h d", d=HD)
                    rs = small[:, 0:32].rearrange("p (t h o) -> p t h o", h=8, o=1)
                    link(tt(xt, xt, rs.broadcast_to([P, TT, 8, HD]), MUL))
                    rope(xt[:, :, :, 0:HALF], xt[:, :, :, HALF:2 * HALF], table(K_COS), table(K_SIN),
                         [sqt[:, c, 0:256].rearrange("p (t h e) -> p t h e", t=TT, h=8) for c in range(4)])

                tok_block(tk, U_K, B_K, 2, m=2)
                dve.wait_ge(g_tr, lay(L, 1, 1))
                v.tensor_copy(gates[:, :, :],
                              ps[:, B_GATE_T % SLOTS, :].rearrange("p (t c) -> p t c", t=TT)[:, :, 0:3 * NH])\
                    .then_inc(bank_free, 1)
                for u in range(8):
                    used(L, U_CMP + u)
                    c = u // 4
                    if u % 4 == 3:
                        tt(hid[:, :], ps[:, (B_CMP + 2 * c) % SLOTS, 0:CMP_HID],
                           row[:, R_B1 + c * CMP_HID:R_B1 + (c + 1) * CMP_HID], ADD).then_inc(bank_free, 2)
                    lo(L, U_CMP + u)
                    if u < 6:
                        for jj in range(8 + 4 * u, 12 + 4 * u):
                            block_rest(jj)
                    if 2 <= u < 6:
                        taps(4, FIRST + 2 * (u - 2), FIRST + 2 * (u - 1))
                    if u == 5:
                        dve.wait_ge(hid_h, lay(L, 2, 1))
                        tt(hkl[:, :, :], ps[:, 6, 0:2 * P].rearrange("p (m k) -> p m k", m=2),
                           f32(hkh[:, :, :]), SUB).then_inc(hid_l, 1)

                def rest_hid():
                    dve.wait_ge(hid_h, lay(L, 2, 2))
                    for m in range(2):
                        ins = tt(hvl[:, m, :].rearrange("p (g j n) -> p g j n", g=NKV, j=HPG),
                                 copies(7, m),
                                 f32(hvh[:, m, :]).rearrange("p (g j n) -> p g j n", g=NKV, j=HPG), SUB)
                    ins.then_inc(hid_l, 1)

                head_norm(tk, 1, 1, 512)
                tok_block(tq[:, :, 0:512], U_Q0, B_Q0, 0, m=6)
                dve.wait_ge(kc_ready, lay(L, 1, 1))
                v.tensor_copy(kc[:, :], ps[:, B_W2 % SLOTS, 0:HD]).then_inc(bank_free, 1)
                used(L, U_W2)
                dve.wait_ge(vcb_zero, lay(L, 1, 1))
                for j in range(HPG):
                    r = slice(NCMP * j, NCMP * (j + 1))
                    ins = v.tensor_copy(vcb[r, :, j, :],
                                        ps[r, (B_W2 + 1) % SLOTS, 0:NKV * HD].rearrange("p (g d) -> p g d", g=NKV))
                ins.then_inc(bank_free, 1)
                lo(L, U_W2)
                evacuated(L, B_W2)
                link(tt(kcw[:, :], kc[:, :], kc[:, :], MUL))
                link(v.reduce_sum(small[:, 0:1], kcw[:, :], AX.X))
                link(ts(small[:, 0:1], small[:, 0:1], 1.0 / HD, EPS, MUL, ADD))
                v.reciprocal(small[:, 0:1], small[:, 0:1]).then_inc(t_rinv, 1)
                dve.wait_ge(t_rs, lay(L, 4, 2))
                link(stt(kc[:, :], kc[:, :], small[:, 0:1], row[:, R_KC:R_KC + HD], MUL, MUL))
                rope(kc[:, 0:HALF], kc[:, HALF:2 * HALF], con_[:, K_COSC:K_COSC + HALF], con_[:, K_SINC:K_SINC + HALF],
                     [kcw[:, n * HALF:(n + 1) * HALF] for n in range(4)])

                head_norm(tq[:, :, 0:512], 3, 2, 0)
                tok_block(tq[:, :, 512:D], U_Q1, B_Q1, 1)
                head_norm(tq[:, :, 512:D], 4, 3, 0)
                tok_block(tv, U_V, B_V, 3)
                barrier(dve, L, 1)

                gc = gates[:, :, :].rearrange("p t (h c) -> p t h c", c=3)[:, :, :, 0]
                link(tt(gc, gc, con_[:, K_VALID:K_VALID + TT].rearrange("p (t o) -> p t o", o=1)
                        .broadcast_to([P, TT, NH]), MUL))
                v.memset(att[:, 0:1], 0.0).then_inc(o_read, 1)
                dve.wait_ge(k_hi, lay(L, 9, 1))
                tt(kcT[:, 1, :], ps[:, 6, 0:P], f32(kcT[:, 0, :]), SUB).then_inc(k_lo, 1)
                for n in range(2 * TT):
                    dve.wait_ge(k_hi, lay(L, 9, n + 2))
                    k = slice(n // 2 * P, (n // 2 + 1) * P)
                    tt(kT[:, n % 2, 1, :, k], ps[:, n % 4, :].rearrange("p (g k) -> p g k", g=NKV),
                       f32(kT[:, n % 2, 0, :, k]), SUB).then_inc(k_lo, 1)

                def steps_done(q, g, c):
                    return lay(L, 16, 4 * q + c, g, 1)

                def rest_q(q, g):
                    dve.wait_ge(q_hi, steps_done(q, g, 1))
                    tt(q2T[HD:P, :, :], ps[HD:P, 7, :].rearrange("p (j k) -> p j k", j=HPG), f32(q2T[HD:P, :, :]), SUB)\
                        .then_inc(q_lo, 1)

                def sub_max(q, g):
                    dve.wait_ge(sc_done, steps_done(q, g, 1))
                    sc = ps[:, 7, 0:P].rearrange("p (j n) -> p j n", j=HPG)
                    link(v.tensor_reduce(att[:, 0:4], sc, AX.X, ALU.max))
                    tt(pcs[:, :, :], sc, att[:, 0:4].rearrange("p (j o) -> p j o", o=1)
                       .broadcast_to([P, HPG, NCMP]), SUB).then_inc(sc_sub, 1)

                def row_max(q, g, j):
                    r = j % 2
                    dve.wait_ge(s_done, lay(L, 64, 16 * q + j + 1, g, 4))
                    link(v.tensor_reduce(att[:, 8 + 2 * r:10 + 2 * r], side(2 * r, q), AX.X, ALU.max))
                    ts(att[:, 16 + 2 * r:18 + 2 * r], att[:, 8 + 2 * r:10 + 2 * r], -SCALE, None, MUL)\
                        .then_inc(s_max, 1)

                def inverse(j):
                    def pair_of(c):
                        return att[:, c:c + 8].rearrange("p (c j) -> p c j", c=2)[:, :, j:j + 2]
                    return v.reciprocal(pair_of(56), pair_of(28))

                def tap(q, g, m):
                    for m in range(m, m + 2):
                        ins = stt(acc[:, m, :], ch[:, m, bass.ds(g + (MID + 4 * q), T)],
                                  col(g + (C_CW + m * CONV_K + MID + 4 * q)), acc[:, m, :], MUL, ADD)
                    return ins

                def weight(c):
                    return att[:, 40 + 4 * c:44 + 4 * c].rearrange("p (j o) -> p j o", o=1).broadcast_to([P, HPG, HD])

                def step(q, g, Q, G):
                    more = Q < TT
                    o = heads(q, g).rearrange("p (j d) -> p j d", j=HPG)

                    def gate(c, n):
                        return gates[:, q, bass.ds(g * 12, 12)].rearrange("p (j c) -> p c j", c=3)[:, c:c + n, :]

                    dve.wait_ge(ptc_tr, steps_done(q, g, 1))
                    v.tensor_copy(ptc[:, :], ps[:, 7, P:2 * P]).then_inc(ptc_ev, 1)
                    link(v.reduce_sum(att[:, 24:28], pc[:, :].rearrange("p (j n) -> p j n", j=HPG), AX.X))
                    row_max(q, g, 2)
                    link(v.reciprocal(att[:, 52:56], att[:, 24:28]))
                    link(tt(att[:, 40:44], att[:, 52:56], gate(0, 1).rearrange("p c j -> p (c j)"), MUL))
                    dve.wait_ge(oc_done, steps_done(q, g, 1))
                    tt(o, ps[:, 7, 2 * P:4 * P].rearrange("p (j d) -> p j d", j=HPG), weight(0), MUL)\
                        .then_inc(oc_read, 1)
                    tap(q, g, 0)
                    row_max(q, g, 3)
                    inverse(0)
                    if more:
                        rest_q(Q, G)
                    tap(q, g, 2)
                    if more:
                        sub_max(Q, G)
                        row_max(Q, G, 0)
                    tap(q, g, 4)
                    if more:
                        row_max(Q, G, 1)
                    else:
                        dve.wait_ge(p_exp, lay(L, 64, 64))
                    inverse(2)
                    link(tap(q, g, 6))
                    link(tt(att[:, 44:52].rearrange("p (c j) -> p c j", c=2),
                            att[:, 56:64].rearrange("p (c j) -> p c j", c=2), gate(1, 2), MUL))
                    dve.wait_ge(pv_done, lay(L, 64, 16 * q + 4, g, 4))
                    dve.wait_ge(oc_read, steps_done(q, g, 1))
                    tt(ot[:, 0, :, :], ps[:, 6, 0:256].rearrange("p (j d) -> p j d", j=HPG), weight(1), MUL)
                    tt(ot[:, 1, :, :], ps[:, 6, 256:512].rearrange("p (j d) -> p j d", j=HPG), weight(2), MUL)\
                        .then_inc(o_read, 1)
                    dve.wait_ge(o_read, lay(L, 17, 4 * q + 2, g, 1))
                    link(tt(o, o, ot[:, 0, :, :], ADD))
                    link(tt(o, o, ot[:, 1, :, :], ADD))

                rest_q(0, 0)
                sub_max(0, 0)
                row_max(0, 0, 0)
                row_max(0, 0, 1)
                steps(step, lambda n: seq.loop("att", n))
                barrier(dve, L, 2)

                def branch_gate(j, c, i=None):
                    scaled(mt[:, j, :], L, U_MERGE + c + j, B_MERGE + c + j, i, 4, 4)
                    lo(L, U_MERGE + c + j, i, 4)

                def branch_out(m, c, i=None):
                    dve.wait_ge(m_sig, lay(L, 2 * DT, 2 + c // 2, i, 2))
                    for j in range(2, 4):
                        used(L, U_MERGE + c + j, i, 4)
                        tt(mt[:, j, :], ps[:, (B_MERGE + j) % SLOTS, :], mt[:, 3 - j, :], MUL).then_inc(bank_free, 1)
                        lo(L, U_MERGE + c + j, i, 4)
                    evacuated(L, B_MERGE + c + 3, i, 4)
                    link(tt(yf[:, m, :], mt[:, 2, :], mt[:, 3, :], ADD))

                norm(L, 2, C_MIX, None)
                dve.wait_ge(ln_mu, lay(L, 1, 1))
                for m in range(DT):
                    stt(acc[:, m, :], ps[:, 4, :], -1.0 / D, acc[:, m, :], MUL, ADD).then_inc(ln_d, 1)
                for m in range(DT):
                    dve.wait_ge(ot_h, lay(L, 8, m + 1))
                    tt(ol[:, m, :], ps[:, 6 + m % 2, :], f32(oh[:, m, :]), SUB).then_inc(ot_l, 1)
                dve.wait_ge(ln_var, lay(L, 8, 8))
                link(ts(ssq[:, :], ps[:, 5, :], 1.0 / D, EPS, MUL, ADD))
                v.reciprocal(ssq[:, :], ssq[:, :]).then_inc(ln_rinv, 1)
                branch_gate(0, 0)
                dve.wait_ge(ln_rs, lay(L, 1, 1))
                dve.wait_ge(ln_d, lay(L, 8, 8))
                for m in range(DT):
                    tt(acc[:, m, :], acc[:, m, :], ssq[:, :], MUL).then_inc(ln_e, 1)
                for m in range(DT):
                    dve.wait_ge(ln_hi, lay(L, 8, m + 1))
                    tt(cvl[:, m, :], acc[:, m, :], f32(cvh[:, m, :]), SUB).then_inc(ln_lo, 1)
                branch_gate(1, 0)
                branch_out(0, 0)
                with seq.loop("merge", DT - 1) as i:
                    branch_gate(0, 4, i)
                    branch_gate(1, 4, i)
                    branch_out(i + 1, 4, i)
                barrier(dve, L, 3)
                for k in range(DT):
                    dve.wait_ge(s_xh, lay(L, 48, 24 + k + 1))
                    tt(xl[:, k, :], yf[:, k, :], f32(xh[:, k, :]), SUB).then_inc(s_xl, 1)
                for m in range(DT):
                    used(L, U_OUT + m)
                    tt(x[:, m, :], ps[:, (B_OUT + m) % SLOTS, :], x[:, m, :], ADD).then_inc(bank_free, 1)
                    lo(L, U_OUT + m)
                barrier(dve, L, 4)
                ffn(L, U_FFN2, B_FFN2, 1, 4, C_F2, 2, 3)
                barrier(dve, L, 5)

                for k in range(2):
                    dve.wait_ge(p_hi_, lay(L, 2, k + 1))
                    tt(pl[:, k, :], pf[:, k, :], f32(ph[:, k, :]), SUB).then_inc(p_lo_, 1)
                norm(L, 5, C_PLE, 3)
                for j in range(2):
                    used(L, U_PROJ + j)
                    for m in range(4 * j, 4 * j + 4):
                        v.tensor_copy(pe_[:, m, :], ps[:, (B_PROJ + m) % SLOTS, :]).then_inc(bank_free, 1)
                    lo(L, U_PROJ + j)
                mean(L, 4, rstd[:, :], ps[:, 4, :])
                for m in range(DT):
                    add_square(L, 4, m)
                rooted(L, 4)
                for m in range(DT):
                    scaled(fa[:, m % 2, :], L, U_PLE + m, B_PLE + m)
                    lo(L, U_PLE + m)
                    if m == 0:
                        mean(L, 5, ssq[:, :], ps[:, 4, :])
                        rooted(L, 5)
                        for k in range(DT):
                            ins = stt(pe_[:, k, :], pe_[:, k, :], col(C_POST + k), ssq[:, :], MUL, MUL)
                        link(ins)
                    dve.wait_ge(g_s, lay(L, DT, m + 1))
                    link(tt(fb[:, m % 2, :], fb[:, m % 2, :], pe_[:, m, :], MUL))
                    link(tt(x[:, m, :], x[:, m, :], fb[:, m % 2, :], ADD))
                barrier(dve, L, 6)


_OUT = "out_0_dram"


def kernel(**inputs):
    import concourse.bacc as bacc
    from concourse.bass_utils import run_bass_kernel_spmd

    i = {k: np.asarray(a) for k, a in inputs.items()}
    stream, cols, rows = pack(i)
    con, masks = constants()
    arrays = {
        "stream": stream, "cols": cols, "rows": rows, "const": con, "masks": masks,
        "xT": np.ascontiguousarray(i["x"][0].T.reshape(DT, P, T).transpose(1, 0, 2)),
        "pT": np.ascontiguousarray(i["p"][:, 0].transpose(0, 2, 1).reshape(DEPTH, 2, P, T).transpose(0, 2, 1, 3)),
    }
    nc = bacc.Bacc("TRN2", target_bir_lowering=False, num_devices=1)
    args = [nc.dram_tensor(n, a.shape, F32, kind="ExternalInput").ap() for n, a in arrays.items()]
    out = nc.dram_tensor(_OUT, (P, DT, T), F32, kind="ExternalOutput").ap()
    build(nc, *args, out)
    got = run_bass_kernel_spmd(nc, [arrays], core_ids=[0]).results[0][_OUT]
    return np.ascontiguousarray(np.asarray(got).transpose(2, 1, 0).reshape(1, T, D))
```
